# Optimizing a Trainium2 kernel written in Bass

```python
import jax
import jax.numpy as jnp
from jax import lax
import numpy as np
import jax, jax.numpy as jnp

D_MODEL = 2048
BATCH = 1
SEQ = 256
DEPTH = 1

GRID_W = 64
CTX_LEN = 256
HEAD_DIM = 64
D_RWKV = D_MODEL // 2
N_RWKV_HEADS = D_RWKV // HEAD_DIM
D_CONV = D_MODEL // 4
D_FOURIER = D_MODEL // 4
N_FOURIER_GROUPS = D_FOURIER // HEAD_DIM
D_MIX = D_RWKV + D_CONV + D_FOURIER
DECAY_LORA = 96
ICLR_LORA = 96
GATE_LORA = 256
D_FF = ((8 * D_MODEL + 3 * 256 - 1) // (3 * 256)) * 256
N_MOD = 6
RMS_EPS = 1e-6
GN_EPS = 64e-5
KK_EPS = 1e-12

R0 = 0
K0 = R0 + D_RWKV
V0 = K0 + D_RWKV
WD0 = V0 + D_RWKV
AD0 = WD0 + DECAY_LORA
GD0 = AD0 + ICLR_LORA
RW_COLS = GD0 + GATE_LORA
CG0 = RW_COLS
CX0 = CG0 + D_CONV
CB0 = CX0 + D_CONV
FT0 = CB0 + D_CONV
D_IN = FT0 + D_FOURIER


def rms_norm(x, g):
    xf = x.astype(jnp.float32)
    y = xf * lax.rsqrt(jnp.mean(xf * xf, axis=-1, keepdims=True) + RMS_EPS)
    return (y * g.astype(jnp.float32)).astype(x.dtype)

def adaln(cvec, w, b):
    m = jax.nn.silu(cvec) @ w + b
    return jnp.split(m[:, None, :], N_MOD, axis=-1)

def modulate(h, shift, scale):
    return h * (1.0 + scale) + shift

def conv3(u, w):
    pad = [(0, 0)] * (u.ndim - 2) + [(1, 1), (0, 0)]
    up = jnp.pad(u, pad)
    return up[..., :-2, :] * w[0] + up[..., 1:-1, :] * w[1] + up[..., 2:, :] * w[2]

def grid_conv3(u, w):
    b, l, ch = u.shape
    rows = l // GRID_W
    return conv3(u.reshape(b, rows, GRID_W, ch), w).reshape(b, l, ch)

def rwkv_streams(rw, dec_w0, dec_up, iclr_a0, iclr_up, k_k, k_a):
    rw = rw.astype(jnp.float32)
    b, l = rw.shape[:2]

    def heads(t):
        return t.reshape(b, l, N_RWKV_HEADS, HEAD_DIM)

    r = rw[..., R0:K0]
    k = rw[..., K0:V0]
    v = rw[..., V0:WD0]
    wd = jnp.tanh(rw[..., WD0:AD0])
    ad = rw[..., AD0:GD0]
    gd = rw[..., GD0:RW_COLS]
    kk = heads(k * k_k)
    kk = kk / jnp.maximum(jnp.sqrt(jnp.sum(kk * kk, axis=-1, keepdims=True)), KK_EPS)
    per_dir = []
    for d in range(2):
        w_log = -jax.nn.softplus(-(dec_w0[d] + wd @ dec_up[d])) - 0.5
        a = jax.nn.sigmoid(iclr_a0[d] + ad @ iclr_up[d])
        kd = k * (1.0 + (a - 1.0) * k_a)
        per_dir.append((heads(jnp.exp(-jnp.exp(w_log))), heads(kd), heads(a)))
    return heads(r), heads(v), kk, per_dir, gd

def wkv_scan(r, w, k, v, kk, a, s0, reverse):
    def step(s, inp):
        r_t, w_t, k_t, v_t, kk_t, a_t = inp
        sa = jnp.einsum('bhij,bhj->bhi', s, -kk_t)
        s = (s * w_t[:, :, None, :] + sa[..., None] * (kk_t * a_t)[:, :, None, :]
             + v_t[..., None] * k_t[:, :, None, :])
        return s, jnp.einsum('bhij,bhj->bhi', s, r_t)

    xs = tuple(jnp.moveaxis(t, 1, 0) for t in (r, w, k, v, kk, a))
    s_fin, ys = lax.scan(step, s0, xs, reverse=reverse)
    return jnp.moveaxis(ys, 0, 1), s_fin

def rwkv_mix(streams, s0, ln_w, ln_b, r_k, g_up):
    r, v, kk, per_dir, gd = streams
    (wf, kf, af), (wb, kb, ab) = per_dir
    yf, sf = wkv_scan(r, wf, kf, v, kk, af, s0[0], False)
    yb, sb = wkv_scan(r, wb, kb, v, kk, ab, s0[1], True)
    y = yf + yb
    mu = jnp.mean(y, axis=-1, keepdims=True)
    var = jnp.mean(jnp.square(y - mu), axis=-1, keepdims=True)
    y = ((y - mu) * lax.rsqrt(var + GN_EPS) * ln_w.reshape(N_RWKV_HEADS, HEAD_DIM)
         + ln_b.reshape(N_RWKV_HEADS, HEAD_DIM))
    y = y + jnp.sum(r * (kf + kb) * r_k, axis=-1, keepdims=True) * v
    b, l = y.shape[:2]
    g = jax.nn.sigmoid(gd) @ g_up
    return y.reshape(b, l, D_RWKV) * g, (sf, sb)

def short_conv_mix(p, conv_w, conv_fn):
    return p[..., CB0:FT0] * conv_fn(p[..., CG0:CX0] * p[..., CX0:CB0], conv_w)

def fourier_mix(p):
    u = p[..., FT0:D_IN].astype(jnp.float32)
    b, l = u.shape[:2]
    u = u.reshape(b, l, N_FOURIER_GROUPS, HEAD_DIM)
    y = jnp.fft.fftn(u, axes=(1, 3), norm='ortho').real
    return y.reshape(b, l, D_FOURIER).astype(p.dtype)

def ffn(h, wg, wu, wd):
    return (jax.nn.silu(h @ wg) * (h @ wu)) @ wd

def first_inputs(seed: int = 0) -> dict:
    key = jax.random.key(seed)
    ks = jax.random.split(key, 32)
    f32 = jnp.float32

    def nrm(k, shape, s):
        return jax.random.normal(k, shape, f32) * s

    L = DEPTH
    left = jax.random.uniform(ks[8], (L, 1, RW_COLS), f32, 0.0, 0.4)
    right = jax.random.uniform(ks[9], (L, 1, RW_COLS), f32, 0.0, 0.4)
    rw_shift = jnp.concatenate([left, 1.0 - 0.5 * (left + right), right], axis=1)
    return {
        'x': nrm(ks[0], (BATCH, SEQ, D_MODEL), 1.0),
        'c': nrm(ks[1], (BATCH, D_MODEL), 1.0),
        'ctx': nrm(ks[2], (BATCH, CTX_LEN, D_MODEL), 1.0),
        'c_ctx': nrm(ks[3], (D_MODEL,), 1.0),
        'w_mod': nrm(ks[4], (L, D_MODEL, N_MOD * D_MODEL), 0.5 * D_MODEL ** -0.5),
        'b_mod': nrm(ks[5], (L, N_MOD * D_MODEL), 0.02),
        'norm_mix': 1.0 + nrm(ks[6], (L, D_MODEL), 0.05),
        'w_in': nrm(ks[7], (L, D_MODEL, D_IN), D_MODEL ** -0.5),
        'rw_shift': rw_shift,
        'dec_w0': jax.random.uniform(ks[10], (L, 2, D_RWKV), f32, -6.0, 1.0),
        'dec_up': nrm(ks[11], (L, 2, DECAY_LORA, D_RWKV), 0.5 * DECAY_LORA ** -0.5),
        'iclr_a0': nrm(ks[12], (L, 2, D_RWKV), 0.1),
        'iclr_up': nrm(ks[13], (L, 2, ICLR_LORA, D_RWKV), 0.5 * ICLR_LORA ** -0.5),
        'k_k': 0.85 + nrm(ks[14], (L, D_RWKV), 0.05),
        'k_a': 1.0 + nrm(ks[15], (L, D_RWKV), 0.05),
        'r_k': nrm(ks[16], (L, N_RWKV_HEADS, HEAD_DIM), 0.1),
        'ln_w': 1.0 + nrm(ks[17], (L, D_RWKV), 0.05),
        'ln_b': nrm(ks[18], (L, D_RWKV), 0.02),
        'g_up': nrm(ks[19], (L, GATE_LORA, D_RWKV), GATE_LORA ** -0.5),
        'conv_w': nrm(ks[20], (L, 3, D_CONV), 0.5),
        'w_out': nrm(ks[21], (L, D_MIX, D_MODEL), D_MIX ** -0.5),
        'norm_ffn': 1.0 + nrm(ks[22], (L, D_MODEL), 0.05),
        'w_gate': nrm(ks[23], (L, D_MODEL, D_FF), D_MODEL ** -0.5),
        'w_up': nrm(ks[24], (L, D_MODEL, D_FF), D_MODEL ** -0.5),
        'w_down': nrm(ks[25], (L, D_FF, D_MODEL), D_FF ** -0.5),
        'norm_final': 1.0 + nrm(ks[26], (D_MODEL,), 0.05),
    }

def first_block(x, c, ctx, c_ctx, w_mod, b_mod, norm_mix, w_in, rw_shift, dec_w0, dec_up,
              iclr_a0, iclr_up, k_k, k_a, r_k, ln_w, ln_b, g_up, conv_w, w_out,
              norm_ffn, w_gate, w_up, w_down, norm_final):
    xc = ctx
    s_zero = jnp.zeros((ctx.shape[0], N_RWKV_HEADS, HEAD_DIM, HEAD_DIM), jnp.float32)
    for i in range(DEPTH):
        sh1, sc1, ga1, sh2, sc2, ga2 = adaln(c, w_mod[i], b_mod[i])
        csh1, csc1, cga1, csh2, csc2, cga2 = adaln(c_ctx[None, :], w_mod[i], b_mod[i])
        px = modulate(rms_norm(x, norm_mix[i]), sh1, sc1) @ w_in[i]
        pc = modulate(rms_norm(xc, norm_mix[i]), csh1, csc1) @ w_in[i]
        rw_args = (dec_w0[i], dec_up[i], iclr_a0[i], iclr_up[i], k_k[i], k_a[i])
        out_args = (ln_w[i], ln_b[i], r_k[i], g_up[i])
        yc_rw, s_ctx = rwkv_mix(rwkv_streams(conv3(pc[..., :RW_COLS], rw_shift[i]), *rw_args),
                                (s_zero, s_zero), *out_args)
        yx_rw, _ = rwkv_mix(rwkv_streams(conv3(px[..., :RW_COLS], rw_shift[i]), *rw_args),
                            s_ctx, *out_args)
        yx = jnp.concatenate([yx_rw.astype(px.dtype),
                              short_conv_mix(px, conv_w[i], grid_conv3),
                              fourier_mix(px)], axis=-1) @ w_out[i]
        x = x + ga1 * yx
        x = x + ga2 * ffn(modulate(rms_norm(x, norm_ffn[i]), sh2, sc2),
                          w_gate[i], w_up[i], w_down[i])
        if i < DEPTH - 1:
            yc = jnp.concatenate([yc_rw.astype(pc.dtype),
                                  short_conv_mix(pc, conv_w[i], conv3),
                                  fourier_mix(pc)], axis=-1) @ w_out[i]
            xc = xc + cga1 * yc
            xc = xc + cga2 * ffn(modulate(rms_norm(xc, norm_ffn[i]), csh2, csc2),
                                 w_gate[i], w_up[i], w_down[i])
    return rms_norm(x, norm_final)


D_MIX_2 = D_MODEL
D_LRU = D_MIX_2 // 2
D_RET = D_MIX_2 - D_LRU
LRU_BLOCKS = 8
LRU_BLOCK_W = D_LRU // LRU_BLOCKS
CONV_W = 4
LRU_C = 8.0
RET_HEADS = 8
RET_HD = D_RET // RET_HEADS
CHUNK = 128
ROPE_BASE = 10000.0
D_FF_2 = ((8 * D_MODEL + 3 * 256 - 1) // (3 * 256)) * 256
EPS = 1e-6
SPLITS = (D_LRU, 2 * D_LRU, 2 * D_LRU + D_RET, 2 * D_LRU + 2 * D_RET, 2 * D_LRU + 3 * D_RET)
D_IN_2 = 2 * D_LRU + 4 * D_RET


def rmsnorm(x, w):
    xf = x.astype(jnp.float32)
    y = xf * lax.rsqrt(jnp.mean(xf * xf, axis=-1, keepdims=True) + EPS)
    return (y * w.astype(jnp.float32)).astype(x.dtype)

def causal_depthwise_conv(x, w, b):
    S = x.shape[1]
    xp = jnp.pad(x, ((0, 0), (CONV_W - 1, 0), (0, 0)))
    y = b
    for tap in range(CONV_W):
        y = y + xp[:, tap:tap + S, :] * w[tap]
    return y

def rg_lru(u, wa, ba, wx, bx, lam):
    B, S, _ = u.shape
    uf = u.astype(jnp.float32)
    ub = uf.reshape(B, S, LRU_BLOCKS, LRU_BLOCK_W)
    r = jax.nn.sigmoid(jnp.einsum('bsnc,ncd->bsnd', ub, wa.astype(jnp.float32)).reshape(B, S, D_LRU) + ba)
    i = jax.nn.sigmoid(jnp.einsum('bsnc,ncd->bsnd', ub, wx.astype(jnp.float32)).reshape(B, S, D_LRU) + bx)
    log_a = LRU_C * r * jax.nn.log_sigmoid(lam.astype(jnp.float32))
    a = jnp.exp(log_a)
    b = jnp.sqrt(-jnp.expm1(2.0 * log_a)) * (i * uf)

    def combine(left, right):
        a1, b1 = left
        a2, b2 = right
        return a1 * a2, a2 * b1 + b2

    _, h = lax.associative_scan(combine, (a, b), axis=1)
    return h.astype(u.dtype)

def rope(t, cos, sin):
    half = t.shape[-1] // 2
    t1, t2 = t[..., :half], t[..., half:]
    c = cos[None, :, None, :]
    s = sin[None, :, None, :]
    return jnp.concatenate([t1 * c - t2 * s, t1 * s + t2 * c], axis=-1)

def retention(q, k, v, g, gn_w):
    B, S, _ = q.shape
    H, Dh, C = RET_HEADS, RET_HD, CHUNK
    N = S // C
    f32 = jnp.float32
    pos = jnp.arange(S, dtype=f32)
    inv_freq = ROPE_BASE ** (-jnp.arange(0, Dh, 2, dtype=f32) / Dh)
    ang = pos[:, None] * inv_freq[None, :]
    cos, sin = jnp.cos(ang), jnp.sin(ang)
    qh = rope(q.astype(f32).reshape(B, S, H, Dh), cos, sin)
    kh = rope(k.astype(f32).reshape(B, S, H, Dh), cos, sin) * (Dh ** -0.5)
    vh = v.astype(f32).reshape(B, S, H, Dh)
    qc = qh.reshape(B, N, C, H, Dh)
    kc = kh.reshape(B, N, C, H, Dh)
    vc = vh.reshape(B, N, C, H, Dh)

    log_gamma = jnp.log1p(-jnp.exp2(-5.0 - jnp.arange(H, dtype=f32)))
    idx = jnp.arange(C)
    diff = idx[:, None] - idx[None, :]
    causal = diff >= 0
    decay = jnp.where(causal[None], jnp.exp(log_gamma[:, None, None] * jnp.where(causal, diff, 0)[None].astype(f32)), 0.0)

    scores = jnp.einsum('bnqhd,bnkhd->bnhqk', qc, kc) * decay[None, None]
    inner = jnp.einsum('bnhqk,bnkhe->bnqhe', scores, vc)

    zeta = jnp.exp(log_gamma[None, :] * (C - 1 - idx).astype(f32)[:, None])
    kv = jnp.einsum('bnkhd,bnkhe->bnhde', kc * zeta[:, :, None], vc)
    chunk_decay = jnp.exp(log_gamma * C)[:, None, None]

    def step(R, kv_n):
        return R * chunk_decay + kv_n, R

    _, R_prev = lax.scan(step, jnp.zeros((B, H, Dh, Dh), f32), jnp.moveaxis(kv, 1, 0))
    R_prev = jnp.moveaxis(R_prev, 0, 1)

    xi = jnp.exp(log_gamma[None, :] * (idx + 1).astype(f32)[:, None])
    cross = jnp.einsum('bnqhd,bnhde->bnqhe', qc * xi[:, :, None], R_prev)
    o = (inner + cross).reshape(B, S, H, Dh)

    mu = jnp.mean(o, axis=-1, keepdims=True)
    var = jnp.mean(jnp.square(o - mu), axis=-1, keepdims=True)
    on = ((o - mu) * lax.rsqrt(var + EPS)).reshape(B, S, D_RET) * gn_w.astype(f32)
    return (jax.nn.silu(g.astype(f32)) * on).astype(q.dtype)

def second_inputs(seed: int = 0) -> dict:
    key = jax.random.key(seed)
    ks = jax.random.split(key, 20)
    f32 = jnp.float32

    def nrm(k, shape, scale):
        return jax.random.normal(k, shape, f32) * scale

    u = jax.random.uniform(ks[8], (DEPTH, D_LRU), f32, 0.9, 0.999)
    s = u ** (1.0 / LRU_C)
    lru_lambda = jnp.log(s) - jnp.log1p(-s)
    return {
        "x": nrm(ks[0], (BATCH, SEQ, D_MODEL), 1.0),
        "ln1_w": 1.0 + nrm(ks[1], (DEPTH, D_MODEL), 0.02),
        "w_in": nrm(ks[2], (DEPTH, D_MODEL, D_IN_2), D_MODEL ** -0.5),
        "conv_w": nrm(ks[3], (DEPTH, CONV_W, D_LRU), CONV_W ** -0.5),
        "conv_b": nrm(ks[4], (DEPTH, D_LRU), 0.01),
        "gate_a_w": nrm(ks[5], (DEPTH, LRU_BLOCKS, LRU_BLOCK_W, LRU_BLOCK_W), LRU_BLOCK_W ** -0.5),
        "gate_a_b": nrm(ks[6], (DEPTH, D_LRU), 0.01),
        "gate_x_w": nrm(ks[7], (DEPTH, LRU_BLOCKS, LRU_BLOCK_W, LRU_BLOCK_W), LRU_BLOCK_W ** -0.5),
        "gate_x_b": nrm(ks[9], (DEPTH, D_LRU), 0.01),
        "lru_lambda": lru_lambda,
        "ret_gn_w": 1.0 + nrm(ks[10], (DEPTH, D_RET), 0.02),
        "w_out": nrm(ks[11], (DEPTH, D_MIX_2, D_MODEL), D_MIX_2 ** -0.5),
        "ln2_w": 1.0 + nrm(ks[12], (DEPTH, D_MODEL), 0.02),
        "w_ffn_gate": nrm(ks[13], (DEPTH, D_MODEL, D_FF_2), D_MODEL ** -0.5),
        "w_ffn_up": nrm(ks[14], (DEPTH, D_MODEL, D_FF_2), D_MODEL ** -0.5),
        "w_ffn_down": nrm(ks[15], (DEPTH, D_FF_2, D_MODEL), D_FF_2 ** -0.5),
        "final_norm_w": 1.0 + nrm(ks[16], (D_MODEL,), 0.02),
    }

def second_block(x, ln1_w, w_in, conv_w, conv_b, gate_a_w, gate_a_b, gate_x_w, gate_x_b,
              lru_lambda, ret_gn_w, w_out, ln2_w, w_ffn_gate, w_ffn_up, w_ffn_down, final_norm_w):
    h = x
    for l in range(DEPTH):
        u = rmsnorm(h, ln1_w[l])
        proj = jnp.einsum('bsd,de->bse', u, w_in[l])
        lru_x, lru_g, q, k, v, ret_g = jnp.split(proj, SPLITS, axis=-1)
        lru_x = causal_depthwise_conv(lru_x, conv_w[l], conv_b[l])
        y_lru = rg_lru(lru_x, gate_a_w[l], gate_a_b[l], gate_x_w[l], gate_x_b[l], lru_lambda[l])
        y_lru = y_lru * jax.nn.gelu(lru_g)
        y_ret = retention(q, k, v, ret_g, ret_gn_w[l])
        y = jnp.concatenate([y_lru, y_ret], axis=-1)
        h = h + jnp.einsum('bse,ed->bsd', y, w_out[l])
        u = rmsnorm(h, ln2_w[l])
        ff = jax.nn.silu(jnp.einsum('bsd,df->bsf', u, w_ffn_gate[l])) * jnp.einsum('bsd,df->bsf', u, w_ffn_up[l])
        h = h + jnp.einsum('bsf,fd->bsd', ff, w_ffn_down[l])
    return rmsnorm(h, final_norm_w)


def setup_inputs(seed=0):
    out = dict(first_inputs(seed))
    for name, value in second_inputs(seed + 1).items():
        if name != "x":
            out[name + "_2"] = value
    return out


def reference(
    x, c, ctx, c_ctx, w_mod, b_mod, norm_mix, w_in, rw_shift, dec_w0, dec_up, iclr_a0, iclr_up,
    k_k, k_a, r_k, ln_w, ln_b, g_up, conv_w, w_out, norm_ffn, w_gate, w_up, w_down, norm_final,
    ln1_w_2, w_in_2, conv_w_2, conv_b_2, gate_a_w_2, gate_a_b_2, gate_x_w_2, gate_x_b_2,
    lru_lambda_2, ret_gn_w_2, w_out_2, ln2_w_2, w_ffn_gate_2, w_ffn_up_2, w_ffn_down_2,
    final_norm_w_2,
):
    x = first_block(
        x, c, ctx, c_ctx, w_mod, b_mod, norm_mix, w_in, rw_shift, dec_w0, dec_up, iclr_a0,
        iclr_up, k_k, k_a, r_k, ln_w, ln_b, g_up, conv_w, w_out, norm_ffn, w_gate, w_up, w_down,
        norm_final,
    )
    return second_block(
        x, ln1_w_2, w_in_2, conv_w_2, conv_b_2, gate_a_w_2, gate_a_b_2, gate_x_w_2, gate_x_b_2,
        lru_lambda_2, ret_gn_w_2, w_out_2, ln2_w_2, w_ffn_gate_2, w_ffn_up_2, w_ffn_down_2,
        final_norm_w_2,
    )


_drawn_inputs = setup_inputs


def setup_inputs(seed=0):
    import zlib

    import numpy as np

    out = dict(_drawn_inputs(seed))
    spreads = {}
    factors = {'dec_up': 6.767,
     'iclr_a0': 7.636,
     'k_k': 3.598,
     'k_a': 3.418,
     'ln_w': 6.689,
     'ln_b': 8.0,
     'norm_ffn': 2.761,
     'ln1_w_2': 2.996,
     'conv_b_2': 9.433,
     'gate_a_b_2': 64.0,
     'gate_x_b_2': 61.984,
     'ret_gn_w_2': 6.841,
     'ln2_w_2': 4.01,
     'final_norm_w_2': 7.625}
    for name, (base, spread) in spreads.items():
        noise = np.random.default_rng([zlib.crc32(name.encode()), seed]).standard_normal(out[name].shape)
        drawn = base * np.exp(spread * noise) if base else spread * noise
        out[name] = jnp.asarray(drawn.astype(out[name].dtype))
    for name, factor in factors.items():
        out[name] = (out[name] * factor).astype(out[name].dtype)
    return out
```

```python
from contextlib import ExitStack

import numpy as np

import concourse.bass as bass
from concourse import mybir

F32 = mybir.dt.float32
F32R = mybir.dt.float32r
ALU = mybir.AluOpType
ACT = mybir.ActivationFunctionType
ds = bass.ds

P = 128
D = 2048
T = 256
KB = D // P
HEAD = 64
D_RWKV, D_CONV, D_FOUR = D // 2, D // 4, D // 4
RB = D_RWKV // P
LORA = 96
GATE = 256
D_FF = ((8 * D + 3 * 256 - 1) // (3 * 256)) * 256
FB = D_FF // P
WD0 = 3 * D_RWKV
GD0 = WD0 + 2 * LORA
CG0 = GD0 + GATE
D_IN = CG0 + 3 * D_CONV + D_FOUR
D_IN_2 = 6 * (D // 2)
GRID_W = 64
RMS_EPS, GN_EPS, KK_EPS = 1e-6, 64e-5, 1e-12
LRU_BLOCKS, LRU_C = 8, 8.0
RET_HEADS = 8
DECAY_SCALE = -float(np.exp(np.float32(-0.5)))

RING = 4
CK, CN = 4, 256
BANK = 512
C = 64
NC = T // C

STREAM = [
    ("mod", 6, 8, KB), ("in_kv", 4, 2, KB), ("in_lora", 1, 2, KB), ("in_r", 2, 2, KB), ("in_rest", 4, 2, KB),
    ("out", 4, 2, KB), ("ffn", 22, 2, KB), ("down", 2, 4, FB),
    ("in_2", 12, 2, KB), ("out_2", 4, 2, KB), ("ffn_2", 22, 2, KB), ("down_2", 2, 4, FB),
]


class Phase:

    def __init__(self, name, trips, pairs, rows, g0, p0):
        self.name, self.trips, self.pairs, self.rows = name, trips, pairs, rows
        self.per_pair = rows // CK
        self.chunks = pairs * self.per_pair
        self.g0, self.p0 = g0, p0

    def chunk(self, i, j):
        return i * self.chunks + (self.g0 + j)

    def slot(self, j):
        return (self.g0 + j) % RING

    def rounds(self, i, j):
        return i * (self.chunks // RING) + (self.g0 + j) // RING

    def pair(self, i, p):
        return i * self.pairs + (self.p0 + p)

    def bank(self, p):
        return 2 * ((self.p0 + p) % 2)

    def last_chunk(self, i, p):
        return self.chunk(i, (p + 1) * self.per_pair - 1)


def phases():
    out, g, p = {}, 0, 0
    for name, trips, pairs, rows in STREAM:
        ph = Phase(name, trips, pairs, rows, g, p)
        assert trips == 1 or ph.chunks % RING == 0
        out[name] = ph
        g += trips * ph.chunks
        p += trips * pairs
    return out, g


class Steps:

    def __init__(self, sem, names):
        self.sem, self.names = sem, list(names)
        assert len(set(self.names)) == len(self.names)
        self.at = 0

    def value(self, name, rounds=0):
        return rounds * len(self.names) + (self.names.index(name) + 1)

    def done(self, ins, name):
        assert self.names[self.at % len(self.names)] == name, (name, self.names[self.at % len(self.names)])
        self.at += 1
        ins.then_inc(self.sem, 1)

    def wait(self, eng, name, rounds=0):
        eng.wait_ge(self.sem, self.value(name, rounds))


class Chain:

    def __init__(self, eng, sem):
        self.eng, self.sem, self.base, self.n, self.i, self.per = eng, sem, 0, 0, None, 0

    def loop(self, i, per):
        self.base, self.i, self.per, self.n = self.base + self.n, i, per, 0

    def end(self, trips):
        assert self.n == self.per, (self.n, self.per)
        self.base, self.n, self.i = self.base + trips * self.per, 0, None

    def mark(self, ins):
        ins.then_inc(self.sem, 1)
        self.n += 1
        return self.base + self.n if self.i is None else self.i * self.per + (self.base + self.n)

    def wait(self, value):
        self.eng.wait_ge(self.sem, value)

    def __call__(self, ins):
        self.wait(self.mark(ins))


def vector_rows():
    order = [
        [("b_mod", 96), ("norm_mix", 16), ("norm_ffn", 16)],
        [("ln1_w_2", 16), ("ln2_w_2", 16), ("norm_final", 16), ("final_norm_w_2", 16), ("dec_w0", 16),
         ("iclr_a0", 16), ("k_k", 8), ("k_a", 8), ("r_k", 8), ("ln_w", 8)],
        [("ln_b", 8), ("conv_w", 12), ("conv_w_2", 32), ("conv_b_2", 8), ("gate_a_b_2", 8), ("gate_x_b_2", 8),
         ("lru_lambda_2", 8), ("ret_gn_w_2", 8), ("c", 16), ("c_ctx", 16)],
        [("shift_rkv", 72), ("shift_gd", 6), ("shift_wd", 3), ("shift_ad", 3)],
    ]
    out = {}
    for t, row in enumerate(order):
        at = 0
        for name, n in row:
            out[name] = (t, at, n)
            at += n
        assert at <= P
    return out


VROWS = vector_rows()


def constants():
    f = np.float32
    eye = np.eye(P, dtype=f)
    blk = np.kron(np.eye(2, dtype=f), np.ones((HEAD, HEAD), f))
    sel = np.zeros((P, P), f)
    sel[0, 0] = sel[1, 0] = sel[2, 1] = sel[3, 1] = 1
    n = np.arange(HEAD)
    cos_h = np.cos(2 * np.pi * np.outer(n, n) / HEAD)
    sin_h = np.sin(2 * np.pi * np.outer(n, n) / HEAD)
    four_h = np.concatenate([np.kron(np.eye(2), cos_h), np.kron(np.eye(2), sin_h)], 1)
    m = np.arange(T)
    ang = 2 * np.pi * (np.outer(m, m) % T) / T
    norm = 1 / np.sqrt(T * HEAD)
    four_t = np.stack([np.cos(ang) * norm, -np.sin(ang) * norm], 1)
    four_t = four_t.reshape(2, P, 2, T).transpose(1, 0, 2, 3).reshape(P, 4 * T)
    basics = np.concatenate([eye, blk, sel, np.ones((P, P), f)], 1).astype(f)
    fourier = np.concatenate([four_h, four_t], 1).astype(f)

    s, t = np.arange(C)[:, None], np.arange(C)[None, :]
    scan = []
    for d in range(2):
        before = s < t if d == 0 else s > t
        two = lambda a: np.kron(np.eye(2), a)
        row = [two(before)]
        size = 1
        while size < C:
            row.append(two(before & (s // (2 * size) == t // (2 * size)) & (s // size != t // size)))
            size *= 2
        scan += row + [np.concatenate([before | (s == t)] * 2, 0)]
    first = np.tile((np.arange(T) % C != 0).astype(f), (P, 1))
    scan = np.concatenate(scan + [first], 1).astype(f)

    half = P // 2
    inv_freq = f(10000.0) ** (-np.arange(0, P, 2, dtype=f) / f(P))
    rot = np.arange(T, dtype=f)[None, :] * inv_freq[:, None]
    cos, sin = np.cos(rot).astype(f), np.sin(rot).astype(f)
    swap = np.zeros((P, P), f)
    swap[np.arange(half) + half, np.arange(half)] = -1
    swap[np.arange(half), np.arange(half) + half] = 1
    log_gamma = np.log1p(-np.exp2(-5.0 - np.arange(RET_HEADS)))
    sp, tt = np.arange(P)[:, None], np.arange(T)[None, :]
    decay = []
    for h in range(RET_HEADS):
        d0 = np.where(tt >= sp, np.exp(log_gamma[h] * np.maximum(tt - sp, 0)) * P ** -0.5, 0)
        decay += [d0, d0[:, :P]]
    ret = np.concatenate([np.concatenate([cos, cos], 0), np.concatenate([sin, sin], 0), swap] + decay, 1).astype(f)
    return {"k_basics": basics, "k_fourier": fourier, "k_scan": scan, "k_ret": ret}


LEVELS = 6
SCAN_DIR = P * (1 + LEVELS) + C


def program(nc, A, out):
    PH, TOTAL = phases()
    order = [PH[row[0]] for row in STREAM]
    base = -(-nc.sbuf_base // 32) * 32
    KIB = 1024

    def at(name, offset, shape, dt=F32):
        return nc.alloc_sbuf_tensor_at(name, shape, dt, offset=base + offset)

    raw = at("raw", 0, [P, RING, CK, CN])
    hi = at("hi", 16 * KIB, [P, RING, CK, CN], F32R)
    lo = at("lo", 32 * KIB, [P, RING, CK, CN], F32R)
    fix = 48 * KIB
    vec = at("vec", fix, [P, 4, P])
    mod = at("mod", fix + 2048, [P, 6, 2, KB])
    gain = at("gain", fix + 2816, [P, 4, KB])
    lcol = at("lcol", fix + 3072, [P, 8, RB])
    basics = at("basics", fix + 3584, [P, 4, P])
    rstd = at("rstd", fix + 5632, [P, 2, T])
    tmp = at("tmp", fix + 7680, [P, 2, 2, T])
    sq = at("sq", fix + 11776, [P, 2, 2 * T])
    nt = at("nt", fix + 15872, [P, 2, 2 * T])
    gd = at("gd", fix + 11776, [P, 2, T])
    wdad = at("wdad", fix + 13824, [P, 2, 2, T])
    px = at("px", fix + 17920, [P, 2, T])
    decw = at("decw", fix + 17920, [P, 4, P])
    xT = at("xT", 68 * KIB, [P, KB, T])
    ymix = at("ymix", 68 * KIB, [P, KB, T])
    R = 84 * KIB
    xrow = at("xrow", R, [P, 2, D])
    crow = at("crow", R + 16 * KIB, [P, 2, D])
    vrow = at("vrow", R + 32 * KIB, [P, 4, P])
    ctxT = at("ctxT", R + 40 * KIB, [P, KB, T])
    c4 = at("c4", R + 56 * KIB, [P, KB, P], F32R)
    csil = at("csil", R + 64 * KIB, [P, 2, KB])
    mrow = at("mrow", R + 66 * KIB, [4, D])
    kv = at("kv", R, [P, 2 * RB, 2, T])
    r = at("r", R + 32 * KIB, [P, RB, T])
    proj = at("proj", R + 40 * KIB, [P, 16, T])
    mov1 = at("mov1", R + 56 * KIB, [P, KB, 2, 2, T], F32R)

    oka = lcol[:, 0, :]
    ident, blk64, sel, ones = (basics[:, n, :] for n in range(4))
    ps = nc.alloc_psum_tensor("ps", [P, 8, BANK], F32)

    xres = nc.dram_tensor("xres", [P, KB * T], F32, kind="Internal").ap()

    def vcol(name, n, count=1, rows=P):
        t, first, _ = VROWS[name]
        return vec[0:rows, t, ds(first + n, count)]

    sems = {}

    def sem(name):
        sems[name] = nc.alloc_semaphore(name)
        return sems[name]

    raw_in = [sem(f"raw_in{s}") for s in range(RING)]
    hi_ready, lo_ready, split_free = sem("hi_ready"), sem("lo_ready"), sem("split_free")
    bank_free, tmp_ready = sem("bank_free"), sem("tmp_ready")
    SPLIT_CREDIT, BANK_CREDIT = RING, 2
    LOWS0 = PH["in_lora"].p0 + 1
    v_chain, a_chain, g_chain = sem("v_chain"), sem("a_chain"), sem("g_chain")
    vec_clear, vec_in, row_in, const_in = sem("vec_clear"), sem("vec_in"), sem("row_in"), sem("const_in")
    vec_turned, vec_ready = sem("vec_turned"), sem("vec_ready")
    turned, ctx_out, x_out = sem("turned"), sem("ctx_out"), sem("x_out")
    csil_ready, chi_ready, c4_clear, c4_ready = sem("csil_ready"), sem("chi_ready"), sem("c4_clear"), sem("c4_ready")
    mrow_ready, mcol_ready, mod_ready, gain_ready = (sem(n) for n in ("mrow_ready", "mcol_ready", "mod_ready", "gain_ready"))
    sq_ready, sq_used, var_ready, sqrt_ready, rstd_ready = (
        sem(n) for n in ("sq_ready", "sq_used", "var_ready", "sqrt_ready", "rstd_ready"))
    nt_ready, nhi_ready, mov_ready = sem("nt_ready"), sem("nhi_ready"), sem("mov_ready")
    shift_ready = sem("shift_ready")
    M0 = R + 56 * KIB
    kfour = at("kfour", M0, [P, 5, T])
    uf = at("uf", M0 + 5 * KIB, [P, 2, 4, 2, P])
    x_spilled, four_in, uf_turned, uf_ready, four_done, conv_mid, mix_done = (
        sem(n) for n in ("x_spilled", "four_in", "uf_turned", "uf_ready", "four_done", "conv_mid",
                         "mix_done"))
    REST_DONE = PH["in_rest"].last_chunk(3, 1) + 1 + SPLIT_CREDIT
    REST_OUT = PH["in_rest"].pair(3, 1) + 1 + BANK_CREDIT

    def per_dir(name, offset, shape, step):
        return [at(f"{name}{d}", offset + d * step, shape) for d in range(2)]

    kscan = at("kscan", R + 40 * KIB, [P, 2 * SCAN_DIR + T])
    strict = [kscan[:, d * SCAN_DIR:d * SCAN_DIR + P] for d in range(2)]
    level = [[kscan[:, d * SCAN_DIR + (1 + n) * P:d * SCAN_DIR + (2 + n) * P] for n in range(LEVELS)] for d in range(2)]
    upto = [kscan[:, d * SCAN_DIR + (1 + LEVELS) * P:(d + 1) * SCAN_DIR] for d in range(2)]
    inside = kscan[:, 2 * SCAN_DIR:2 * SCAN_DIR + T]
    S0 = R + 49 * KIB
    bdV = at("bdV", S0, [P, NC, P])
    tokV = at("tokV", S0 + 2048, [P, NC, P])
    S = per_dir("S", S0 + 4096, [P, P], 512)
    pc = per_dir("pc", S0 + 5120, [P, NC], 32)
    kk = at("kk", fix + 5632, [P, 2 * T])
    kq = at("kq", fix + 7680, [P, 2 * T])
    kn = at("kn", fix + 9728, [P, 2 * T])
    DIR = 33 * KIB
    bdA = per_dir("bdA", M0, [P, NC, P + C], DIR)
    bdB = per_dir("bdB", M0 + 3072, [P, NC, P], DIR)
    bdK = per_dir("bdK", M0 + 5120, [P, NC, P], DIR)
    tokR = per_dir("tokR", M0 + 7168, [P, NC, 2, P], DIR)
    tokBQ = per_dir("tokBQ", M0 + 11264, [P, NC, P + C], DIR)
    tokK = per_dir("tokK", M0 + 14336, [P, NC, P], DIR)
    U = per_dir("U", M0 + 16384, [P, NC, P], DIR)
    ULa = per_dir("ULa", M0 + 18432, [P, NC, P], DIR)
    MT = per_dir("MT", M0 + 20480, [P, NC, P], DIR)
    RT = per_dir("RT", M0 + 22528, [P, NC, C], DIR)
    XY = per_dir("XY", M0 + 23552, [P, NC, 2, P], DIR)
    lw, L, ex, en, av, kd = ([x for x in per_dir(n, M0 + 27648 + 1024 * k, [P, T], DIR)]
                             for k, n in enumerate(("lw", "L", "ex", "en", "av", "kd")))
    XT, AT, BM = bdB, U, bdK

    bcol = lcol[:, 6, 0:4]

    def scan_steps(sems_of, names):
        return [Steps(sems_of[d], [(q, n) for q in range(2) for n in names(q, d)]) for d in range(2)]

    def pe_names(q, d):
        out = (["kk"] if q == 0 and d == 0 else []) + ["zz"] + (["rk"] if q and d else []) + ["G1", "G2", "tA", "tB", "tK"]
        out += (["tV"] if d == 0 else []) + ["MV", "L0"]
        for l in range(1, LEVELS):
            out += [f"Y{l}", f"X{l}"]
        return out + ["Z", "A", "B"] + [f"st{n}" for n in range(NC)]

    def act_names(q, d):
        out = (["bc0", "bc1", "ksq", "ksqrt"] if q == 0 and d == 0 else []) + (["bv0", "bv1"] if d == 0 else [])
        out += ["sg", "sa", "eex", "en", "pc"] + (["ep"] if q else []) + ["U", "oA", "oB", "oK"] + (["oV"] if d == 0 else [])
        return out + ["oMV"] + [f"Yb{l}" for l in range(1, LEVELS)] + ["Z"]

    def dve_names(q, d):
        out = (["kq", "kv", "n0", "n1", "n2", "n3", "n4", "kk"] if q == 0 and d == 0 else []) + (["S"] if q == 0 else [])
        out += ["lw", "L", "Lx", "kf", "kd", "ba"] + (["rk0", "rk1", "bonus"] if q and d else [])
        out += ["a0", "a1", "b0", "b1", "k0", "k1"] + (["rho", "Q", "R"] if q else []) + ["M", "T0", "X0"]
        for l in range(1, LEVELS):
            out += ([f"X{l}"] if l < LEVELS - 1 else []) + [f"T{l}"]
        out += ["AT"] + (["rho2"] if q else []) + ["Bm"] + (["Y0"] if q else [])
        return out + [f"s{n}" for n in range(NC - q)] + (["y"] if q else [])

    def pool_names(q, d):
        return [f"m{l}" for l in range(LEVELS)]

    scan_pe = scan_steps([sem(f"scan_pe{d}") for d in range(2)], pe_names)
    scan_act = scan_steps([sem(f"scan_act{d}") for d in range(2)], act_names)
    scan_dve = scan_steps([sem(f"scan_dve{d}") for d in range(2)], dve_names)
    scan_pool = scan_steps([sem(f"scan_pool{d}") for d in range(2)], pool_names)
    decw_in, kscan_in, bd_clear, wd_ready = sem("decw_in"), sem("kscan_in"), sem("bd_clear"), sem("wd_ready")

    def in_order(d):
        return range(NC) if d == 0 else range(NC - 1, -1, -1)

    def chunks_of(ap):
        return ap.rearrange("p (c t) -> p c t", c=NC)

    def over_chunks(ap):
        n = ap.shape[-1]
        return ap.rearrange("p (a n) -> p a n", a=1).broadcast_to([P, NC, n])

    def over_banks(ap):
        n = ap.shape[-1]
        return ap.rearrange("p (a b n) -> p a b n", a=1, b=1).broadcast_to([P, 2, NC // 2, n])

    def two_banks(b, width, first, count):
        return ps[:, b:b + 2, 0:2 * width].rearrange("p b (c n) -> p b c n", c=2)[:, :, :, first:first + count]

    def in_pairs(ap):
        return ap.rearrange("p (a b) n -> p a b n", a=2)

    gup = at("gup", M0, [P, 2, D_RWKV])
    gate = at("gate", M0 + 8 * KIB, [P, RB, T])
    yc = at("yc", M0 + 16 * KIB, [P, 2 * T])
    ysq = at("ysq", M0 + 18 * KIB, [P, 2 * T])
    yv = at("yv", M0 + 20 * KIB, [P, 2 * T])
    yn = at("yn", M0 + 22 * KIB, [P, 2 * T])
    gup_in, gd_ready, gate_mm, gate_out, gn_pe, gn_act, gn_dve, ymix_done = (
        sem(n) for n in ("gup_in", "gd_ready", "gate_mm", "gate_out", "gn_pe", "gn_act", "gn_dve", "ymix_done"))
    gnp, gna, gnd = (Steps(s, n) for s, n in (
        (gn_pe, ["mean", "var"]), (gn_act, ["sq", "sqrt", "w0", "w1"]),
        (gn_dve, ["c", "v", "n0", "n1", "n2", "n3", "n4", "yn", "b", "g"])))

    mov = at("mov", R + 88 * KIB, [P, KB, 2, T], F32R)
    hid = at("hid", R, [P, FB, 2, T], F32R)
    gbuf = at("gbuf", fix + 11776, [P, 2, T])
    sbuf = at("sbuf", fix + 13824, [P, 2, T])
    ubuf = at("ubuf", fix + 15872, [P, 2, T])
    yhi, ylo, x_back, res_done = sem("yhi"), sem("ylo"), sem("x_back"), sem("res_done")
    ffn_g, ffn_s, ffn_h, ffn_hi, ffn_lo = (sem(n) for n in ("ffn_g", "ffn_s", "ffn_h", "ffn_hi", "ffn_lo"))
    knt = at("knt", M0 + 27648, [P, 2 * T])

    LX, LG, RQ, RK, RV, RG = (n * RB for n in range(6))
    p2 = at("p2", R, [P, 6 * RB, T])
    lu = at("lu", R + 48 * KIB, [P, RB, T])
    la = at("la", R + 56 * KIB, [P, RB, T])
    lb = at("lb", R + 64 * KIB, [P, RB, T])
    linv = at("linv", R + 72 * KIB, [P, RB, T])
    gw = at("gw", R + 80 * KIB, [P, 2, LRU_BLOCKS, P])
    Q0 = R + 88 * KIB
    KRET = 2 * T + P + RET_HEADS * (T + P)
    kret = at("kret", Q0, [P, KRET])
    rcos, rsin = (kret[:, n * T:(n + 1) * T] for n in range(2))
    swap = kret[:, 2 * T:2 * T + P]
    rqk = at("rqk", Q0 + 14848, [P, 2, T])
    rqc = at("rqc", Q0 + 16896, [P, 2, T])
    rv = at("rv", Q0 + 18944, [P, T])
    rvt = at("rvt", Q0 + 19968, [P, 2, P])
    rp = at("rp", Q0 + 20992, [P, T + P])
    ro = at("ro", Q0 + 22528, [P, RET_HEADS, T])
    oc, osq, ov, on = (at(n, fix + 11776 + 2048 * k, [P, 2 * T]) for k, n in enumerate(("oc", "osq", "ov", "on")))
    orow = at("orow", R, [P, 2, D])
    IN2_DONE = PH["in_2"].last_chunk(11, 1) + 1 + SPLIT_CREDIT
    IN2_OUT = PH["in_2"].pair(11, 1) + 1 + BANK_CREDIT
    x_done, x_scaled, lam_exp, lam_ready, gw_in, kret_in = (
        sem(n) for n in ("x_done", "x_scaled", "lam_exp", "lam_ready", "gw_in", "kret_in"))
    lru_mid, lru_u, lru_gates, lru_i, lru_t, lru_sq, lru_iu, lru_out, lru_gelu, ret_silu = (
        sem(n) for n in ("lru_mid", "lru_u", "lru_gates", "lru_i", "lru_t", "lru_sq", "lru_iu", "lru_out", "lru_gelu", "ret_silu"))
    retp, reta, retd, retg = (Steps(sem(s), n) for s, n in (
        ("ret_pe", ["vt", "sw", "sc", "o"]), ("ret_act", ["vt", "o"]), ("ret_dve", ["qs", "qr", "pr"]), ("ret_pool", ["v", "qc"])))
    rnp, rna, rnd = (Steps(sem(s), n) for s, n in (
        ("rn_pe", ["mean", "var"]), ("rn_act", ["sq", "sqrt"]),
        ("rn_dve", ["c", "v", "n0", "n1", "n2", "n3", "n4", "yn", "w0", "w1", "g"])))
    y2_done, y2_hi, y2_lo, row_turned, row_act, row_dve, result_out = (
        sem(n) for n in ("y2_done", "y2_hi", "y2_lo", "row_turned", "row_act", "row_dve", "result_out"))

    def both(ap):
        return ap.rearrange("p (a n) -> p a n", a=1).broadcast_to([P, 2, T])

    def qk_of(h):
        return p2[:, RQ:RQ + 2 * RB, :].rearrange("p (a h) t -> p a h t", a=2)[:, :, ds(h, 1), :]

    def weights(w, rows, col):
        return w[rows * P:(rows + CK) * P, ds(col, CN)].rearrange("(k p) n -> p k n", p=P)

    def chunk_source(ph, i, j):
        p, q = j // ph.per_pair, (j % ph.per_pair) * CK
        if ph.name == "mod":
            return weights(A["w_mod"], q, i * D + p * CN)
        if ph.name == "in_kv":
            return weights(A["w_in"], q, i * (2 * CN) + (D_RWKV + p * CN))
        if ph.name == "in_lora":
            return weights(A["w_in"], q, (WD0, GD0)[p])
        if ph.name == "in_r":
            return weights(A["w_in"], q, i * (2 * CN) + p * CN)
        if ph.name == "in_rest":
            return weights(A["w_in"], q, i * (2 * CN) + (CG0 + p * CN))
        if ph.name in ("ffn", "ffn_2"):
            tail = "" if ph.name == "ffn" else "_2"
            w = A[("w_gate", "w_up")[p]] if not tail else A[("w_ffn_gate_2", "w_ffn_up_2")[p]]
            return weights(w, q, i * CN)
        w = {"out": "w_out", "down": "w_down", "in_2": "w_in_2", "out_2": "w_out_2", "down_2": "w_ffn_down_2"}[ph.name]
        return weights(A[w], q, i * (ph.pairs * CN) + p * CN)

    def loop(eng, ph, body):
        if ph.trips == 1:
            body(0)
            return
        ends = ph is order[-1]
        with eng.Fori(0, ph.trips - ends) as i:
            body(i)
        if ends:
            body(ph.trips - 1)

    with nc.Block() as block:

        @block.sync
        def _(sp):
            sp.dma_start(xrow[:, :, :], A["x"][0].rearrange("(a p) d -> p a d", p=P)).then_inc(row_in, 16)
            sp.dma_start(crow[:, :, :], A["ctx"][0].rearrange("(a p) d -> p a d", p=P)).then_inc(row_in, 16)
            for ph in order:
                def trip(i):
                    for j in range(ph.chunks):
                        sp.wait_ge(lo_ready, ph.chunk(i, j) + 1)
                        sp.dma_start(raw[:, ph.slot(j), :, :], chunk_source(ph, i, j)).then_inc(raw_in[ph.slot(j)], 16)
                if ph.name == "in_r":
                    sp.wait_ge(mov_ready, 2 * KB)
                    sp.dma_start(xres.rearrange("p (k t) -> p k t", k=KB), xT[:, :, :]).then_inc(x_spilled, 16)
                loop(sp, ph, trip)
            for n in range(8):
                sp.wait_ge((row_act, row_dve)[n % 2], n // 2 + 1)
                sp.dma_start(out[0, (n % 2) * P:(n % 2 + 1) * P, (n // 2) * BANK:(n // 2 + 1) * BANK],
                             orow[:, n % 2, (n // 2) * BANK:(n // 2 + 1) * BANK]).then_inc(result_out, 16)
            sp.wait_ge(x_spilled, 16)
            sp.wait_ge(result_out, 8 * 16)

        @block.gpsimd
        def _(pool):
            pool.memset(vrow[:, :, :], 0.0).then_inc(vec_clear, 1)
            pool.memset(c4[:, :, :].bitcast(F32), 0.0).then_inc(c4_clear, 1)
            pool.dma_start(basics[:, :, :], A["k_basics"].rearrange("p (a n) -> p a n", a=4)).then_inc(const_in, 16)
            pool.wait_ge(vec_clear, 1)
            for name, (t, first, n) in VROWS.items():
                if name.startswith("shift"):
                    c0, width = {"shift_rkv": (0, P), "shift_gd": (GD0, P), "shift_wd": (WD0, LORA),
                                 "shift_ad": (WD0 + LORA, LORA)}[name]
                    src = A["rw_shift"][:, c0:c0 + n // 3 * width]
                    for tap in range(3):
                        pool.dma_start(vrow[first + tap * (n // 3):first + (tap + 1) * (n // 3), t, 0:width],
                                       src[tap].rearrange("(n c) -> n c", c=width)).then_inc(vec_in, 16)
                    continue
                src = A[name]
                names = " ".join("abcd"[:len(src.shape)])
                flat = src.rearrange(f"{names} -> ({names})") if len(src.shape) > 1 else src
                pool.dma_start(vrow[first:first + n, t, :], flat.rearrange("(n c) -> n c", c=P)).then_inc(vec_in, 16)

            pool.wait_ge(split_free, REST_DONE)
            pool.dma_start(kfour[:, :, :], A["k_fourier"].rearrange("p (a n) -> p a n", a=5)).then_inc(four_in, 16)
            pool.wait_ge(mix_done, 1)
            pool.dma_start(kscan[:, :], A["k_scan"]).then_inc(kscan_in, 16)

            def load_lora(b):
                for n, name in enumerate(("dec_up", "iclr_up")):
                    pool.dma_start(decw[0:LORA, 2 * n:2 * n + 2, :], A[name][:, :, ds(b, P)].rearrange("d p n -> p d n"))\
                        .then_inc(decw_in, 16)

            load_lora(0)
            for bd in [bdV[:, :, :]] + [x[d][:, :, 0:P] for d in range(2) for x in (bdA, bdB, bdK)]:
                pool.memset(bd, 0.0).then_inc(bd_clear, 1)

            def mask_levels(b):
                for q in range(2):
                    for l in range(LEVELS):
                        for d in range(2):
                            dst = (ULa, MT)[l % 2][d]
                            if l == 0:
                                scan_act[d].wait(pool, (q, "U"), b)
                            else:
                                scan_pe[d].wait(pool, (q, ("MV", "L0", "Y1", "Y2", "Y3")[l - 1]), b)
                                if l == 2:
                                    scan_dve[d].wait(pool, (q, "T0"), b)
                            scan_pool[d].done(pool.tensor_tensor(dst[:, :, :], U[d][:, :, :], over_chunks(level[d][l]), ALU.mult),
                                              (q, f"m{l}"))

            pool.wait_ge(kscan_in, 16)
            with pool.Fori(0, RB - 1) as b:
                mask_levels(b)
                scan_pe[1].wait(pool, (1, "zz"), b)
                load_lora(b * P + P)
            mask_levels(RB - 1)

            scan_dve[0].wait(pool, (1, "y"), RB - 1)
            scan_dve[1].wait(pool, (1, "y"), RB - 1)
            pool.dma_start(gup[:, :, :], A["g_up"].rearrange("(k p) n -> p k n", p=P)).then_inc(gup_in, 16)
            pool.wait_ge(ylo, 4)
            pool.wait_ge(x_spilled, 16)
            pool.dma_start(xT[:, :, :], xres.rearrange("p (k t) -> p k t", k=KB)).then_inc(x_back, 16)

            pool.wait_ge(x_done, 2)
            for n, name in enumerate(("gate_a_w_2", "gate_x_w_2")):
                pool.dma_start(gw[:, n, :, :], A[name].rearrange("n c d -> c n d")).then_inc(gw_in, 16)
            pool.wait_ge(split_free, IN2_DONE)
            pool.dma_start(kret[:, :], A["k_ret"]).then_inc(kret_in, 16)
            pool.wait_ge(lru_u, RB)
            pool.wait_ge(lru_i, 2 * RB)
            pool.tensor_tensor(lb[:, :, :], lb[:, :, :], lu[:, :, :], ALU.mult).then_inc(lru_iu, 1)
            def head(h, first=False):
                if not first:
                    retp.wait(pool, "vt", h - 1)
                retg.done(pool.tensor_copy(rv[:, :], p2[:, ds(h + RV, 1), :]), "v")
                if not first:
                    retd.wait(pool, "qr", h - 1)
                retg.done(pool.tensor_tensor(rqc[:, :, :], qk_of(h), both(rcos), ALU.mult), "qc")

            pool.wait_ge(kret_in, 16)
            pool.wait_ge(bank_free, IN2_OUT)
            head(0, True)
            with pool.Fori(0, RET_HEADS - 1) as i:
                head(i + 1)
        VEC_DMAS = sum(3 if n.startswith("shift") else 1 for n in VROWS)

        @block.scalar
        def _(act):
            chain = Chain(act, a_chain)

            def split(ph, i, j):
                if isinstance(i, int) and ph.chunk(i, j) >= TOTAL:
                    return
                s = ph.slot(j)
                act.wait_ge(raw_in[s], (ph.rounds(i, j) + 1) * 16)
                act.wait_ge(split_free, ph.chunk(i, j) + 1)
                act.activation(hi[:, s, :, :], raw[:, s, :, :], ACT.Copy).then_inc(hi_ready, 1)

            def gemm(ph, evacuate):
                def trip(i):
                    for p in range(ph.pairs):
                        for j in range(p * ph.per_pair + 2, (p + 1) * ph.per_pair + 2):
                            split(ph, i, j)
                        evacuate(i, p)
                loop(act, ph, trip)

            def lows(ph, i, p, wait=True):
                if wait:
                    act.wait_ge(split_free, ph.last_chunk(i, p) + (1 + SPLIT_CREDIT))
                b, t = ph.bank(p), (ph.p0 + p) % 2
                act.activation(tmp[:, t, :, :], ps[:, b:b + 2, T:2 * T], ACT.Copy).then_inc(tmp_ready, 1)

            def sqrt_of_variance(n, width):
                act.wait_ge(var_ready, n + 1)
                act.activation(nt[:, 1, 0:width], nt[:, 0, 0:width], ACT.Sqrt).then_inc(sqrt_ready, 1)

            def squares(n):
                act.wait_ge(x_done, n)
                for k in range(KB):
                    if n * KB + k >= 2:
                        act.wait_ge(sq_used, n * KB + k - 1)
                    act.activation(sq[:, k % 2, 0:T], xT[:, k, :], ACT.Square).then_inc(sq_ready, 1)

            def normed_hi(n, dest, shift):
                with act.Fori(0, KB // 2) as i:
                    for e in range(2):
                        act.wait_ge(nt_ready, i * 2 + (n * KB + e + 1))
                        if shift is None:
                            ins = act.activation(dest(i * 2 + e), nt[:, e, 0:T], ACT.Copy)
                        else:
                            ins = act.activation(dest(i * 2 + e), nt[:, e, 0:T], ACT.Identity, bias=shift(i * 2 + e))
                        ins.then_inc(nhi_ready, 1)

            act.wait_ge(vec_turned, 1)
            act.activation(vec[:, :, :], ps[:, 0, :].rearrange("p (a n) -> p a n", a=4), ACT.Copy).then_inc(vec_ready, 1)
            act.wait_ge(vec_ready, 1)
            act.activation(csil[:, 0, :], vcol("c", 0, KB), ACT.Silu).then_inc(csil_ready, 1)
            act.activation(csil[:, 1, :], vcol("c_ctx", 0, KB), ACT.Silu).then_inc(csil_ready, 1)
            act.wait_ge(csil_ready, 2)
            act.wait_ge(c4_clear, 1)
            for q in range(2):
                act.activation(c4[:, :, 2 * q:2 * q + 1], csil[:, q, :], ACT.Copy).then_inc(chi_ready, 1)
            for k in range(KB):
                act.wait_ge(turned, k + 1)
                act.activation(ctxT[:, k, :], ps[:, 1 + k % 4, 0:T], ACT.Copy).then_inc(ctx_out, 1)
                if k >= 2:
                    act.wait_ge(sq_used, k - 1)
                act.activation(sq[:, k % 2, :], ps[:, 1 + k % 4, :], ACT.Square).then_inc(sq_ready, 1)
            sqrt_of_variance(0, 2 * T)
            for j in range(2):
                split(PH["mod"], 0, j)
            gemm(PH["mod"], lambda i, p: None)
            act.wait_ge(gain_ready, 3)
            normed_hi(0, lambda k: mov1[:, k, 0, 0, :], lambda k: mod[:, 0, 1, ds(k, 1)])
            normed_hi(1, lambda k: mov1[:, k, 0, 1, :], lambda k: mod[:, 0, 0, ds(k, 1)])

            def shift_both(i, p):
                ph = PH["in_kv"]
                act.wait_ge(split_free, ph.last_chunk(i, p) + (1 + SPLIT_CREDIT))
                for blk in range(2):
                    n = i * 4 + (2 * p + blk)
                    act.activation(kv[:, ds(n, 1), :, :], ps[:, ph.bank(p) + blk, :], ACT.Copy,
                                   scale=vcol("shift_rkv", n + (3 * RB + RB))).then_inc(shift_ready, 1)

            def shift_lora(i, p):
                ph = PH["in_lora"]
                act.wait_ge(split_free, ph.last_chunk(i, p) + (1 + SPLIT_CREDIT))
                if p == 0:
                    for blk, name in enumerate(("shift_wd", "shift_ad")):
                        act.activation(wdad[0:LORA, blk, :, :], ps[0:LORA, blk, :], ACT.Copy,
                                       scale=vcol(name, 1, rows=LORA)).then_inc(shift_ready, 1)
                    return
                lows(ph, i, p, wait=False)
                for blk in range(2):
                    act.wait_ge(bank_free, ph.pair(i, p) + (1 + BANK_CREDIT))
                    act.activation(gd[:, blk, :], px[:, blk, :], ACT.Copy, scale=vcol("shift_gd", 2 + blk)).then_inc(shift_ready, 1)

            def shift_r(i, p):
                lows(PH["in_r"], i, p)
                for blk in range(2):
                    n = i * 4 + (2 * p + blk)
                    act.wait_ge(bank_free, PH["in_r"].pair(i, p) + (1 + BANK_CREDIT))
                    act.activation(r[:, ds(n, 1), :], px[:, blk, :], ACT.Copy,
                                   scale=vcol("shift_rkv", n + 3 * RB)).then_inc(shift_ready, 1)

            gemm(PH["in_kv"], shift_both)
            gemm(PH["in_lora"], shift_lora)
            gemm(PH["in_r"], shift_r)
            gemm(PH["in_rest"], lambda i, p: lows(PH["in_rest"], i, p))
            act.activation(wdad[0:LORA, 0, :, :], wdad[0:LORA, 0, :, :], ACT.Tanh).then_inc(wd_ready, 1)
            act.wait_ge(conv_mid, 1)
            for blk in range(4):
                act.activation(ymix[:, RB + blk, :], proj[:, blk, :], ACT.Copy, scale=vcol("conv_w", 4 + blk)).then_inc(conv_mid, 1)
            for n in range(4):
                act.wait_ge(uf_turned, n + 1)
                act.activation(uf[:, n // 2, 2 * (n % 2):2 * (n % 2) + 2, :, :], ps[:, 4 + n, :], ACT.Copy).then_inc(uf_ready, 1)

            def scan_block(b):
                for q in range(2):
                    for d in range(2):
                        done, pe, dve = scan_act[d].done, scan_pe[d], scan_dve[d]
                        if q == 0 and d == 0:
                            for n, name in enumerate(("dec_w0", "iclr_a0")):
                                done(act.activation(bcol[:, 2 * n:2 * n + 2], vcol(name, 0, 2 * RB).rearrange("p (d n) -> p d n", d=2)[:, :, ds(b, 1)],
                                                    ACT.Copy), (q, f"bc{n}"))
                            dve.wait(act, (0, "kq"), b)
                            done(act.activation(kn[:, :], kq[:, :], ACT.Square), (q, "ksq"))
                            dve.wait(act, (0, "kv"), b)
                            done(act.activation(kk[:, :], kn[:, :], ACT.Sqrt), (q, "ksqrt"))
                            dve.wait(act, (0, "kk"), b)
                        if d == 0:
                            for h in range(2):
                                hs = slice(h * HEAD, (h + 1) * HEAD)
                                done(act.activation(bdV[hs, :, hs], kv[hs, ds(b + RB, 1), q, :], ACT.Copy), (q, f"bv{h}"))
                        pe.wait(act, (q, "zz"), b)
                        if q == 0 and d == 0:
                            scan_act[0].wait(act, (q, "bc1"), b)
                        done(act.activation(lw[d][:, :], ps[:, 4 * d + 3, 0:T], ACT.Sigmoid, bias=bcol[:, d:d + 1]), (q, "sg"))
                        done(act.activation(av[d][:, :], ps[:, 4 * d + 3, T:2 * T], ACT.Sigmoid, bias=bcol[:, 2 + d:3 + d]), (q, "sa"))
                    for d in range(2):
                        done, dve = scan_act[d].done, scan_dve[d]
                        dve.wait(act, (q, "Lx"), b)
                        done(act.activation(ex[d][:, :], ex[d][:, :], ACT.Exp), (q, "eex"))
                        done(act.activation(en[d][:, :], L[d][:, :], ACT.Exp, scale=-1.0), (q, "en"))
                        last = C - 1 if d == 0 else 0
                        done(act.activation(pc[d][:, :], chunks_of(L[d][:, :])[:, :, last], ACT.Exp), (q, "pc"))
                        if q:
                            scan_act[d].wait(act, (q, "pc"), b)
                            done(act.activation(L[d][:, :], L[d][:, :], ACT.Exp), (q, "ep"))
                    for d in range(2):
                        scan_pe[d].wait(act, (q, "G1"), b)
                        if q:
                            scan_dve[d].wait(act, (q, "Q"), b)
                        scan_act[d].done(act.activation(in_pairs(U[d][:, :, :]), two_banks(4 * d, P + C * q, 0, P), ACT.Copy), (q, "U"))
                    for name, src, bank, dst in (("oA", "tA", 0, lambda d: tokR[d][:, :, 0, :]), ("oB", "tB", 1, lambda d: tokBQ[d][:, :, 0:P]),
                                                 ("oK", "tK", 2, lambda d: tokK[d][:, :, :]), ("oV", "tV", 3, lambda d: tokV[:, :, :]),
                                                 ("oMV", "MV", 0, lambda d: tokR[d][:, :, 1, :])):
                        for d in range(2 if name != "oV" else 1):
                            scan_pe[d].wait(act, (q, src), b)
                            scan_act[d].done(act.activation(dst(d), ps[:, 4 * d + bank, :], ACT.Copy), (q, name))
                    for l in range(1, LEVELS):
                        for d in range(2):
                            scan_pe[d].wait(act, (q, f"Y{l}"), b)
                            scan_act[d].done(act.activation(XY[d][:, :, 1, :], ps[:, 4 * d + (2 if l % 2 else 1), :], ACT.Copy), (q, f"Yb{l}"))
                    for d in range(2):
                        scan_pe[d].wait(act, (q, "Z"), b)
                        scan_act[d].done(act.activation(XY[d][:, :, :, :].rearrange("p (a b) z n -> p a (b z n)", a=2), ps[:, 4 * d + 2:4 * d + 4, :],
                                                        ACT.Copy, scale=-1.0), (q, "Z"))

            act.wait_ge(bd_clear, 7)
            with act.Fori(0, RB) as b:
                scan_block(b)
            act.activation(gd[:, :, :], gd[:, :, :], ACT.Sigmoid).then_inc(gd_ready, 1)
            for n in range(RB // 2):
                act.wait_ge(gate_mm, n + 1)
                act.activation(gate[:, 2 * n:2 * n + 2, :], ps[:, n % 4, :], ACT.Copy).then_inc(gate_out, 1)
            with act.Fori(0, RB // 2) as i:
                gnd.wait(act, "c", i)
                gna.done(act.activation(ysq[:, :], yc[:, :], ACT.Square), "sq")
                gnd.wait(act, "v", i)
                gna.done(act.activation(yn[:, :], yv[:, :], ACT.Sqrt), "sqrt")
                gnd.wait(act, "yn", i)
                for blk in range(2):
                    n = i * 2 + blk
                    gna.done(act.activation(yn[:, blk * T:(blk + 1) * T], yn[:, blk * T:(blk + 1) * T], ACT.Identity,
                                            scale=vcol("ln_w", n), bias=vcol("ln_b", n)), f"w{blk}")
            for n in range(4):
                act.wait_ge(ymix_done, 1)
                act.activation(mov[:, 4 * n:4 * n + 4, 0, :], ymix[:, 4 * n:4 * n + 4, :], ACT.Copy).then_inc(yhi, 1)
            def gated(e, ph):
                def evacuate(i, p):
                    lows(ph, i, p)
                    if p == 0:
                        act.wait_ge(bank_free, ph.pair(i, p) + (1 + BANK_CREDIT))
                        act.activation(sbuf[:, :, :], gbuf[:, :, :], ACT.Silu).then_inc(ffn_s, 1)
                    else:
                        act.wait_ge(ffn_h, i + (e * PH["ffn"].trips + 1))
                        act.activation(hid[:, ds(i * 2, 2), 0, :], ubuf[:, :, :], ACT.Copy).then_inc(ffn_hi, 1)
                return evacuate

            def norm_and_ffn(e, stat, norm, shift, suffix):
                squares(stat)
                sqrt_of_variance(stat, T)
                normed_hi(norm, lambda k: mov[:, ds(k, 1), 0, :], shift)
                gemm(PH["ffn" + suffix], gated(e, PH["ffn" + suffix]))
                gemm(PH["down" + suffix], lambda i, p: lows(PH["down" + suffix], i, p))

            gemm(PH["out"], lambda i, p: lows(PH["out"], i, p))
            norm_and_ffn(0, 1, 2, lambda k: mod[:, 3, 0, ds(k, 1)], "")
            for stat in (2, 3):
                squares(stat)
                sqrt_of_variance(stat, T)
            normed_hi(3, lambda k: mov[:, ds(k, 1), 0, :], None)
            gemm(PH["in_2"], lambda i, p: lows(PH["in_2"], i, p))
            lam = vcol("lru_lambda_2", 0, RB)
            act.activation(lcol[:, 1, :], lam, ACT.Abs).then_inc(lam_exp, 1)
            act.wait_ge(lam_exp, 1)
            act.activation(lcol[:, 2, :], lcol[:, 1, :], ACT.Exp, scale=-1.0).then_inc(lam_exp, 1)
            act.wait_ge(bank_free, IN2_OUT)
            for n in range(RB):
                act.activation(lu[:, n, :], p2[:, LX + n, :], ACT.Identity, scale=vcol("conv_w_2", 3 * RB + n), bias=vcol("conv_b_2", n))\
                   .then_inc(lru_mid, 1)
            for n in range(RB):
                act.wait_ge(lru_gates, n // 2 + 1)
                half = slice((n % 2) * T, (n % 2 + 1) * T)
                act.activation(la[:, n, :], ps[:, n // 2, half], ACT.Sigmoid, bias=vcol("gate_a_b_2", n)).then_inc(lru_i, 1)
                act.activation(lb[:, n, :], ps[:, 4 + n // 2, half], ACT.Sigmoid, bias=vcol("gate_x_b_2", n)).then_inc(lru_i, 1)
            act.wait_ge(lam_ready, 1)
            act.wait_ge(lru_i, 2 * RB)
            for n in range(RB):
                act.activation(la[:, n, :], la[:, n, :], ACT.Tanh, scale=lcol[:, 1, n:n + 1]).then_inc(lru_t, 1)
            act.wait_ge(lru_t, RB)
            act.wait_ge(lru_u, RB)
            act.activation(p2[:, LX:LX + RB, :], la[:, :, :], ACT.Sqrt, scale=-4.0).then_inc(lru_sq, 1)
            act.activation(p2[:, LG:LG + RB, :], p2[:, LG:LG + RB, :], ACT.Gelu_apprx_tanh).then_inc(lru_gelu, 1)
            act.activation(p2[:, RG:RG + RB, :], p2[:, RG:RG + RB, :], ACT.Silu).then_inc(ret_silu, 1)
            def head(h, first=False):
                retp.wait(act, "vt", h)
                if not first:
                    retp.wait(act, "o", h - 1)
                reta.done(act.activation(rvt[:, :, :], ps[:, 1, 0:T], ACT.Copy), "vt")
                retp.wait(act, "o", h)
                reta.done(act.activation(ro[:, ds(h, 1), :], ps[:, 3, 0:T], ACT.Copy), "o")

            head(0, True)
            with act.Fori(0, RET_HEADS - 1) as i:
                head(i + 1)
            with act.Fori(0, RET_HEADS // 2) as i:
                rnd.wait(act, "c", i)
                rna.done(act.activation(osq[:, :], oc[:, :], ACT.Square), "sq")
                rnd.wait(act, "v", i)
                rna.done(act.activation(on[:, :], ov[:, :], ACT.Sqrt), "sqrt")
            act.wait_ge(y2_done, 1)
            for n in range(4):
                act.activation(mov[:, 4 * n:4 * n + 4, 0, :], p2[:, 4 * n:4 * n + 4, :], ACT.Copy).then_inc(y2_hi, 1)
            gemm(PH["out_2"], lambda i, p: lows(PH["out_2"], i, p))
            norm_and_ffn(1, 4, 4, None, "_2")
            squares(5)
            sqrt_of_variance(5, T)
            for n in range(0, 8, 2):
                act.wait_ge(row_turned, n + 1)
                act.activation(orow[:, n % 2, (n // 2) * BANK:(n // 2 + 1) * BANK], ps[:, n, :], ACT.Copy).then_inc(row_act, 1)

        @block.vector
        def _(dve):
            chain = Chain(dve, v_chain)
            dve.sem_inc(lo_ready, RING)
            dve.sem_inc(bank_free, BANK_CREDIT)

            def split(ph, i, j):
                if isinstance(i, int) and ph.chunk(i, j) >= TOTAL:
                    return
                s = ph.slot(j)
                dve.wait_ge(hi_ready, ph.chunk(i, j) + 1)
                dve.tensor_tensor(lo[:, s, :, :], raw[:, s, :, :], hi[:, s, :, :].bitcast(F32), ALU.subtract)\
                   .then_inc(lo_ready, 1)

            def gemm(ph, evacuate, per_trip=0):
                def trip(i):
                    if per_trip:
                        chain.loop(i if ph.trips > 1 else None, per_trip)
                    for p in range(ph.pairs):
                        for j in range(p * ph.per_pair + 2, (p + 1) * ph.per_pair + 2):
                            split(ph, i, j)
                        evacuate(i, p)
                assert not (per_trip and ph is order[-1])
                loop(dve, ph, trip)
                if per_trip:
                    chain.end(ph.trips)

            def summed(ph, i, p, dest):
                b, t = ph.bank(p), (ph.p0 + p) % 2
                dve.wait_ge(tmp_ready, ph.pair(i, p) + (1 - LOWS0))
                return dve.tensor_tensor(dest, ps[:, b:b + 2, 0:T], tmp[:, t, :, :], ALU.add)

            def variance(n, width):
                v, s, y = nt[:, 0, 0:width], nt[:, 1, 0:width], rstd[:, :, :].rearrange("p a t -> p (a t)")[:, 0:width]
                dve.wait_ge(sq_used, (n + 1) * KB)
                dve.tensor_scalar(v, ps[:, 7, 0:width], 1.0 / D, RMS_EPS, ALU.mult, ALU.add).then_inc(var_ready, 1)
                dve.wait_ge(sqrt_ready, n + 1)
                chain(dve.reciprocal(y, s))
                chain(dve.tensor_tensor(s, y, y, ALU.mult))
                chain(dve.tensor_tensor(s, s, v, ALU.mult))
                chain(dve.tensor_scalar(s, s, -0.5, 1.5, ALU.mult, ALU.add))
                chain(dve.tensor_tensor(y, y, s, ALU.mult))

            def normed(n, src, g, rs, shift, hi_of, lo_of):
                with dve.Fori(0, KB // 2) as i:
                    for e in range(2):
                        dve.scalar_tensor_tensor(out=nt[:, e, 0:T], in0=src(i * 2 + e), scalar=g(i * 2 + e), in1=rs,
                                                 op0=ALU.mult, op1=ALU.mult).then_inc(nt_ready, 1)
                    for e in range(2):
                        k = i * 2 + e
                        dve.wait_ge(nhi_ready, i * 2 + (n * KB + e + 1))
                        if shift is None:
                            ins = dve.tensor_tensor(lo_of(k), nt[:, e, 0:T], hi_of(k).bitcast(F32), ALU.subtract)
                        else:
                            ins = dve.scalar_tensor_tensor(out=lo_of(k), in0=nt[:, e, 0:T], scalar=shift(k),
                                                           in1=hi_of(k).bitcast(F32), op0=ALU.add, op1=ALU.subtract)
                        ins.then_inc(mov_ready, 1)
                    dve.wait_ge(mov_ready, i * 2 + (n * KB + 2))

            dve.wait_ge(vec_ready, 1)
            for q in range(2):
                dve.wait_ge(chi_ready, q + 1)
                dve.tensor_tensor(c4[:, :, 2 * q + 1:2 * q + 2], csil[:, q, :],
                                  c4[:, :, 2 * q:2 * q + 1].bitcast(F32), ALU.subtract).then_inc(c4_ready, 1)
            for k in range(KB):
                dve.wait_ge(sq_ready, k + 1)
                dve.tensor_copy(xT[:, k, :], ps[:, 1 + k % 4, T:2 * T]).then_inc(x_out, 1)
            variance(0, 2 * T)
            for j in range(2):
                split(PH["mod"], 0, j)

            def mod_row(i, p):
                ph = PH["mod"]
                dve.wait_ge(split_free, ph.last_chunk(i, p) + (1 + SPLIT_CREDIT))
                dve.tensor_copy(mrow[:, p * CN:(p + 1) * CN], ps[0:4, ph.bank(p), 0:CN]).then_inc(bank_free, 1)
                if p == ph.pairs - 1:
                    dve.wait_ge(mcol_ready, i + 1)
                    for q in range(2):
                        dve.tensor_tensor(mod[:, ds(i, 1), q, :],
                                          ps[:, 5, 0:2 * KB].rearrange("p (k q) -> p q k", q=2)[:, q, :],
                                          vcol("b_mod", i * KB, KB), ALU.add).then_inc(mod_ready, 1)
            gemm(PH["mod"], mod_row)
            dve.wait_ge(mod_ready, 12)
            for n, (part, q, norm) in enumerate([(1, 0, "norm_mix"), (1, 1, "norm_mix"), (4, 0, "norm_ffn")]):
                dve.scalar_tensor_tensor(out=gain[:, n, :], in0=mod[:, part, q, :], scalar=1.0, in1=vcol(norm, 0, KB),
                                         op0=ALU.add, op1=ALU.mult).then_inc(gain_ready, 1)
            dve.wait_ge(gain_ready, 3)
            for n, (src, q) in enumerate([(ctxT, 1), (xT, 0)]):
                normed(n, lambda k: src[:, ds(k, 1), :], lambda k: gain[:, q, ds(k, 1)], rstd[:, 1 - q, :],
                       lambda k: mod[:, 0, q, ds(k, 1)], lambda k: mov1[:, ds(k, 1), 0, 1 - q, :], lambda k: mov1[:, ds(k, 1), 1, 1 - q, :])

            def outer_taps(dest, src, before, after):
                n = dest.shape[-1]
                chain(dve.scalar_tensor_tensor(out=dest[:, :, 1:n], in0=src[:, :, 0:n - 1], scalar=before,
                                               in1=dest[:, :, 1:n], op0=ALU.mult, op1=ALU.add))
                return dve.scalar_tensor_tensor(out=dest[:, :, 0:n - 1], in0=src[:, :, 1:n], scalar=after,
                                                in1=dest[:, :, 0:n - 1], op0=ALU.mult, op1=ALU.add)

            def shift_both(i, p):
                ph = PH["in_kv"]
                for blk in range(2):
                    n = i * 4 + (2 * p + blk)
                    dve.wait_ge(shift_ready, n + 1)
                    ins = outer_taps(kv[:, ds(n, 1), :, :].rearrange("p n q t -> p (n q) t"),
                                     ps[:, ph.bank(p) + blk, :].rearrange("p (q t) -> p q t", q=2),
                                     vcol("shift_rkv", n + RB), vcol("shift_rkv", n + (6 * RB + RB)))
                    if blk == 0:
                        chain(ins)
                ins.then_inc(bank_free, 1)

            def shift_lora(i, p):
                ph = PH["in_lora"]
                if p == 0:
                    for blk, name in enumerate(("shift_wd", "shift_ad")):
                        dve.wait_ge(shift_ready, 2 * RB + blk + 1)
                        ins = outer_taps(wdad[0:LORA, blk, :, :], ps[0:LORA, blk, :].rearrange("p (q t) -> p q t", q=2),
                                         vcol(name, 0, rows=LORA), vcol(name, 2, rows=LORA))
                        if blk == 0:
                            chain(ins)
                    ins.then_inc(bank_free, 1)
                    return
                summed(ph, i, p, px[:, :, :]).then_inc(bank_free, 1)
                dve.wait_ge(bank_free, ph.pair(i, p) + (1 + BANK_CREDIT))
                for blk in range(2):
                    dve.wait_ge(shift_ready, 2 * RB + 2 + blk + 1)
                    chain(outer_taps(gd[:, blk:blk + 1, :], px[:, blk:blk + 1, :], vcol("shift_gd", blk), vcol("shift_gd", 4 + blk)))

            def shift_r(i, p):
                ph = PH["in_r"]
                summed(ph, i, p, px[:, :, :]).then_inc(bank_free, 1)
                dve.wait_ge(bank_free, ph.pair(i, p) + (1 + BANK_CREDIT))
                for blk in range(2):
                    n = i * 4 + (2 * p + blk)
                    dve.wait_ge(shift_ready, n + (2 * RB + 4 + 1))
                    chain(outer_taps(r[:, ds(n, 1), :], px[:, blk:blk + 1, :], vcol("shift_rkv", n), vcol("shift_rkv", n + 6 * RB)))

            gemm(PH["in_kv"], shift_both, per_trip=6)
            gemm(PH["in_lora"], shift_lora, per_trip=7)
            gemm(PH["in_r"], shift_r, per_trip=8)
            gemm(PH["in_rest"], lambda i, p: summed(PH["in_rest"], i, p, proj[:, ds(i * 4 + 2 * p, 2), :]).then_inc(bank_free, 1))
            chain(dve.tensor_tensor(proj[:, 0:4, :], proj[:, 0:4, :], proj[:, 4:8, :], ALU.mult))
            dve.wait_ge(x_spilled, 16)
            dve.sem_inc(conv_mid, 1)
            for blk in range(4):
                dve.wait_ge(conv_mid, blk + 2)
                dest, src = (x.rearrange("p (n t) -> p n t", t=GRID_W) for x in (ymix[:, RB + blk, :], proj[:, blk, :]))
                chain(outer_taps(dest, src, vcol("conv_w", blk), vcol("conv_w", 8 + blk)))
                chain(dve.tensor_tensor(ymix[:, RB + blk, :], ymix[:, RB + blk, :], proj[:, 8 + blk, :], ALU.mult))
            for n in range(2):
                dve.wait_ge(four_done, n + 1)
                chain(dve.tensor_copy(ymix[:, RB + 4 + 2 * n:RB + 6 + 2 * n, :], ps[:, n, :].rearrange("p (a t) -> p a t", a=2)))
            dve.sem_inc(mix_done, 1)

            def scan_block(b):
                def own(d, name, q):
                    scan_dve[d].wait(dve, (q, name), b)

                for q in range(2):
                    kq_, kkq = (x[:, q * T:(q + 1) * T] for x in (kq, kk))
                    for d in range(2):
                        done, act, pe = scan_dve[d].done, scan_act[d], scan_pe[d]
                        step = lambda ins, name: (done(ins, (q, name)), own(d, name, q))
                        if q == 0 and d == 0:
                            done(dve.tensor_scalar(kq[:, :], kv[:, ds(b, 1), :, :].rearrange("p a q t -> p (a q t)"), vcol("k_k", b), None, ALU.mult), (q, "kq"))
                            pe.wait(dve, (q, "kk"), b)
                            done(dve.tensor_scalar(kn[:, :], ps[:, 2, :], KK_EPS * KK_EPS, None, ALU.max), (q, "kv"))
                            act.wait(dve, (q, "ksqrt"), b)
                            step(dve.reciprocal(kk[:, :], kk[:, :]), "n0")
                            step(dve.tensor_tensor(knt[:, :], kk[:, :], kk[:, :], ALU.mult), "n1")
                            step(dve.tensor_tensor(knt[:, :], knt[:, :], kn[:, :], ALU.mult), "n2")
                            step(dve.tensor_scalar(knt[:, :], knt[:, :], -0.5, 1.5, ALU.mult, ALU.add), "n3")
                            step(dve.tensor_tensor(kk[:, :], kk[:, :], knt[:, :], ALU.mult), "n4")
                            step(dve.tensor_tensor(kk[:, :], kk[:, :], kq[:, :], ALU.mult), "kk")
                        if q == 0:
                            step(dve.memset(S[d][:, :], 0.0), "S")
                        act.wait(dve, (q, "sg"), b)
                        step(dve.tensor_scalar(lw[d][:, :], lw[d][:, :], DECAY_SCALE, None, ALU.mult), "lw")
                        way = slice(None, None, 1 if d == 0 else -1)
                        step(dve.tensor_tensor_scan(L[d][:, way], inside, lw[d][:, way], 0.0, ALU.mult, ALU.add), "L")
                        done(dve.tensor_tensor(ex[d][:, :], L[d][:, :], lw[d][:, :], ALU.subtract), (q, "Lx"))
                        act.wait(dve, (q, "sa"), b)
                        step(dve.tensor_scalar(kd[d][:, :], av[d][:, :], vcol("k_a", b), oka[:, ds(b, 1)], ALU.mult, ALU.add), "kf")
                        step(dve.tensor_tensor(kd[d][:, :], kd[d][:, :], kv[:, ds(b, 1), q, :].rearrange("p a t -> p (a t)"), ALU.mult), "kd")
                        step(dve.tensor_tensor(av[d][:, :], av[d][:, :], kkq, ALU.mult), "ba")
                        if q and d:
                            step(dve.tensor_tensor(kn[:, 0:T], kd[0][:, :], kd[1][:, :], ALU.add), "rk0")
                            done(dve.scalar_tensor_tensor(out=kn[:, 0:T], in0=kn[:, 0:T], scalar=vcol("r_k", b),
                                                          in1=r[:, ds(b, 1), :].rearrange("p a t -> p (a t)"), op0=ALU.mult, op1=ALU.mult), (q, "rk1"))
                            pe.wait(dve, (q, "rk"), b)
                            done(dve.tensor_tensor(kn[:, T:2 * T], ps[:, 6, 0:T], kv[:, ds(b + RB, 1), q, :].rearrange("p a t -> p (a t)"), ALU.mult), (q, "bonus"))
                    for d in range(2):
                        done, act = scan_dve[d].done, scan_act[d]
                        for name, x, e, dst in (("a", kkq, ex[d], bdA[d]), ("b", av[d], en[d], bdB[d]), ("k", kd[d], en[d], bdK[d])):
                            act.wait(dve, (q, "en" if name != "a" else "eex"), b)
                            for h in range(2):
                                hs = slice(h * HEAD, (h + 1) * HEAD)
                                done(dve.tensor_tensor(dst[hs, :, hs], chunks_of(x[hs, :]), chunks_of(e[hs, :]), ALU.mult), (q, f"{name}{h}"))
                        if q:
                            act.wait(dve, (q, "ep"), b)
                            done(dve.tensor_tensor(bdA[d][:, :, P:P + C], chunks_of(r[:, ds(b, 1), :].rearrange("p a t -> p (a t)")),
                                                   chunks_of(L[d][:, :]), ALU.mult), (q, "rho"))
                    for d in range(2):
                        done, pe = scan_dve[d].done, scan_pe[d]
                        w = P + C * q
                        if q:
                            pe.wait(dve, (q, "G1"), b)
                            done(dve.tensor_tensor(in_pairs(tokBQ[d][:, :, P:P + C]), two_banks(4 * d, w, P, C), over_banks(upto[d]), ALU.mult), (q, "Q"))
                        pe.wait(dve, (q, "G2"), b)
                        if q:
                            done(dve.tensor_tensor(in_pairs(RT[d][:, :, :]), two_banks(4 * d + 2, w, P, C), over_banks(upto[d]), ALU.mult), (q, "R"))
                        done(dve.tensor_tensor(in_pairs(MT[d][:, :, :]), two_banks(4 * d + 2, w, 0, P), over_banks(strict[d]), ALU.mult), (q, "M"))
                    for d in range(2):
                        done, pe = scan_dve[d].done, scan_pe[d]
                        scan_pool[d].wait(dve, (q, "m0"), b)
                        pe.wait(dve, (q, "L0"), b)
                        done(dve.tensor_tensor(XT[d][:, :, :], over_chunks(ident), ULa[d][:, :, :], ALU.subtract), (q, "T0"))
                        done(dve.tensor_tensor(XY[d][:, :, 0, :], over_chunks(ident), ps[:, 4 * d + 1, :].rearrange("p (c n) -> p c n", c=NC), ALU.subtract), (q, "X0"))
                    for l in range(1, LEVELS):
                        for d in range(2):
                            done, pe = scan_dve[d].done, scan_pe[d]
                            pe.wait(dve, (q, f"X{l}"), b)
                            bank = lambda n: ps[:, 4 * d + n, :].rearrange("p (c n) -> p c n", c=NC)
                            if l < LEVELS - 1:
                                done(dve.tensor_tensor(XY[d][:, :, 0, :], XY[d][:, :, 0, :], bank(3), ALU.subtract), (q, f"X{l}"))
                            done(dve.tensor_tensor(XT[d][:, :, :], XT[d][:, :, :], bank(0), ALU.subtract), (q, f"T{l}"))
                    for d in range(2):
                        done, pe = scan_dve[d].done, scan_pe[d]
                        w = P + C * q
                        pe.wait(dve, (q, "A"), b)
                        done(dve.tensor_tensor(in_pairs(AT[d][:, :, :]), two_banks(4 * d, w, 0, P), over_banks(ident), ALU.add), (q, "AT"))
                        if q:
                            done(dve.tensor_tensor(in_pairs(bdA[d][:, :, P:P + C]), two_banks(4 * d, w, P, C), in_pairs(bdA[d][:, :, P:P + C]), ALU.add), (q, "rho2"))
                        pe.wait(dve, (q, "B"), b)
                        done(dve.tensor_tensor(BM[d][:, :, :], ps[:, 4 * d + 2, :].rearrange("p (c n) -> p c n", c=NC),
                                               pc[d][:, :].rearrange("p (c n) -> p c n", n=1).broadcast_to([P, NC, P]), ALU.mult), (q, "Bm"))
                        if q:
                            y = ymix[:, ds(b, 1), :].rearrange("p a t -> p (a t)")
                            if d == 0:
                                step0 = dve.tensor_copy(y, ps[:, 3, 0:T])
                            else:
                                scan_dve[0].wait(dve, (q, "Y0"), b)
                                step0 = dve.tensor_tensor(y, ps[:, 7, 0:T], y, ALU.add)
                            done(step0, (q, "Y0"))
                    for n in range(NC - q):
                        for d in range(2):
                            c = in_order(d)[n]
                            scan_pe[d].wait(dve, (q, f"st{n}"), b)
                            own(d, f"s{n - 1}" if n else "Bm", q)
                            scan_dve[d].done(dve.scalar_tensor_tensor(out=S[d][:, :], in0=ps[:, 4 * d, c * P:(c + 1) * P], scalar=pc[d][:, c:c + 1],
                                                                      in1=BM[d][:, c, :], op0=ALU.mult, op1=ALU.add), (q, f"s{n}"))
                    if q:
                        for d in range(2):
                            scan_pe[d].wait(dve, (q, f"st{NC - 1}"), b)
                            if d:
                                scan_dve[0].wait(dve, (q, "y"), b)
                            else:
                                scan_dve[1].wait(dve, (q, "Y0"), b)
                            scan_dve[d].done(dve.tensor_tensor(y, ps[:, 4 * d + 3, T:2 * T], y, ALU.add), (q, "y"))
                        chain_b(dve.tensor_copy(r[:, ds(b, 1), :], kn[:, T:2 * T].rearrange("p (a t) -> p a t", a=1)))

            chain(dve.tensor_scalar(oka, vcol("k_a", 0, RB), -1.0, 1.0, ALU.mult, ALU.add))
            dve.wait_ge(kscan_in, 16)
            dve.wait_ge(bd_clear, 7)
            with dve.Fori(0, RB) as b:
                chain.loop(b, 1)
                chain_b = chain
                scan_block(b)
            chain.end(RB)
            with dve.Fori(0, RB // 2) as i:
                y, bonus, g = (x[:, ds(i * 2, 2), :].rearrange("p a t -> p (a t)") for x in (ymix, r, gate))
                step = lambda ins, name: (gnd.done(ins, name), gnd.wait(dve, name, i))
                gnp.wait(dve, "mean", i)
                gnd.done(dve.scalar_tensor_tensor(out=yc[:, :], in0=ps[:, 4, :], scalar=-1.0 / HEAD, in1=y, op0=ALU.mult, op1=ALU.add), "c")
                gnp.wait(dve, "var", i)
                gnd.done(dve.tensor_scalar(yv[:, :], ps[:, 5, :], 1.0 / HEAD, GN_EPS, ALU.mult, ALU.add), "v")
                gna.wait(dve, "sqrt", i)
                step(dve.reciprocal(yn[:, :], yn[:, :]), "n0")
                step(dve.tensor_tensor(ysq[:, :], yn[:, :], yn[:, :], ALU.mult), "n1")
                step(dve.tensor_tensor(ysq[:, :], ysq[:, :], yv[:, :], ALU.mult), "n2")
                step(dve.tensor_scalar(ysq[:, :], ysq[:, :], -0.5, 1.5, ALU.mult, ALU.add), "n3")
                step(dve.tensor_tensor(yn[:, :], yn[:, :], ysq[:, :], ALU.mult), "n4")
                gnd.done(dve.tensor_tensor(yn[:, :], yn[:, :], yc[:, :], ALU.mult), "yn")
                gna.wait(dve, "w1", i)
                step(dve.tensor_tensor(yn[:, :], yn[:, :], bonus, ALU.add), "b")
                dve.wait_ge(gate_out, RB // 2)
                step(dve.tensor_tensor(y, yn[:, :], g, ALU.mult), "g")
            dve.sem_inc(ymix_done, 1)
            for n in range(4):
                dve.wait_ge(yhi, n + 1)
                dve.tensor_tensor(mov[:, 4 * n:4 * n + 4, 1, :], ymix[:, 4 * n:4 * n + 4, :], mov[:, 4 * n:4 * n + 4, 0, :].bitcast(F32), ALU.subtract)\
                   .then_inc(ylo, 1)
            def residual(ph, part):
                def evacuate(i, p):
                    summed(ph, i, p, px[:, :, :]).then_inc(bank_free, 1)
                    dve.wait_ge(bank_free, ph.pair(i, p) + (1 + BANK_CREDIT))
                    n = i * (2 * ph.pairs) + 2 * p
                    if part is None:
                        chain(dve.tensor_tensor(xT[:, ds(n, 2), :], px[:, :, :], xT[:, ds(n, 2), :], ALU.add))
                        return
                    for blk in range(2):
                        ins = dve.scalar_tensor_tensor(out=xT[:, ds(n + blk, 1), :], in0=px[:, blk:blk + 1, :], scalar=mod[:, part, 0, ds(n + blk, 1)],
                                                       in1=xT[:, ds(n + blk, 1), :], op0=ALU.mult, op1=ALU.add)
                        mark = chain.mark(ins)
                    chain.wait(mark)
                return evacuate, ph.pairs * (1 if part is None else 2)

            def add_residual(name, part):
                if PH[name] is order[-1]:
                    last_residual(PH[name])
                else:
                    gemm(PH[name], *residual(PH[name], part))
                dve.sem_inc(x_done, 1)

            def last_residual(ph):
                def evacuate(i, p):
                    summed(ph, i, p, px[:, :, :]).then_inc(bank_free, 1)
                    dve.wait_ge(bank_free, ph.pair(i, p) + (1 + BANK_CREDIT))
                    n = i * (2 * ph.pairs) + 2 * p
                    dve.tensor_tensor(xT[:, ds(n, 2), :], px[:, :, :], xT[:, ds(n, 2), :], ALU.add).then_inc(res_done, 1)
                    dve.wait_ge(res_done, i * ph.pairs + (p + 1))
                gemm(ph, evacuate)

            def gated(e, ph):
                before = e * PH["ffn"].trips
                def evacuate(i, p):
                    if p == 0:
                        summed(ph, i, p, gbuf[:, :, :]).then_inc(bank_free, 1)
                        return
                    dve.wait_ge(ffn_lo, i + (before + 1))
                    summed(ph, i, p, ubuf[:, :, :]).then_inc(bank_free, 1)
                    dve.wait_ge(bank_free, ph.pair(i, p) + (1 + BANK_CREDIT))
                    dve.wait_ge(ffn_s, i + (before + 1))
                    dve.tensor_tensor(ubuf[:, :, :], sbuf[:, :, :], ubuf[:, :, :], ALU.mult).then_inc(ffn_h, 1)
                    dve.wait_ge(ffn_hi, i + (before + 1))
                    dve.tensor_tensor(hid[:, ds(i * 2, 2), 1, :], ubuf[:, :, :], hid[:, ds(i * 2, 2), 0, :].bitcast(F32), ALU.subtract)\
                       .then_inc(ffn_lo, 1)
                return evacuate

            def norm_and_ffn(e, stat, norm, g, shift, suffix, gate_part):
                variance(stat, T)
                normed(norm, lambda k: xT[:, ds(k, 1), :], g, rstd[:, 0, :], shift,
                       lambda k: mov[:, ds(k, 1), 0, :], lambda k: mov[:, ds(k, 1), 1, :])
                gemm(PH["ffn" + suffix], gated(e, PH["ffn" + suffix]))
                add_residual("down" + suffix, gate_part)

            dve.sem_inc(ffn_lo, 1)
            dve.wait_ge(x_back, 16)
            add_residual("out", 2)
            norm_and_ffn(0, 1, 2, lambda k: gain[:, 2, ds(k, 1)], lambda k: mod[:, 3, 0, ds(k, 1)], "", 5)

            def scale_residual(stat, name, n0):
                variance(stat, T)
                for k in range(KB):
                    dve.scalar_tensor_tensor(out=xT[:, k, :], in0=xT[:, k, :], scalar=vcol(name, k), in1=rstd[:, 0, :], op0=ALU.mult, op1=ALU.mult)\
                       .then_inc(x_scaled, 1)
                dve.wait_ge(x_scaled, n0 + KB)

            scale_residual(2, "norm_final", 0)
            dve.sem_inc(x_done, 1)
            variance(3, T)
            normed(3, lambda k: xT[:, ds(k, 1), :], lambda k: vcol("ln1_w_2", k), rstd[:, 0, :], None,
                   lambda k: mov[:, ds(k, 1), 0, :], lambda k: mov[:, ds(k, 1), 1, :])
            gemm(PH["in_2"], lambda i, p: summed(PH["in_2"], i, p, p2[:, ds(i * 4 + 2 * p, 2), :]).then_inc(bank_free, 1))
            dve.wait_ge(bank_free, IN2_OUT)
            dve.wait_ge(lam_exp, 2)
            lw1, e1, w1, w2, s1 = (lcol[:, n, :] for n in range(1, 6))
            chain(dve.tensor_scalar(w1, e1, 2.0, None, ALU.add))
            chain(dve.reciprocal(w1, w1))
            chain(dve.tensor_tensor(w1, w1, e1, ALU.mult))
            chain(dve.tensor_tensor(w2, w1, w1, ALU.mult))
            chain(dve.tensor_scalar(s1, w2, 1.0 / 17, None, ALU.mult))
            for n in range(15, 1, -2):
                chain(dve.scalar_tensor_tensor(out=s1, in0=s1, scalar=1.0 / n, in1=w2, op0=ALU.add, op1=ALU.mult))
            chain(dve.scalar_tensor_tensor(out=s1, in0=s1, scalar=1.0, in1=w1, op0=ALU.add, op1=ALU.mult))
            chain(dve.tensor_scalar(e1, vcol("lru_lambda_2", 0, RB), 0.0, LRU_C / 2, ALU.min, ALU.mult))
            dve.scalar_tensor_tensor(out=lw1, in0=s1, scalar=-LRU_C, in1=e1, op0=ALU.mult, op1=ALU.add).then_inc(lam_ready, 1)
            marks = {}
            for tap in (2, 1, 0):
                lag = 3 - tap
                for n in range(RB):
                    if tap == 2:
                        dve.wait_ge(lru_mid, n + 1)
                    else:
                        chain.wait(marks[n])
                    ins = dve.scalar_tensor_tensor(out=lu[:, n, lag:T], in0=p2[:, LX + n, 0:T - lag], scalar=vcol("conv_w_2", tap * RB + n),
                                                   in1=lu[:, n, lag:T], op0=ALU.mult, op1=ALU.add)
                    if tap:
                        marks[n] = chain.mark(ins)
                    else:
                        ins.then_inc(lru_u, 1)
            dve.wait_ge(lru_t, RB)
            chain(dve.tensor_scalar(linv[:, :, :], la[:, :, :], -1.0, 1.0, ALU.mult, ALU.add))
            chain(dve.reciprocal(linv[:, :, :], linv[:, :, :]))
            dve.wait_ge(lru_sq, 1)
            dve.wait_ge(lru_iu, 1)
            m1 = chain.mark(dve.scalar_tensor_tensor(out=la[:, :, :], in0=la[:, :, :], scalar=1.0, in1=linv[:, :, :], op0=ALU.add, op1=ALU.mult))
            chain(dve.tensor_tensor(linv[:, :, :], linv[:, :, :], p2[:, LX:LX + RB, :], ALU.mult))
            chain(dve.tensor_tensor(lb[:, :, :], lb[:, :, :], linv[:, :, :], ALU.mult))
            for n in range(RB):
                m1 = chain.mark(dve.tensor_tensor_scan(lu[:, n, :], la[:, n, :], lb[:, n, :], 0.0, ALU.mult, ALU.add))
            chain.wait(m1)
            dve.wait_ge(lru_gelu, 1)
            chain(dve.tensor_tensor(p2[:, LX:LX + RB, :], lu[:, :, :], p2[:, LG:LG + RB, :], ALU.mult))
            def head(h, first=False):
                retp.wait(dve, "sw", h)
                if not first:
                    retp.wait(dve, "sc", h - 1)
                retd.done(dve.tensor_tensor(rqk[:, :, :], ps[:, 0, :].rearrange("p (a t) -> p a t", a=2), both(rsin), ALU.mult), "qs")
                retd.wait(dve, "qs", h)
                retg.wait(dve, "qc", h)
                retd.done(dve.tensor_tensor(rqk[:, :, :], rqk[:, :, :], rqc[:, :, :], ALU.add), "qr")
                retp.wait(dve, "sc", h)
                if not first:
                    retp.wait(dve, "o", h - 1)
                retd.done(dve.tensor_tensor(rp[:, :], ps[:, 2, 0:T + P], kret[:, ds(h * (T + P) + (2 * T + P), T + P)], ALU.mult), "pr")

            dve.wait_ge(kret_in, 16)
            head(0, True)
            with dve.Fori(0, RET_HEADS - 1) as i:
                head(i + 1)
            dve.wait_ge(ret_silu, 1)
            with dve.Fori(0, RET_HEADS // 2) as i:
                o = ro[:, ds(i * 2, 2), :].rearrange("p a t -> p (a t)")
                step = lambda ins, name: (rnd.done(ins, name), rnd.wait(dve, name, i))
                rnp.wait(dve, "mean", i)
                rnd.done(dve.scalar_tensor_tensor(out=oc[:, :], in0=ps[:, 4, :], scalar=-1.0 / P, in1=o, op0=ALU.mult, op1=ALU.add), "c")
                rnp.wait(dve, "var", i)
                rnd.done(dve.tensor_scalar(ov[:, :], ps[:, 5, :], 1.0 / P, RMS_EPS, ALU.mult, ALU.add), "v")
                rna.wait(dve, "sqrt", i)
                step(dve.reciprocal(on[:, :], on[:, :]), "n0")
                step(dve.tensor_tensor(osq[:, :], on[:, :], on[:, :], ALU.mult), "n1")
                step(dve.tensor_tensor(osq[:, :], osq[:, :], ov[:, :], ALU.mult), "n2")
                step(dve.tensor_scalar(osq[:, :], osq[:, :], -0.5, 1.5, ALU.mult, ALU.add), "n3")
                step(dve.tensor_tensor(on[:, :], on[:, :], osq[:, :], ALU.mult), "n4")
                step(dve.tensor_tensor(on[:, :], on[:, :], oc[:, :], ALU.mult), "yn")
                for blk in range(2):
                    n = i * 2 + blk
                    half = slice(blk * T, (blk + 1) * T)
                    rnd.done(dve.tensor_scalar(on[:, half], on[:, half], vcol("ret_gn_w_2", n), None, ALU.mult), f"w{blk}")
                rnd.wait(dve, "w1", i)
                step(dve.tensor_tensor(p2[:, ds(i * 2 + RB, 2), :].rearrange("p a t -> p (a t)"), on[:, :],
                                       p2[:, ds(i * 2 + RG, 2), :].rearrange("p a t -> p (a t)"), ALU.mult), "g")
            dve.sem_inc(y2_done, 1)
            for n in range(4):
                dve.wait_ge(y2_hi, n + 1)
                dve.tensor_tensor(mov[:, 4 * n:4 * n + 4, 1, :], p2[:, 4 * n:4 * n + 4, :], mov[:, 4 * n:4 * n + 4, 0, :].bitcast(F32), ALU.subtract)\
                   .then_inc(y2_lo, 1)
            add_residual("out_2", None)
            norm_and_ffn(1, 4, 4, lambda k: vcol("ln2_w_2", k), None, "_2", None)
            scale_residual(5, "final_norm_w_2", KB)
            for n in range(1, 8, 2):
                dve.wait_ge(row_turned, n + 1)
                dve.tensor_copy(orow[:, n % 2, (n // 2) * BANK:(n // 2 + 1) * BANK], ps[:, n, :]).then_inc(row_dve, 1)

        @block.tensor
        def _(pe):
            pe.sem_inc(split_free, SPLIT_CREDIT)

            def gemm(ph, product):
                def trip(i):
                    for p in range(ph.pairs):
                        pe.wait_ge(bank_free, ph.pair(i, p) + 1)
                        for c in range(ph.per_pair):
                            j = p * ph.per_pair + c
                            pe.wait_ge(lo_ready, ph.chunk(i, j) + (1 + RING))
                            for kk in range(CK):
                                k = c * CK + kk
                                mm = product(p, ph.slot(j), kk, k, k == 0, k == ph.rows - 1)
                            mm.then_inc(split_free, 1)
                    after(i) if after else None
                after = AFTER.get(ph.name)
                loop(pe, ph, trip)

            def on_x(ph, moving):
                def product(p, s, kk, k, first, last):
                    for blk in range(2):
                        b, w = ph.bank(p) + blk, slice(blk * P, (blk + 1) * P)
                        pe.matmul(ps[:, b, :], hi[:, s, kk, w], moving(k, None), start=first, stop=False)
                        mm = pe.matmul(ps[:, b, 0:T], lo[:, s, kk, w], moving(k, 0), start=False, stop=last)
                    return mm
                return product

            def on_both(ph, widths):
                def product(p, s, kk, k, first, last):
                    for blk in range(2):
                        b, w = ph.bank(p) + blk, slice(blk * widths, (blk + 1) * widths)
                        pe.matmul(ps[0:widths, b, :], hi[:, s, kk, w], mov1[:, k, 0, :, :], start=first, stop=False)
                        pe.matmul(ps[0:widths, b, :], hi[:, s, kk, w], mov1[:, k, 1, :, :], start=False, stop=False)
                        mm = pe.matmul(ps[0:widths, b, :], lo[:, s, kk, w], mov1[:, k, 0, :, :], start=False, stop=last)
                    return mm
                return product

            def sums_of_squares(n, width):
                for k in range(KB):
                    pe.wait_ge(sq_ready, n * KB + k + 1)
                    pe.matmul(ps[:, 7, 0:width], ones, sq[:, k % 2, 0:width], start=(k == 0), stop=(k == KB - 1))\
                      .then_inc(sq_used, 1)

            AFTER = {}
            pe.wait_ge(const_in, 16)
            pe.wait_ge(vec_in, 16 * VEC_DMAS)
            for t in range(4):
                mm = pe.transpose(ps[:, 0, t * P:(t + 1) * P], vrow[:, t, :], ident)
            mm.then_inc(vec_turned, 1)
            pe.wait_ge(row_in, 32)
            for k in range(KB + 1):
                if k < KB:
                    if k >= 4:
                        pe.wait_ge(sq_ready, k - 3)
                        pe.wait_ge(x_out, k - 3)
                    for a, src in enumerate((crow, xrow)):
                        for h in range(2):
                            mm = pe.transpose(ps[:, 1 + k % 4, (2 * a + h) * P:(2 * a + h + 1) * P],
                                              src[:, h, k * P:(k + 1) * P], ident)
                    mm.then_inc(turned, 1)
                if k >= 1:
                    pe.wait_ge(sq_ready, k)
                    pe.matmul(ps[:, 7, :], ones, sq[:, (k - 1) % 2, :], start=(k == 1), stop=(k == KB)).then_inc(sq_used, 1)
            pe.wait_ge(c4_ready, 2)
            pe.wait_ge(vec_ready, 1)
            pe.wait_ge(x_out, KB)
            pe.wait_ge(ctx_out, KB)

            def mod_rows(p, s, kk, k, first, last):
                b = PH["mod"].bank(p)
                pe.matmul(ps[:, b, 0:CN], c4[:, k, :], hi[:, s, kk, :], start=first, stop=False)
                return pe.matmul(ps[:, b, 0:CN], c4[:, k, :], lo[:, s, kk, :], start=False, stop=last)

            def mod_columns(i):
                pe.wait_ge(bank_free, PH["mod"].pair(i, PH["mod"].pairs - 1) + (1 + BANK_CREDIT))
                for k in range(KB):
                    mm = pe.matmul(ps[:, 5, 2 * k:2 * k + 2], mrow[:, k * P:(k + 1) * P], sel[0:4, 0:2], start=True, stop=True)
                mm.then_inc(mcol_ready, 1)
            AFTER["mod"] = mod_columns
            gemm(PH["mod"], mod_rows)
            pe.wait_ge(mov_ready, 2 * KB)
            gemm(PH["in_kv"], on_both(PH["in_kv"], P))
            lora_both, lora_x = on_both(PH["in_lora"], LORA), on_x(PH["in_lora"], lambda k, h: mov1[:, k, :, 1, :] if h is None else mov1[:, k, h, 1, :])
            gemm(PH["in_lora"], lambda p, *a: (lora_both, lora_x)[p](p, *a))
            for name in ("in_r", "in_rest"):
                gemm(PH[name], on_x(PH[name], lambda k, h: mov1[:, k, :, 1, :] if h is None else mov1[:, k, h, 1, :]))
            pe.wait_ge(bank_free, REST_OUT)
            pe.wait_ge(four_in, 16)
            for n in range(4):
                h = n // 2
                for blk in range(2 * (n % 2), 2 * (n % 2) + 2):
                    mm = pe.matmul(ps[:, 4 + n, (blk % 2) * T:(blk % 2 + 1) * T], proj[:, 12 + blk, h * P:(h + 1) * P], kfour[:, 0, :],
                                   start=True, stop=True)
                mm.then_inc(uf_turned, 1)
            pe.wait_ge(uf_ready, 4)
            for blk in range(4):
                for n, (h, cs) in enumerate((h, cs) for h in range(2) for cs in range(2)):
                    mm = pe.matmul(ps[:, blk // 2, (blk % 2) * T:(blk % 2 + 1) * T], uf[:, h, blk, cs, :], kfour[:, 1 + 2 * h + cs, :],
                                   start=(n == 0), stop=(n == 3))
                if blk % 2:
                    mm.then_inc(four_done, 1)

            def scan_block(b):
                for q in range(2):
                    w = P + C * q

                    def each(d, name, bank, lhs, rhs, n=P, begin=True, end=True, fin=True, paired=False):
                        for c in range(NC):
                            if paired:
                                o = ps[:, 4 * d + bank + c // 2, (c % 2) * n:(c % 2 + 1) * n]
                            else:
                                o = ps[:, 4 * d + bank, c * n:(c + 1) * n]
                            mm = lhs(c, o) if rhs is None else pe.matmul(o, lhs(c), rhs(c), start=begin, stop=end)
                        if fin:
                            scan_pe[d].done(mm, (q, name))

                    def two(d, name, bank, lhs1, rhs1, lhs2, rhs2, n):
                        for c in range(NC):
                            o = ps[:, 4 * d + bank, c * n:(c + 1) * n]
                            pe.matmul(o, lhs1(c), rhs1(c), start=True, stop=False)
                            mm = pe.matmul(o, lhs2(c), rhs2(c), start=False, stop=True)
                        if name:
                            scan_pe[d].done(mm, (q, name))

                    for d in range(2):
                        act, dve = scan_act[d], scan_dve[d]
                        if q == 0 and d == 0:
                            act.wait(pe, (0, "ksq"), b)
                            scan_pe[0].done(pe.matmul(ps[:, 2, :], blk64, kn[:, :], start=True, stop=True), (q, "kk"))
                        if q:
                            scan_dve[d].wait(pe, (0, f"s{NC - 1}"), b)
                        for n in range(2):
                            mm = pe.matmul(ps[:, 4 * d + 3, n * T:(n + 1) * T], decw[0:LORA, 2 * n + d, :], wdad[0:LORA, n, q, :], start=True, stop=True)
                        scan_pe[d].done(mm, (q, "zz"))
                        if q and d:
                            dve.wait(pe, (q, "rk1"), b)
                            scan_pe[d].done(pe.matmul(ps[:, 6, 0:T], blk64, kn[:, 0:T], start=True, stop=True), (q, "rk"))
                    for d in range(2):
                        act, dve = scan_act[d], scan_dve[d]
                        dve.wait(pe, (q, "rho" if q else "k1"), b)
                        act.wait(pe, (q, "sa"), b)
                        each(d, "G1", 0, lambda c: bdB[d][:, c, :], lambda c: bdA[d][:, c, 0:w], w, paired=True)
                        each(d, "G2", 2, lambda c: bdK[d][:, c, :], lambda c: bdA[d][:, c, 0:w], w, paired=True)
                    for d in range(2):
                        act, dve = scan_act[d], scan_dve[d]
                        act.wait(pe, (q, "U"), b)
                        each(d, "tA", 0, lambda c, o: pe.transpose(o, bdA[d][:, c, 0:P], ident), None)
                        each(d, "tB", 1, lambda c, o: pe.transpose(o, bdB[d][:, c, :], ident), None)
                        dve.wait(pe, (q, "M"), b)
                        each(d, "tK", 2, lambda c, o: pe.transpose(o, bdK[d][:, c, :], ident), None)
                        if d == 0:
                            act.wait(pe, (q, "bv1"), b)
                            each(d, "tV", 3, lambda c, o: pe.transpose(o, bdV[:, c, :], ident), None)
                    for d in range(2):
                        act, dve = scan_act[d], scan_dve[d]
                        scan_act[0].wait(pe, (q, "oV"), b)
                        act.wait(pe, (q, "oK"), b)
                        each(d, "MV", 0, lambda c: MT[d][:, c, :], lambda c: tokV[:, c, :])
                        scan_pool[d].wait(pe, (q, "m0"), b)
                        each(d, "L0", 1, lambda c, o: pe.transpose(o, ULa[d][:, c, :], ident), None)
                    for l in range(1, LEVELS):
                        lev = (ULa, MT)[l % 2]
                        for d in range(2):
                            scan_pool[d].wait(pe, (q, f"m{l}"), b)
                            scan_dve[d].wait(pe, (q, f"X{l - 1}"), b)
                            scan_dve[d].wait(pe, (q, f"T{l - 1}"), b)
                            each(d, f"Y{l}", 2 if l % 2 else 1, lambda c: lev[d][:, c, :], lambda c: XY[d][:, c, 0, :])
                        for d in range(2):
                            scan_act[d].wait(pe, (q, f"Yb{l}"), b)
                            if l == 1:
                                scan_act[d].wait(pe, (q, "oMV"), b)
                            if l < LEVELS - 1:
                                each(d, None, 3, lambda c: XT[d][:, c, :], lambda c: XY[d][:, c, 1, :], fin=False)
                            each(d, f"X{l}", 0, lambda c: XY[d][:, c, 1, :], lambda c: XT[d][:, c, :])
                    for d in range(2):
                        scan_dve[d].wait(pe, (q, f"T{LEVELS - 1}"), b)
                        each(d, "Z", 2, lambda c: XT[d][:, c, :], lambda c: tokR[d][:, c, :, :], 2 * P, paired=True)
                    for d in range(2):
                        scan_act[d].wait(pe, (q, "Z"), b)
                        each(d, "A", 0, lambda c: XY[d][:, c, 0, :], lambda c: tokBQ[d][:, c, 0:w], w, paired=True)
                        two(d, None if q else "B", 2, lambda c: tokK[d][:, c, :], lambda c: tokV[:, c, :],
                            lambda c: tokBQ[d][:, c, 0:P], lambda c: XY[d][:, c, 1, :], P)
                        if q:
                            two(d, "B", 3, lambda c: tokV[:, c, :], lambda c: RT[d][:, c, :],
                                lambda c: XY[d][:, c, 1, :], lambda c: tokBQ[d][:, c, P:P + C], C)
                    for n in range(NC):
                        for d in range(2):
                            c = in_order(d)[n]
                            if n:
                                scan_dve[d].wait(pe, (q, f"s{n - 1}"), b)
                            else:
                                scan_dve[d].wait(pe, (q, "Y0" if q else "Bm"), b)
                            if q:
                                mm = pe.matmul(ps[:, 4 * d + 3, T + c * C:T + (c + 1) * C], S[d][:, :], bdA[d][:, c, P:P + C], start=True, stop=True)
                            if n < NC - q:
                                mm = pe.matmul(ps[:, 4 * d, c * P:(c + 1) * P], AT[d][:, c, :], S[d][:, :], start=True, stop=True)
                            scan_pe[d].done(mm, (q, f"st{n}"))
                for d in range(2):
                    scan_dve[d].wait(pe, (1, "y"), b)

            pe.wait_ge(wd_ready, 1)
            pe.wait_ge(mix_done, 1)
            with pe.Fori(0, RB) as b:
                pe.wait_ge(decw_in, b * 32 + 32)
                scan_block(b)
            pe.wait_ge(scan_dve[0].sem, RB * len(scan_dve[0].names))
            pe.wait_ge(scan_dve[1].sem, RB * len(scan_dve[1].names))
            pe.wait_ge(gup_in, 16)
            pe.wait_ge(gd_ready, 1)
            for n in range(RB):
                if n >= 8:
                    pe.wait_ge(gate_out, n // 2 - 3)
                for k in range(2):
                    mm = pe.matmul(ps[:, n // 2 % 4, (n % 2) * T:(n % 2 + 1) * T], gup[:, k, n * P:(n + 1) * P], gd[:, k, :], start=(k == 0), stop=(k == 1))
                if n % 2:
                    mm.then_inc(gate_mm, 1)
            with pe.Fori(0, RB // 2) as i:
                gnp.done(pe.matmul(ps[:, 4, :], blk64, ymix[:, ds(i * 2, 2), :], start=True, stop=True), "mean")
                gna.wait(pe, "sq", i)
                gnp.done(pe.matmul(ps[:, 5, :], blk64, ysq[:, :], start=True, stop=True), "var")
            pe.wait_ge(gate_out, RB // 2)
            on_mov = lambda k, h: mov[:, k, :, :] if h is None else mov[:, k, h, :]
            on_hid = lambda k, h: hid[:, k, :, :] if h is None else hid[:, k, h, :]

            def norm_and_ffn(e, stat, norm, suffix):
                sums_of_squares(stat, T)
                pe.wait_ge(mov_ready, (norm + 1) * KB)
                gemm(PH["ffn" + suffix], on_x(PH["ffn" + suffix], on_mov))
                pe.wait_ge(ffn_lo, (e + 1) * PH["ffn"].trips + 1)
                gemm(PH["down" + suffix], on_x(PH["down" + suffix], on_hid))

            pe.wait_ge(ylo, 4)
            gemm(PH["out"], on_x(PH["out"], on_mov))
            norm_and_ffn(0, 1, 2, "")
            sums_of_squares(2, T)
            sums_of_squares(3, T)
            pe.wait_ge(mov_ready, 4 * KB)
            gemm(PH["in_2"], on_x(PH["in_2"], on_mov))
            pe.wait_ge(gw_in, 32)
            pe.wait_ge(bank_free, IN2_OUT)
            for n in range(RB):
                pe.wait_ge(lru_u, n + 1)
                for g in range(2):
                    mm = pe.matmul(ps[:, 4 * g + n // 2, (n % 2) * T:(n % 2 + 1) * T], gw[:, g, n, :], lu[:, n, :], start=True, stop=True)
                if n % 2:
                    mm.then_inc(lru_gates, 1)
            pe.wait_ge(lru_i, 2 * RB)
            def head(h, first=False):
                retg.wait(pe, "v", h)
                if not first:
                    reta.wait(pe, "vt", h - 1)
                for n in range(2):
                    mm = pe.transpose(ps[:, 1, n * P:(n + 1) * P], rv[:, n * P:(n + 1) * P], ident)
                retp.done(mm, "vt")
                if not first:
                    retd.wait(pe, "qs", h - 1)
                retp.done(pe.matmul(ps[:, 0, :].rearrange("p (a b t) -> p a b t", a=2, b=1), swap, qk_of(h), start=True, stop=True), "sw")
                retd.wait(pe, "qr", h)
                pe.matmul(ps[:, 2, 0:T], rqk[:, 1, 0:P], rqk[:, 0, :], start=True, stop=True)
                retp.done(pe.matmul(ps[:, 2, T:T + P], rqk[:, 1, P:T], rqk[:, 0, P:T], start=True, stop=True), "sc")
                retd.wait(pe, "pr", h)
                reta.wait(pe, "vt", h)
                if not first:
                    reta.wait(pe, "o", h - 1)
                pe.matmul(ps[:, 3, 0:T], rvt[:, 0, :], rp[:, 0:T], start=True, stop=False)
                retp.done(pe.matmul(ps[:, 3, P:T], rvt[:, 1, :], rp[:, T:T + P], start=False, stop=True), "o")

            pe.wait_ge(kret_in, 16)
            head(0, True)
            with pe.Fori(0, RET_HEADS - 1) as i:
                head(i + 1)
            reta.wait(pe, "o", RET_HEADS - 1)
            with pe.Fori(0, RET_HEADS // 2) as i:
                rnp.done(pe.matmul(ps[:, 4, :], ones, ro[:, ds(i * 2, 2), :], start=True, stop=True), "mean")
                rna.wait(pe, "sq", i)
                rnp.done(pe.matmul(ps[:, 5, :], ones, osq[:, :], start=True, stop=True), "var")
                rnd.wait(pe, "v", i)
            pe.wait_ge(y2_lo, 4)
            gemm(PH["out_2"], on_x(PH["out_2"], on_mov))
            norm_and_ffn(1, 4, 4, "_2")
            sums_of_squares(5, T)
            pe.wait_ge(x_scaled, 2 * KB)
            pe.wait_ge(bank_free, PH["down_2"].pair(1, 3) + 1 + BANK_CREDIT)
            for n in range(8):
                for k in range(4):
                    mm = pe.transpose(ps[:, n, k * P:(k + 1) * P], xT[:, 4 * (n // 2) + k, (n % 2) * P:(n % 2 + 1) * P], ident)
                mm.then_inc(row_turned, 1)


INPUTS = ["x", "c", "ctx", "c_ctx", "w_mod", "b_mod", "norm_mix", "w_in", "rw_shift", "dec_w0", "dec_up", "iclr_a0",
          "iclr_up", "k_k", "k_a", "r_k", "ln_w", "ln_b", "g_up", "conv_w", "w_out", "norm_ffn", "w_gate", "w_up",
          "w_down", "norm_final", "ln1_w_2", "w_in_2", "conv_w_2", "conv_b_2", "gate_a_w_2", "gate_a_b_2",
          "gate_x_w_2", "gate_x_b_2", "lru_lambda_2", "ret_gn_w_2", "w_out_2", "ln2_w_2", "w_ffn_gate_2",
          "w_ffn_up_2", "w_ffn_down_2", "final_norm_w_2"]


def kernel(**inputs):
    import concourse.bacc as bacc
    from concourse.bass_utils import run_bass_kernel_spmd as run

    nc = bacc.Bacc("TRN2", target_bir_lowering=False, num_devices=1)
    arrays = {"in_" + n: np.ascontiguousarray(inputs[n]) for n in INPUTS}
    arrays = {n: a[0] if a.shape[0] == 1 and n[3:] not in ("x", "c", "ctx") and a.ndim > 1 else a for n, a in arrays.items()}
    arrays.update(constants())
    given = {n: nc.dram_tensor(n, a.shape, F32, kind="ExternalInput").ap() for n, a in arrays.items()}
    given = {n.removeprefix("in_"): ap for n, ap in given.items()}
    out = nc.dram_tensor("out_h", (1, T, D), F32, kind="ExternalOutput").ap()
    program(nc, given, out)
    return run(nc, [arrays], core_ids=[0]).results[0]["out_h"]
```

```python
from contextlib import ExitStack

import numpy as np

import concourse.bass as bass
from concourse import mybir

F32 = mybir.dt.float32
F32R = mybir.dt.float32r
ALU = mybir.AluOpType
ACT = mybir.ActivationFunctionType
ds = bass.ds

P = 128
D = 2048
T = 256
KB = D // P
HEAD = 64
D_RWKV, D_CONV, D_FOUR = D // 2, D // 4, D // 4
RB = D_RWKV // P
LORA = 96
GATE = 256
D_FF = ((8 * D + 3 * 256 - 1) // (3 * 256)) * 256
FB = D_FF // P
WD0 = 3 * D_RWKV
GD0 = WD0 + 2 * LORA
CG0 = GD0 + GATE
D_IN = CG0 + 3 * D_CONV + D_FOUR
D_IN_2 = 6 * (D // 2)
GRID_W = 64
RMS_EPS, GN_EPS, KK_EPS = 1e-6, 64e-5, 1e-12
LRU_BLOCKS, LRU_C = 8, 8.0
RET_HEADS = 8
DECAY_SCALE = -float(np.exp(np.float32(-0.5)))

RING = 4
CK, CN = 4, 256
BANK = 512
C = 64
NC = T // C

STREAM = [
    ("mod", 6, 8, KB), ("in_kv", 4, 2, KB), ("in_lora", 1, 2, KB), ("in_r", 2, 2, KB), ("in_rest", 4, 2, KB),
    ("out", 4, 2, KB), ("ffn", 22, 2, KB), ("down", 2, 4, FB),
    ("in_2", 12, 2, KB), ("out_2", 4, 2, KB), ("ffn_2", 22, 2, KB), ("down_2", 2, 4, FB),
]


class Phase:

    def __init__(self, name, trips, pairs, rows, g0, p0):
        self.name, self.trips, self.pairs, self.rows = name, trips, pairs, rows
        self.per_pair = rows // CK
        self.chunks = pairs * self.per_pair
        self.g0, self.p0 = g0, p0

    def chunk(self, i, j):
        return i * self.chunks + (self.g0 + j)

    def slot(self, j):
        return (self.g0 + j) % RING

    def rounds(self, i, j):
        return i * (self.chunks // RING) + (self.g0 + j) // RING

    def pair(self, i, p):
        return i * self.pairs + (self.p0 + p)

    def bank(self, p):
        return 2 * ((self.p0 + p) % 2)

    def last_chunk(self, i, p):
        return self.chunk(i, (p + 1) * self.per_pair - 1)


def phases():
    out, g, p = {}, 0, 0
    for name, trips, pairs, rows in STREAM:
        ph = Phase(name, trips, pairs, rows, g, p)
        assert trips == 1 or ph.chunks % RING == 0
        out[name] = ph
        g += trips * ph.chunks
        p += trips * pairs
    return out, g


class Steps:

    def __init__(self, sem, names):
        self.sem, self.names = sem, list(names)
        assert len(set(self.names)) == len(self.names)
        self.at = 0

    def value(self, name, rounds=0):
        return rounds * len(self.names) + (self.names.index(name) + 1)

    def done(self, ins, name):
        assert self.names[self.at % len(self.names)] == name, (name, self.names[self.at % len(self.names)])
        self.at += 1
        ins.then_inc(self.sem, 1)

    def wait(self, eng, name, rounds=0):
        eng.wait_ge(self.sem, self.value(name, rounds))


class Chain:

    def __init__(self, eng, sem):
        self.eng, self.sem, self.base, self.n, self.i, self.per = eng, sem, 0, 0, None, 0

    def loop(self, i, per):
        self.base, self.i, self.per, self.n = self.base + self.n, i, per, 0

    def end(self, trips):
        assert self.n == self.per, (self.n, self.per)
        self.base, self.n, self.i = self.base + trips * self.per, 0, None

    def mark(self, ins):
        ins.then_inc(self.sem, 1)
        self.n += 1
        return self.base + self.n if self.i is None else self.i * self.per + (self.base + self.n)

    def wait(self, value):
        self.eng.wait_ge(self.sem, value)

    def __call__(self, ins):
        self.wait(self.mark(ins))


def vector_rows():
    order = [
        [("b_mod", 96), ("norm_mix", 16), ("norm_ffn", 16)],
        [("ln1_w_2", 16), ("ln2_w_2", 16), ("norm_final", 16), ("final_norm_w_2", 16), ("dec_w0", 16),
         ("iclr_a0", 16), ("k_k", 8), ("k_a", 8), ("r_k", 8), ("ln_w", 8)],
        [("ln_b", 8), ("conv_w", 12), ("conv_w_2", 32), ("conv_b_2", 8), ("gate_a_b_2", 8), ("gate_x_b_2", 8),
         ("lru_lambda_2", 8), ("ret_gn_w_2", 8), ("c", 16), ("c_ctx", 16)],
        [("shift_rkv", 72), ("shift_gd", 6), ("shift_wd", 3), ("shift_ad", 3)],
    ]
    out = {}
    for t, row in enumerate(order):
        at = 0
        for name, n in row:
            out[name] = (t, at, n)
            at += n
        assert at <= P
    return out


VROWS = vector_rows()


def constants():
    f = np.float32
    eye = np.eye(P, dtype=f)
    blk = np.kron(np.eye(2, dtype=f), np.ones((HEAD, HEAD), f))
    sel = np.zeros((P, P), f)
    sel[0, 0] = sel[1, 0] = sel[2, 1] = sel[3, 1] = 1
    n = np.arange(HEAD)
    cos_h = np.cos(2 * np.pi * np.outer(n, n) / HEAD)
    sin_h = np.sin(2 * np.pi * np.outer(n, n) / HEAD)
    four_h = np.concatenate([np.kron(np.eye(2), cos_h), np.kron(np.eye(2), sin_h)], 1)
    m = np.arange(T)
    ang = 2 * np.pi * (np.outer(m, m) % T) / T
    norm = 1 / np.sqrt(T * HEAD)
    four_t = np.stack([np.cos(ang) * norm, -np.sin(ang) * norm], 1)
    four_t = four_t.reshape(2, P, 2, T).transpose(1, 0, 2, 3).reshape(P, 4 * T)
    basics = np.concatenate([eye, blk, sel, np.ones((P, P), f)], 1).astype(f)
    fourier = np.concatenate([four_h, four_t], 1).astype(f)

    s, t = np.arange(C)[:, None], np.arange(C)[None, :]
    scan = []
    for d in range(2):
        before = s < t if d == 0 else s > t
        two = lambda a: np.kron(np.eye(2), a)
        row = [two(before)]
        size = 1
        while size < C:
            row.append(two(before & (s // (2 * size) == t // (2 * size)) & (s // size != t // size)))
            size *= 2
        scan += row + [np.concatenate([before | (s == t)] * 2, 0)]
    first = np.tile((np.arange(T) % C != 0).astype(f), (P, 1))
    scan = np.concatenate(scan + [first], 1).astype(f)

    half = P // 2
    inv_freq = f(10000.0) ** (-np.arange(0, P, 2, dtype=f) / f(P))
    rot = np.arange(T, dtype=f)[None, :] * inv_freq[:, None]
    cos, sin = np.cos(rot).astype(f), np.sin(rot).astype(f)
    swap = np.zeros((P, P), f)
    swap[np.arange(half) + half, np.arange(half)] = -1
    swap[np.arange(half), np.arange(half) + half] = 1
    log_gamma = np.log1p(-np.exp2(-5.0 - np.arange(RET_HEADS)))
    sp, tt = np.arange(P)[:, None], np.arange(T)[None, :]
    decay = []
    for h in range(RET_HEADS):
        d0 = np.where(tt >= sp, np.exp(log_gamma[h] * np.maximum(tt - sp, 0)) * P ** -0.5, 0)
        decay += [d0, d0[:, :P]]
    ret = np.concatenate([np.concatenate([cos, cos], 0), np.concatenate([sin, sin], 0), swap] + decay, 1).astype(f)
    return {"k_basics": basics, "k_fourier": fourier, "k_scan": scan, "k_ret": ret}


LEVELS = 6
SCAN_DIR = P * (1 + LEVELS) + C


def program(nc, A, out):
    PH, TOTAL = phases()
    order = [PH[row[0]] for row in STREAM]
    base = -(-nc.sbuf_base // 32) * 32
    KIB = 1024

    def at(name, offset, shape, dt=F32):
        return nc.alloc_sbuf_tensor_at(name, shape, dt, offset=base + offset)

    raw = at("raw", 0, [P, RING, CK, CN])
    hi = at("hi", 16 * KIB, [P, RING, CK, CN], F32R)
    lo = at("lo", 32 * KIB, [P, RING, CK, CN], F32R)
    fix = 48 * KIB
    vec = at("vec", fix, [P, 4, P])
    mod = at("mod", fix + 2048, [P, 6, 2, KB])
    gain = at("gain", fix + 2816, [P, 4, KB])
    lcol = at("lcol", fix + 3072, [P, 8, RB])
    basics = at("basics", fix + 3584, [P, 4, P])
    rstd = at("rstd", fix + 5632, [P, 2, T])
    tmp = at("tmp", fix + 7680, [P, 2, 2, T])
    sq = at("sq", fix + 11776, [P, 2, 2 * T])
    nt = at("nt", fix + 15872, [P, 2, 2 * T])
    gd = at("gd", fix + 11776, [P, 2, T])
    wdad = at("wdad", fix + 13824, [P, 2, 2, T])
    px = at("px", fix + 17920, [P, 2, T])
    decw = at("decw", fix + 17920, [P, 4, P])
    xT = at("xT", 68 * KIB, [P, KB, T])
    ymix = at("ymix", 68 * KIB, [P, KB, T])
    R = 84 * KIB
    xrow = at("xrow", R, [P, 2, D])
    crow = at("crow", R + 16 * KIB, [P, 2, D])
    vrow = at("vrow", R + 32 * KIB, [P, 4, P])
    ctxT = at("ctxT", R + 40 * KIB, [P, KB, T])
    c4 = at("c4", R + 56 * KIB, [P, KB, P], F32R)
    csil = at("csil", R + 64 * KIB, [P, 2, KB])
    mrow = at("mrow", R + 66 * KIB, [4, D])
    kv = at("kv", R, [P, 2 * RB, 2, T])
    r = at("r", R + 32 * KIB, [P, RB, T])
    proj = at("proj", R + 40 * KIB, [P, 16, T])
    mov1 = at("mov1", R + 56 * KIB, [P, KB, 2, 2, T], F32R)

    oka = lcol[:, 0, :]
    ident, blk64, sel, ones = (basics[:, n, :] for n in range(4))
    ps = nc.alloc_psum_tensor("ps", [P, 8, BANK], F32)

    xres = nc.dram_tensor("xres", [P, KB * T], F32, kind="Internal").ap()

    def vcol(name, n, count=1, rows=P):
        t, first, _ = VROWS[name]
        return vec[0:rows, t, ds(first + n, count)]

    sems = {}

    def sem(name):
        sems[name] = nc.alloc_semaphore(name)
        return sems[name]

    raw_in = [sem(f"raw_in{s}") for s in range(RING)]
    hi_ready, lo_ready, split_free = sem("hi_ready"), sem("lo_ready"), sem("split_free")
    bank_free, tmp_ready = sem("bank_free"), sem("tmp_ready")
    SPLIT_CREDIT, BANK_CREDIT = RING, 2
    LOWS0 = PH["in_lora"].p0 + 1
    v_chain, a_chain, g_chain = sem("v_chain"), sem("a_chain"), sem("g_chain")
    vec_clear, vec_in, row_in, const_in = sem("vec_clear"), sem("vec_in"), sem("row_in"), sem("const_in")
    vec_turned, vec_ready = sem("vec_turned"), sem("vec_ready")
    turned, ctx_out, x_out = sem("turned"), sem("ctx_out"), sem("x_out")
    csil_ready, chi_ready, c4_clear, c4_ready = sem("csil_ready"), sem("chi_ready"), sem("c4_clear"), sem("c4_ready")
    mrow_ready, mcol_ready, mod_ready, gain_ready = (sem(n) for n in ("mrow_ready", "mcol_ready", "mod_ready", "gain_ready"))
    sq_ready, sq_used, var_ready, sqrt_ready, rstd_ready = (
        sem(n) for n in ("sq_ready", "sq_used", "var_ready", "sqrt_ready", "rstd_ready"))
    nt_ready, nhi_ready, mov_ready = sem("nt_ready"), sem("nhi_ready"), sem("mov_ready")
    shift_ready = sem("shift_ready")
    M0 = R + 56 * KIB
    kfour = at("kfour", M0, [P, 5, T])
    uf = at("uf", M0 + 5 * KIB, [P, 2, 4, 2, P])
    x_spilled, four_in, uf_turned, uf_ready, four_done, conv_mid, mix_done = (
        sem(n) for n in ("x_spilled", "four_in", "uf_turned", "uf_ready", "four_done", "conv_mid",
                         "mix_done"))
    REST_DONE = PH["in_rest"].last_chunk(3, 1) + 1 + SPLIT_CREDIT
    REST_OUT = PH["in_rest"].pair(3, 1) + 1 + BANK_CREDIT

    def per_dir(name, offset, shape, step):
        return [at(f"{name}{d}", offset + d * step, shape) for d in range(2)]

    kscan = at("kscan", R + 40 * KIB, [P, 2 * SCAN_DIR + T])
    strict = [kscan[:, d * SCAN_DIR:d * SCAN_DIR + P] for d in range(2)]
    level = [[kscan[:, d * SCAN_DIR + (1 + n) * P:d * SCAN_DIR + (2 + n) * P] for n in range(LEVELS)] for d in range(2)]
    upto = [kscan[:, d * SCAN_DIR + (1 + LEVELS) * P:(d + 1) * SCAN_DIR] for d in range(2)]
    inside = kscan[:, 2 * SCAN_DIR:2 * SCAN_DIR + T]
    S0 = R + 49 * KIB
    bdV = at("bdV", S0, [P, NC, P])
    tokV = at("tokV", S0 + 2048, [P, NC, P])
    S = per_dir("S", S0 + 4096, [P, P], 512)
    kk = at("kk", fix + 5632, [P, 2 * T])
    kq = at("kq", fix + 7680, [P, 2 * T])
    kn = at("kn", fix + 9728, [P, 2 * T])
    DIR = 33 * KIB
    def per_unit(name, shape, ctx_offset, x_offset):
        return [[at(f"{name}{q}{d}", ((hi2, lo2)[d] + ctx_offset) if q == 0 else M0 + x_offset + d * DIR, shape) for d in range(2)]
                for q in range(2)]

    hi2, lo2 = 24 * KIB, 40 * KIB
    bdA = per_unit("bdA", [P, NC, P + C], 0, 0)
    bdB = per_unit("bdB", [P, NC, P], 3072, 3072)
    bdK = per_unit("bdK", [P, NC, P], 5120, 5120)
    pc = [per_dir(f"pc{q}", S0 + 5120 + 64 * q, [P, NC], 32) for q in range(2)]
    tokR = per_dir("tokR", M0 + 7168, [P, NC, 2, P], DIR)
    tokBQ = per_dir("tokBQ", M0 + 11264, [P, NC, P + C], DIR)
    tokK = per_dir("tokK", M0 + 14336, [P, NC, P], DIR)
    U = per_dir("U", M0 + 16384, [P, NC, P], DIR)
    ULa = per_dir("ULa", M0 + 18432, [P, NC, P], DIR)
    MT = per_dir("MT", M0 + 20480, [P, NC, P], DIR)
    RT = per_dir("RT", M0 + 22528, [P, NC, C], DIR)
    XY = per_dir("XY", M0 + 23552, [P, NC, 2, P], DIR)
    lw, L, ex, en, av, kd = ([x for x in per_dir(n, M0 + 27648 + 1024 * k, [P, T], DIR)]
                             for k, n in enumerate(("lw", "L", "ex", "en", "av", "kd")))
    XT, AT, BM = bdB, U, bdK
    bcol = lcol[:, 6, 0:4]

    FRONT = range(1, LEVELS)

    def steps(kind, names):
        return [Steps(sem(f"{kind}{d}"), [(q, n) for q in range(2) for n in names(q, d)]) for d in range(2)]

    def front_pe_names(q, d):
        return ["zz"] + (["kk"] if q == 0 and d == 0 else []) + (["rk"] if q and d else []) + ["G1"]

    def front_act_names(q, d):
        out = (["bc0", "bc1"] if q == 0 and d == 0 else []) + (["bv0", "bv1"] if d == 0 else []) + ["sg", "sa"]
        out += (["ksq"] if q == 0 and d == 0 else []) + ["eex", "en", "pc"] + (["ep"] if q else [])
        return out + (["ksqrt"] if q == 0 and d == 0 else [])

    def front_dve_names(q, d):
        out = (["kq"] if q == 0 and d == 0 else []) + ["lw", "L", "Lx"] + (["kv"] if q == 0 and d == 0 else []) + ["kf", "kd"]
        if q:
            return out + ["ba"] + (["rk0", "rk1"] if d else []) + ["k0", "k1", "a0", "a1", "b0", "b1", "rho"] + (["bonus"] if d else [])
        if d == 0:
            return out + ["n0", "k0", "k1", "n1", "n2", "n3", "n4", "n5", "kk", "ba", "a0", "a1", "b0", "b1"]
        return out + ["k0", "k1", "ba", "a0", "a1", "b0", "b1"]

    def pe_names(q, d):
        out = ["G2", "tA", "tB", "tK"] + (["tV"] if d == 0 else []) + ["MV", "L0"]
        for l in range(1, LEVELS):
            out += [f"Y{l}"] + ([f"X{l}"] if l < LEVELS - 1 else []) + [f"T{l}"]
        return out + ["Z", "A", "B"] + [f"st{n}" for n in range(NC)]

    def act_names(q, d):
        return ["U", "oA", "oB", "oMV"] + [f"Yb{l}" for l in range(1, LEVELS)] + ["Z"]

    def dve_names(q, d):
        out = (["Q", "R"] if q else ["S"]) + ["M", "oK"] + (["oV"] if d == 0 else []) + ["T0", "X0"]
        for l in range(1, LEVELS):
            out += ([f"X{l}"] if l < LEVELS - 1 else []) + [f"T{l}"]
        out += ["AT"] + (["rho2"] if q else []) + ["Bm"] + (["Y0"] if q else [])
        return out + [f"s{n}" for n in range(NC - q)] + (["y"] if q else [])

    def pool_names(q, d):
        return [f"m{l}" for l in range(LEVELS)]

    front_pe, front_act, front_dve = (steps(k, n) for k, n in (
        ("front_pe", front_pe_names), ("front_act", front_act_names), ("front_dve", front_dve_names)))
    scan_pe, scan_act, scan_dve, scan_pool = (steps(k, n) for k, n in (
        ("scan_pe", pe_names), ("scan_act", act_names), ("scan_dve", dve_names), ("scan_pool", pool_names)))

    def following(b, q):
        return (b, 1) if q == 0 else (b + 1, 0)

    decw_in, kscan_in, bd_clear, wd_ready = sem("decw_in"), sem("kscan_in"), sem("bd_clear"), sem("wd_ready")

    def in_order(d):
        return range(NC) if d == 0 else range(NC - 1, -1, -1)

    def chunks_of(ap):
        return ap.rearrange("p (c t) -> p c t", c=NC)

    def over_chunks(ap):
        n = ap.shape[-1]
        return ap.rearrange("p (a n) -> p a n", a=1).broadcast_to([P, NC, n])

    def over_banks(ap):
        n = ap.shape[-1]
        return ap.rearrange("p (a b n) -> p a b n", a=1, b=1).broadcast_to([P, 2, NC // 2, n])

    def two_banks(b, width, first, count):
        return ps[:, b:b + 2, 0:2 * width].rearrange("p b (c n) -> p b c n", c=2)[:, :, :, first:first + count]

    def in_pairs(ap):
        return ap.rearrange("p (a b) n -> p a b n", a=2)

    gup = at("gup", M0, [P, 2, D_RWKV])
    gate = at("gate", M0 + 8 * KIB, [P, RB, T])
    yc = at("yc", M0 + 16 * KIB, [P, 2 * T])
    ysq = at("ysq", M0 + 18 * KIB, [P, 2 * T])
    yv = at("yv", M0 + 20 * KIB, [P, 2 * T])
    yn = at("yn", M0 + 22 * KIB, [P, 2 * T])
    gup_in, gd_ready, gate_mm, gate_out, gn_pe, gn_act, gn_dve, ymix_done = (
        sem(n) for n in ("gup_in", "gd_ready", "gate_mm", "gate_out", "gn_pe", "gn_act", "gn_dve", "ymix_done"))
    gnp, gna, gnd = (Steps(s, n) for s, n in (
        (gn_pe, ["mean", "var"]), (gn_act, ["sq", "sqrt", "w0", "w1"]),
        (gn_dve, ["c", "v", "n0", "n1", "n2", "n3", "n4", "yn", "b", "g"])))

    mov = at("mov", R + 88 * KIB, [P, KB, 2, T], F32R)
    hid = at("hid", R, [P, FB, 2, T], F32R)
    gbuf = at("gbuf", fix + 11776, [P, 2, T])
    sbuf = at("sbuf", fix + 13824, [P, 2, T])
    ubuf = at("ubuf", fix + 15872, [P, 2, T])
    yhi, ylo, x_back, res_done = sem("yhi"), sem("ylo"), sem("x_back"), sem("res_done")
    ffn_g, ffn_s, ffn_h, ffn_hi, ffn_lo = (sem(n) for n in ("ffn_g", "ffn_s", "ffn_h", "ffn_hi", "ffn_lo"))
    knt = at("knt", M0 + 27648, [P, 2 * T])

    LX, LG, RQ, RK, RV, RG = (n * RB for n in range(6))
    p2 = at("p2", R, [P, 6 * RB, T])
    lu = at("lu", R + 48 * KIB, [P, RB, T])
    la = at("la", R + 56 * KIB, [P, RB, T])
    lb = at("lb", R + 64 * KIB, [P, RB, T])
    linv = at("linv", R + 72 * KIB, [P, RB, T])
    gw = at("gw", R + 80 * KIB, [P, 2, LRU_BLOCKS, P])
    Q0 = R + 88 * KIB
    KRET = 2 * T + P + RET_HEADS * (T + P)
    kret = at("kret", Q0, [P, KRET])
    rcos, rsin = (kret[:, n * T:(n + 1) * T] for n in range(2))
    swap = kret[:, 2 * T:2 * T + P]
    rqk = at("rqk", Q0 + 14848, [P, 2, T])
    rqc = at("rqc", Q0 + 16896, [P, 2, T])
    rv = at("rv", Q0 + 18944, [P, T])
    rvt = at("rvt", Q0 + 19968, [P, 2, P])
    rp = at("rp", Q0 + 20992, [P, T + P])
    ro = at("ro", Q0 + 22528, [P, RET_HEADS, T])
    oc, osq, ov, on = (at(n, fix + 11776 + 2048 * k, [P, 2 * T]) for k, n in enumerate(("oc", "osq", "ov", "on")))
    orow = at("orow", R, [P, 2, D])
    IN2_DONE = PH["in_2"].last_chunk(11, 1) + 1 + SPLIT_CREDIT
    IN2_OUT = PH["in_2"].pair(11, 1) + 1 + BANK_CREDIT
    x_done, x_scaled, lam_exp, lam_ready, gw_in, kret_in = (
        sem(n) for n in ("x_done", "x_scaled", "lam_exp", "lam_ready", "gw_in", "kret_in"))
    lru_mid, lru_u, lru_gates, lru_i, lru_t, lru_sq, lru_iu, lru_out, lru_gelu, ret_silu = (
        sem(n) for n in ("lru_mid", "lru_u", "lru_gates", "lru_i", "lru_t", "lru_sq", "lru_iu", "lru_out", "lru_gelu", "ret_silu"))
    retp, reta, retd, retg = (Steps(sem(s), n) for s, n in (
        ("ret_pe", ["vt", "sw", "sc", "o"]), ("ret_act", ["vt", "o"]), ("ret_dve", ["qs", "qr", "pr"]), ("ret_pool", ["v", "qc"])))
    rnp, rna, rnd = (Steps(sem(s), n) for s, n in (
        ("rn_pe", ["mean", "var"]), ("rn_act", ["sq", "sqrt"]),
        ("rn_dve", ["c", "v", "n0", "n1", "n2", "n3", "n4", "yn", "w0", "w1", "g"])))
    y2_done, y2_hi, y2_lo, row_turned, row_act, row_dve, result_out = (
        sem(n) for n in ("y2_done", "y2_hi", "y2_lo", "row_turned", "row_act", "row_dve", "result_out"))

    def both(ap):
        return ap.rearrange("p (a n) -> p a n", a=1).broadcast_to([P, 2, T])

    def qk_of(h):
        return p2[:, RQ:RQ + 2 * RB, :].rearrange("p (a h) t -> p a h t", a=2)[:, :, ds(h, 1), :]

    def weights(w, rows, col):
        return w[rows * P:(rows + CK) * P, ds(col, CN)].rearrange("(k p) n -> p k n", p=P)

    def chunk_source(ph, i, j):
        p, q = j // ph.per_pair, (j % ph.per_pair) * CK
        if ph.name == "mod":
            return weights(A["w_mod"], q, i * D + p * CN)
        if ph.name == "in_kv":
            return weights(A["w_in"], q, i * (2 * CN) + (D_RWKV + p * CN))
        if ph.name == "in_lora":
            return weights(A["w_in"], q, (WD0, GD0)[p])
        if ph.name == "in_r":
            return weights(A["w_in"], q, i * (2 * CN) + p * CN)
        if ph.name == "in_rest":
            return weights(A["w_in"], q, i * (2 * CN) + (CG0 + p * CN))
        if ph.name in ("ffn", "ffn_2"):
            tail = "" if ph.name == "ffn" else "_2"
            w = A[("w_gate", "w_up")[p]] if not tail else A[("w_ffn_gate_2", "w_ffn_up_2")[p]]
            return weights(w, q, i * CN)
        w = {"out": "w_out", "down": "w_down", "in_2": "w_in_2", "out_2": "w_out_2", "down_2": "w_ffn_down_2"}[ph.name]
        return weights(A[w], q, i * (ph.pairs * CN) + p * CN)

    def loop(eng, ph, body):
        if ph.trips == 1:
            body(0)
            return
        ends = ph is order[-1]
        with eng.Fori(0, ph.trips - ends) as i:
            body(i)
        if ends:
            body(ph.trips - 1)

    with nc.Block() as block:

        @block.sync
        def _(sp):
            sp.dma_start(xrow[:, :, :], A["x"][0].rearrange("(a p) d -> p a d", p=P)).then_inc(row_in, 16)
            sp.dma_start(crow[:, :, :], A["ctx"][0].rearrange("(a p) d -> p a d", p=P)).then_inc(row_in, 16)
            for ph in order:
                def trip(i):
                    for j in range(ph.chunks):
                        sp.wait_ge(lo_ready, ph.chunk(i, j) + 1)
                        sp.dma_start(raw[:, ph.slot(j), :, :], chunk_source(ph, i, j)).then_inc(raw_in[ph.slot(j)], 16)
                if ph.name == "in_r":
                    sp.wait_ge(mov_ready, 2 * KB)
                    sp.dma_start(xres.rearrange("p (k t) -> p k t", k=KB), xT[:, :, :]).then_inc(x_spilled, 16)
                loop(sp, ph, trip)
            for n in range(8):
                sp.wait_ge((row_act, row_dve)[n % 2], n // 2 + 1)
                sp.dma_start(out[0, (n % 2) * P:(n % 2 + 1) * P, (n // 2) * BANK:(n // 2 + 1) * BANK],
                             orow[:, n % 2, (n // 2) * BANK:(n // 2 + 1) * BANK]).then_inc(result_out, 16)
            sp.wait_ge(x_spilled, 16)
            sp.wait_ge(result_out, 8 * 16)

        @block.gpsimd
        def _(pool):
            pool.memset(vrow[:, :, :], 0.0).then_inc(vec_clear, 1)
            pool.memset(c4[:, :, :].bitcast(F32), 0.0).then_inc(c4_clear, 1)
            pool.dma_start(basics[:, :, :], A["k_basics"].rearrange("p (a n) -> p a n", a=4)).then_inc(const_in, 16)
            pool.wait_ge(vec_clear, 1)
            for name, (t, first, n) in VROWS.items():
                if name.startswith("shift"):
                    c0, width = {"shift_rkv": (0, P), "shift_gd": (GD0, P), "shift_wd": (WD0, LORA),
                                 "shift_ad": (WD0 + LORA, LORA)}[name]
                    src = A["rw_shift"][:, c0:c0 + n // 3 * width]
                    for tap in range(3):
                        pool.dma_start(vrow[first + tap * (n // 3):first + (tap + 1) * (n // 3), t, 0:width],
                                       src[tap].rearrange("(n c) -> n c", c=width)).then_inc(vec_in, 16)
                    continue
                src = A[name]
                names = " ".join("abcd"[:len(src.shape)])
                flat = src.rearrange(f"{names} -> ({names})") if len(src.shape) > 1 else src
                pool.dma_start(vrow[first:first + n, t, :], flat.rearrange("(n c) -> n c", c=P)).then_inc(vec_in, 16)

            pool.wait_ge(split_free, REST_DONE)
            pool.dma_start(kfour[:, :, :], A["k_fourier"].rearrange("p (a n) -> p a n", a=5)).then_inc(four_in, 16)
            pool.wait_ge(mix_done, 1)
            pool.dma_start(kscan[:, :], A["k_scan"]).then_inc(kscan_in, 16)

            def load_lora(b):
                for n, name in enumerate(("dec_up", "iclr_up")):
                    pool.dma_start(decw[0:LORA, 2 * n:2 * n + 2, :], A[name][:, :, ds(b, P)].rearrange("d p n -> p d n"))\
                        .then_inc(decw_in, 16)

            load_lora(0)
            for bd in [bdV[:, :, :]] + [x[q][d][:, :, 0:P] for q in range(2) for d in range(2) for x in (bdA, bdB, bdK)]:
                pool.memset(bd, 0.0).then_inc(bd_clear, 1)

            def mask_levels(b, q):
                for l in range(LEVELS):
                    for d in range(2):
                        dst = (ULa, MT)[l % 2][d]
                        if l == 0:
                            scan_act[d].wait(pool, (q, "U"), b)
                        else:
                            scan_pe[d].wait(pool, (q, ("MV", "L0", "Y1", "Y2", "Y3")[l - 1]), b)
                            if l == 2:
                                scan_dve[d].wait(pool, (q, "T0"), b)
                        scan_pool[d].done(pool.tensor_tensor(dst[:, :, :], U[d][:, :, :], over_chunks(level[d][l]), ALU.mult),
                                          (q, f"m{l}"))

            pool.wait_ge(kscan_in, 16)
            with pool.Fori(0, RB - 1) as b:
                mask_levels(b, 0)
                front_pe[1].wait(pool, (1, "zz"), b)
                load_lora(b * P + P)
                mask_levels(b, 1)
            mask_levels(RB - 1, 0)
            mask_levels(RB - 1, 1)

            scan_dve[0].wait(pool, (1, "y"), RB - 1)
            scan_dve[1].wait(pool, (1, "y"), RB - 1)
            pool.dma_start(gup[:, :, :], A["g_up"].rearrange("(k p) n -> p k n", p=P)).then_inc(gup_in, 16)
            pool.wait_ge(ylo, 4)
            pool.wait_ge(x_spilled, 16)
            pool.dma_start(xT[:, :, :], xres.rearrange("p (k t) -> p k t", k=KB)).then_inc(x_back, 16)

            pool.wait_ge(x_done, 2)
            for n, name in enumerate(("gate_a_w_2", "gate_x_w_2")):
                pool.dma_start(gw[:, n, :, :], A[name].rearrange("n c d -> c n d")).then_inc(gw_in, 16)
            pool.wait_ge(split_free, IN2_DONE)
            pool.dma_start(kret[:, :], A["k_ret"]).then_inc(kret_in, 16)
            pool.wait_ge(lru_u, RB)
            pool.wait_ge(lru_i, 2 * RB)
            pool.tensor_tensor(lb[:, :, :], lb[:, :, :], lu[:, :, :], ALU.mult).then_inc(lru_iu, 1)
            def head(h, first=False):
                if not first:
                    retp.wait(pool, "vt", h - 1)
                retg.done(pool.tensor_copy(rv[:, :], p2[:, ds(h + RV, 1), :]), "v")
                if not first:
                    retd.wait(pool, "qr", h - 1)
                retg.done(pool.tensor_tensor(rqc[:, :, :], qk_of(h), both(rcos), ALU.mult), "qc")

            pool.wait_ge(kret_in, 16)
            pool.wait_ge(bank_free, IN2_OUT)
            head(0, True)
            with pool.Fori(0, RET_HEADS - 1) as i:
                head(i + 1)
        VEC_DMAS = sum(3 if n.startswith("shift") else 1 for n in VROWS)

        @block.scalar
        def _(act):
            chain = Chain(act, a_chain)

            def split(ph, i, j):
                if isinstance(i, int) and ph.chunk(i, j) >= TOTAL:
                    return
                s = ph.slot(j)
                act.wait_ge(raw_in[s], (ph.rounds(i, j) + 1) * 16)
                act.wait_ge(split_free, ph.chunk(i, j) + 1)
                act.activation(hi[:, s, :, :], raw[:, s, :, :], ACT.Copy).then_inc(hi_ready, 1)

            def gemm(ph, evacuate):
                def trip(i):
                    for p in range(ph.pairs):
                        for j in range(p * ph.per_pair + 2, (p + 1) * ph.per_pair + 2):
                            split(ph, i, j)
                        evacuate(i, p)
                loop(act, ph, trip)

            def lows(ph, i, p, wait=True):
                if wait:
                    act.wait_ge(split_free, ph.last_chunk(i, p) + (1 + SPLIT_CREDIT))
                b, t = ph.bank(p), (ph.p0 + p) % 2
                act.activation(tmp[:, t, :, :], ps[:, b:b + 2, T:2 * T], ACT.Copy).then_inc(tmp_ready, 1)

            def sqrt_of_variance(n, width):
                act.wait_ge(var_ready, n + 1)
                act.activation(nt[:, 1, 0:width], nt[:, 0, 0:width], ACT.Sqrt).then_inc(sqrt_ready, 1)

            def squares(n):
                act.wait_ge(x_done, n)
                for k in range(KB):
                    if n * KB + k >= 2:
                        act.wait_ge(sq_used, n * KB + k - 1)
                    act.activation(sq[:, k % 2, 0:T], xT[:, k, :], ACT.Square).then_inc(sq_ready, 1)

            def normed_hi(n, dest, shift):
                with act.Fori(0, KB // 2) as i:
                    for e in range(2):
                        act.wait_ge(nt_ready, i * 2 + (n * KB + e + 1))
                        if shift is None:
                            ins = act.activation(dest(i * 2 + e), nt[:, e, 0:T], ACT.Copy)
                        else:
                            ins = act.activation(dest(i * 2 + e), nt[:, e, 0:T], ACT.Identity, bias=shift(i * 2 + e))
                        ins.then_inc(nhi_ready, 1)

            act.wait_ge(vec_turned, 1)
            act.activation(vec[:, :, :], ps[:, 0, :].rearrange("p (a n) -> p a n", a=4), ACT.Copy).then_inc(vec_ready, 1)
            act.wait_ge(vec_ready, 1)
            act.activation(csil[:, 0, :], vcol("c", 0, KB), ACT.Silu).then_inc(csil_ready, 1)
            act.activation(csil[:, 1, :], vcol("c_ctx", 0, KB), ACT.Silu).then_inc(csil_ready, 1)
            act.wait_ge(csil_ready, 2)
            act.wait_ge(c4_clear, 1)
            for q in range(2):
                act.activation(c4[:, :, 2 * q:2 * q + 1], csil[:, q, :], ACT.Copy).then_inc(chi_ready, 1)
            for k in range(KB):
                act.wait_ge(turned, k + 1)
                act.activation(ctxT[:, k, :], ps[:, 1 + k % 4, 0:T], ACT.Copy).then_inc(ctx_out, 1)
                if k >= 2:
                    act.wait_ge(sq_used, k - 1)
                act.activation(sq[:, k % 2, :], ps[:, 1 + k % 4, :], ACT.Square).then_inc(sq_ready, 1)
            sqrt_of_variance(0, 2 * T)
            for j in range(2):
                split(PH["mod"], 0, j)
            gemm(PH["mod"], lambda i, p: None)
            act.wait_ge(gain_ready, 3)
            normed_hi(0, lambda k: mov1[:, k, 0, 0, :], lambda k: mod[:, 0, 1, ds(k, 1)])
            normed_hi(1, lambda k: mov1[:, k, 0, 1, :], lambda k: mod[:, 0, 0, ds(k, 1)])

            def shift_both(i, p):
                ph = PH["in_kv"]
                act.wait_ge(split_free, ph.last_chunk(i, p) + (1 + SPLIT_CREDIT))
                for blk in range(2):
                    n = i * 4 + (2 * p + blk)
                    act.activation(kv[:, ds(n, 1), :, :], ps[:, ph.bank(p) + blk, :], ACT.Copy,
                                   scale=vcol("shift_rkv", n + (3 * RB + RB))).then_inc(shift_ready, 1)

            def shift_lora(i, p):
                ph = PH["in_lora"]
                act.wait_ge(split_free, ph.last_chunk(i, p) + (1 + SPLIT_CREDIT))
                if p == 0:
                    for blk, name in enumerate(("shift_wd", "shift_ad")):
                        act.activation(wdad[0:LORA, blk, :, :], ps[0:LORA, blk, :], ACT.Copy,
                                       scale=vcol(name, 1, rows=LORA)).then_inc(shift_ready, 1)
                    return
                lows(ph, i, p, wait=False)
                for blk in range(2):
                    act.wait_ge(bank_free, ph.pair(i, p) + (1 + BANK_CREDIT))
                    act.activation(gd[:, blk, :], px[:, blk, :], ACT.Copy, scale=vcol("shift_gd", 2 + blk)).then_inc(shift_ready, 1)

            def shift_r(i, p):
                lows(PH["in_r"], i, p)
                for blk in range(2):
                    n = i * 4 + (2 * p + blk)
                    act.wait_ge(bank_free, PH["in_r"].pair(i, p) + (1 + BANK_CREDIT))
                    act.activation(r[:, ds(n, 1), :], px[:, blk, :], ACT.Copy,
                                   scale=vcol("shift_rkv", n + 3 * RB)).then_inc(shift_ready, 1)

            gemm(PH["in_kv"], shift_both)
            gemm(PH["in_lora"], shift_lora)
            gemm(PH["in_r"], shift_r)
            gemm(PH["in_rest"], lambda i, p: lows(PH["in_rest"], i, p))
            act.activation(wdad[0:LORA, 0, :, :], wdad[0:LORA, 0, :, :], ACT.Tanh).then_inc(wd_ready, 1)
            act.wait_ge(conv_mid, 1)
            for blk in range(4):
                act.activation(ymix[:, RB + blk, :], proj[:, blk, :], ACT.Copy, scale=vcol("conv_w", 4 + blk)).then_inc(conv_mid, 1)
            for n in range(4):
                act.wait_ge(uf_turned, n + 1)
                act.activation(uf[:, n // 2, 2 * (n % 2):2 * (n % 2) + 2, :, :], ps[:, 4 + n, :], ACT.Copy).then_inc(uf_ready, 1)

            def front(b, q, stage):
                def done(d, ins, name):
                    front_act[d].done(ins, (q, name))
                first = q == 0
                if stage == 1:
                    if first:
                        for n, name in enumerate(("dec_w0", "iclr_a0")):
                            done(0, act.activation(bcol[:, 2 * n:2 * n + 2], vcol(name, 0, 2 * RB).rearrange("p (d n) -> p d n", d=2)[:, :, ds(b, 1)],
                                                   ACT.Copy), f"bc{n}")
                    for h in range(2):
                        hs = slice(h * HEAD, (h + 1) * HEAD)
                        done(0, act.activation(bdV[hs, :, hs], kv[hs, ds(b + RB, 1), q, :], ACT.Copy), f"bv{h}")
                    if first:
                        front_act[0].wait(act, (q, "bc1"), b)
                    for d in range(2):
                        front_pe[d].wait(act, (q, "zz"), b)
                        done(d, act.activation(lw[d][:, :], ps[:, 4 * d + 1, 0:T], ACT.Sigmoid, bias=bcol[:, d:d + 1]), "sg")
                        done(d, act.activation(av[d][:, :], ps[:, 4 * d + 1, T:2 * T], ACT.Sigmoid, bias=bcol[:, 2 + d:3 + d]), "sa")
                    if first:
                        front_dve[0].wait(act, (q, "kq"), b)
                        done(0, act.activation(kn[:, :], kq[:, :], ACT.Square), "ksq")
                if stage == 2:
                    for d in range(2):
                        front_dve[d].wait(act, (q, "Lx"), b)
                        done(d, act.activation(ex[d][:, :], ex[d][:, :], ACT.Exp), "eex")
                        done(d, act.activation(en[d][:, :], L[d][:, :], ACT.Exp, scale=-1.0), "en")
                        last = C - 1 if d == 0 else 0
                        done(d, act.activation(pc[q][d][:, :], chunks_of(L[d][:, :])[:, :, last], ACT.Exp), "pc")
                        if q:
                            front_act[d].wait(act, (q, "pc"), b)
                            done(d, act.activation(L[d][:, :], L[d][:, :], ACT.Exp), "ep")
                    if first:
                        front_dve[0].wait(act, (q, "kv"), b)
                        done(0, act.activation(kk[:, :], kn[:, :], ACT.Sqrt), "ksqrt")

            def unit(b, q, ahead=True):
                for d in range(2):
                    front_pe[d].wait(act, (q, "G1"), b)
                    if q:
                        scan_dve[d].wait(act, (q, "Q"), b)
                    scan_act[d].done(act.activation(in_pairs(U[d][:, :, :]), two_banks(4 * d, P + C * q, 0, P), ACT.Copy), (q, "U"))
                for name, src, bank, dst in (("oA", "tA", 0, lambda d: tokR[d][:, :, 0, :]), ("oB", "tB", 1, lambda d: tokBQ[d][:, :, 0:P]),
                                             ("oMV", "MV", 0, lambda d: tokR[d][:, :, 1, :])):
                    for d in range(2):
                        scan_pe[d].wait(act, (q, src), b)
                        scan_act[d].done(act.activation(dst(d), ps[:, 4 * d + bank, :], ACT.Copy), (q, name))
                for l in FRONT:
                    for d in range(2):
                        scan_pe[d].wait(act, (q, f"Y{l}"), b)
                        scan_act[d].done(act.activation(XY[d][:, :, 1, :], ps[:, 4 * d + 2, :], ACT.Copy), (q, f"Yb{l}"))
                    if ahead:
                        front(*following(b, q), l)
                for d in range(2):
                    scan_pe[d].wait(act, (q, "Z"), b)
                    scan_act[d].done(act.activation(XY[d][:, :, :, :].rearrange("p (a b) z n -> p a (b z n)", a=2), ps[:, 4 * d + 2:4 * d + 4, :],
                                                    ACT.Copy, scale=-1.0), (q, "Z"))
                for d in range(2):
                    scan_pe[d].wait(act, (q, f"st{NC - 1}"), b)

            act.wait_ge(bd_clear, 13)
            for stage in FRONT:
                front(0, 0, stage)
            with act.Fori(0, RB - 1) as b:
                unit(b, 0)
                unit(b, 1)
            unit(RB - 1, 0)
            unit(RB - 1, 1, ahead=False)
            act.activation(gd[:, :, :], gd[:, :, :], ACT.Sigmoid).then_inc(gd_ready, 1)
            for n in range(RB // 2):
                act.wait_ge(gate_mm, n + 1)
                act.activation(gate[:, 2 * n:2 * n + 2, :], ps[:, n % 4, :], ACT.Copy).then_inc(gate_out, 1)
            with act.Fori(0, RB // 2) as i:
                gnd.wait(act, "c", i)
                gna.done(act.activation(ysq[:, :], yc[:, :], ACT.Square), "sq")
                gnd.wait(act, "v", i)
                gna.done(act.activation(yn[:, :], yv[:, :], ACT.Sqrt), "sqrt")
                gnd.wait(act, "yn", i)
                for blk in range(2):
                    n = i * 2 + blk
                    gna.done(act.activation(yn[:, blk * T:(blk + 1) * T], yn[:, blk * T:(blk + 1) * T], ACT.Identity,
                                            scale=vcol("ln_w", n), bias=vcol("ln_b", n)), f"w{blk}")
            for n in range(4):
                act.wait_ge(ymix_done, 1)
                act.activation(mov[:, 4 * n:4 * n + 4, 0, :], ymix[:, 4 * n:4 * n + 4, :], ACT.Copy).then_inc(yhi, 1)
            def gated(e, ph):
                def evacuate(i, p):
                    lows(ph, i, p)
                    if p == 0:
                        act.wait_ge(bank_free, ph.pair(i, p) + (1 + BANK_CREDIT))
                        act.activation(sbuf[:, :, :], gbuf[:, :, :], ACT.Silu).then_inc(ffn_s, 1)
                    else:
                        act.wait_ge(ffn_h, i + (e * PH["ffn"].trips + 1))
                        act.activation(hid[:, ds(i * 2, 2), 0, :], ubuf[:, :, :], ACT.Copy).then_inc(ffn_hi, 1)
                return evacuate

            def norm_and_ffn(e, stat, norm, shift, suffix):
                squares(stat)
                sqrt_of_variance(stat, T)
                normed_hi(norm, lambda k: mov[:, ds(k, 1), 0, :], shift)
                gemm(PH["ffn" + suffix], gated(e, PH["ffn" + suffix]))
                gemm(PH["down" + suffix], lambda i, p: lows(PH["down" + suffix], i, p))

            gemm(PH["out"], lambda i, p: lows(PH["out"], i, p))
            norm_and_ffn(0, 1, 2, lambda k: mod[:, 3, 0, ds(k, 1)], "")
            for stat in (2, 3):
                squares(stat)
                sqrt_of_variance(stat, T)
            normed_hi(3, lambda k: mov[:, ds(k, 1), 0, :], None)
            gemm(PH["in_2"], lambda i, p: lows(PH["in_2"], i, p))
            lam = vcol("lru_lambda_2", 0, RB)
            act.activation(lcol[:, 1, :], lam, ACT.Abs).then_inc(lam_exp, 1)
            act.wait_ge(lam_exp, 1)
            act.activation(lcol[:, 2, :], lcol[:, 1, :], ACT.Exp, scale=-1.0).then_inc(lam_exp, 1)
            act.wait_ge(bank_free, IN2_OUT)
            for n in range(RB):
                act.activation(lu[:, n, :], p2[:, LX + n, :], ACT.Identity, scale=vcol("conv_w_2", 3 * RB + n), bias=vcol("conv_b_2", n))\
                   .then_inc(lru_mid, 1)
            for n in range(RB):
                act.wait_ge(lru_gates, n // 2 + 1)
                half = slice((n % 2) * T, (n % 2 + 1) * T)
                act.activation(la[:, n, :], ps[:, n // 2, half], ACT.Sigmoid, bias=vcol("gate_a_b_2", n)).then_inc(lru_i, 1)
                act.activation(lb[:, n, :], ps[:, 4 + n // 2, half], ACT.Sigmoid, bias=vcol("gate_x_b_2", n)).then_inc(lru_i, 1)
            act.wait_ge(lam_ready, 1)
            act.wait_ge(lru_i, 2 * RB)
            for n in range(RB):
                act.activation(la[:, n, :], la[:, n, :], ACT.Tanh, scale=lcol[:, 1, n:n + 1]).then_inc(lru_t, 1)
            act.wait_ge(lru_t, RB)
            act.wait_ge(lru_u, RB)
            act.activation(p2[:, LX:LX + RB, :], la[:, :, :], ACT.Sqrt, scale=-4.0).then_inc(lru_sq, 1)
            act.activation(p2[:, LG:LG + RB, :], p2[:, LG:LG + RB, :], ACT.Gelu_apprx_tanh).then_inc(lru_gelu, 1)
            act.activation(p2[:, RG:RG + RB, :], p2[:, RG:RG + RB, :], ACT.Silu).then_inc(ret_silu, 1)
            def head(h, first=False):
                retp.wait(act, "vt", h)
                if not first:
                    retp.wait(act, "o", h - 1)
                reta.done(act.activation(rvt[:, :, :], ps[:, 1, 0:T], ACT.Copy), "vt")
                retp.wait(act, "o", h)
                reta.done(act.activation(ro[:, ds(h, 1), :], ps[:, 3, 0:T], ACT.Copy), "o")

            head(0, True)
            with act.Fori(0, RET_HEADS - 1) as i:
                head(i + 1)
            with act.Fori(0, RET_HEADS // 2) as i:
                rnd.wait(act, "c", i)
                rna.done(act.activation(osq[:, :], oc[:, :], ACT.Square), "sq")
                rnd.wait(act, "v", i)
                rna.done(act.activation(on[:, :], ov[:, :], ACT.Sqrt), "sqrt")
            act.wait_ge(y2_done, 1)
            for n in range(4):
                act.activation(mov[:, 4 * n:4 * n + 4, 0, :], p2[:, 4 * n:4 * n + 4, :], ACT.Copy).then_inc(y2_hi, 1)
            gemm(PH["out_2"], lambda i, p: lows(PH["out_2"], i, p))
            norm_and_ffn(1, 4, 4, None, "_2")
            squares(5)
            sqrt_of_variance(5, T)
            for n in range(0, 8, 2):
                act.wait_ge(row_turned, n + 1)
                act.activation(orow[:, n % 2, (n // 2) * BANK:(n // 2 + 1) * BANK], ps[:, n, :], ACT.Copy).then_inc(row_act, 1)

        @block.vector
        def _(dve):
            chain = Chain(dve, v_chain)
            dve.sem_inc(lo_ready, RING)
            dve.sem_inc(bank_free, BANK_CREDIT)

            def split(ph, i, j):
                if isinstance(i, int) and ph.chunk(i, j) >= TOTAL:
                    return
                s = ph.slot(j)
                dve.wait_ge(hi_ready, ph.chunk(i, j) + 1)
                dve.tensor_tensor(lo[:, s, :, :], raw[:, s, :, :], hi[:, s, :, :].bitcast(F32), ALU.subtract)\
                   .then_inc(lo_ready, 1)

            def gemm(ph, evacuate, per_trip=0):
                def trip(i):
                    if per_trip:
                        chain.loop(i if ph.trips > 1 else None, per_trip)
                    for p in range(ph.pairs):
                        for j in range(p * ph.per_pair + 2, (p + 1) * ph.per_pair + 2):
                            split(ph, i, j)
                        evacuate(i, p)
                assert not (per_trip and ph is order[-1])
                loop(dve, ph, trip)
                if per_trip:
                    chain.end(ph.trips)

            def summed(ph, i, p, dest):
                b, t = ph.bank(p), (ph.p0 + p) % 2
                dve.wait_ge(tmp_ready, ph.pair(i, p) + (1 - LOWS0))
                return dve.tensor_tensor(dest, ps[:, b:b + 2, 0:T], tmp[:, t, :, :], ALU.add)

            def variance(n, width):
                v, s, y = nt[:, 0, 0:width], nt[:, 1, 0:width], rstd[:, :, :].rearrange("p a t -> p (a t)")[:, 0:width]
                dve.wait_ge(sq_used, (n + 1) * KB)
                dve.tensor_scalar(v, ps[:, 7, 0:width], 1.0 / D, RMS_EPS, ALU.mult, ALU.add).then_inc(var_ready, 1)
                dve.wait_ge(sqrt_ready, n + 1)
                chain(dve.reciprocal(y, s))
                chain(dve.tensor_tensor(s, y, y, ALU.mult))
                chain(dve.tensor_tensor(s, s, v, ALU.mult))
                chain(dve.tensor_scalar(s, s, -0.5, 1.5, ALU.mult, ALU.add))
                chain(dve.tensor_tensor(y, y, s, ALU.mult))

            def normed(n, src, g, rs, shift, hi_of, lo_of):
                with dve.Fori(0, KB // 2) as i:
                    for e in range(2):
                        dve.scalar_tensor_tensor(out=nt[:, e, 0:T], in0=src(i * 2 + e), scalar=g(i * 2 + e), in1=rs,
                                                 op0=ALU.mult, op1=ALU.mult).then_inc(nt_ready, 1)
                    for e in range(2):
                        k = i * 2 + e
                        dve.wait_ge(nhi_ready, i * 2 + (n * KB + e + 1))
                        if shift is None:
                            ins = dve.tensor_tensor(lo_of(k), nt[:, e, 0:T], hi_of(k).bitcast(F32), ALU.subtract)
                        else:
                            ins = dve.scalar_tensor_tensor(out=lo_of(k), in0=nt[:, e, 0:T], scalar=shift(k),
                                                           in1=hi_of(k).bitcast(F32), op0=ALU.add, op1=ALU.subtract)
                        ins.then_inc(mov_ready, 1)
                    dve.wait_ge(mov_ready, i * 2 + (n * KB + 2))

            dve.wait_ge(vec_ready, 1)
            for q in range(2):
                dve.wait_ge(chi_ready, q + 1)
                dve.tensor_tensor(c4[:, :, 2 * q + 1:2 * q + 2], csil[:, q, :],
                                  c4[:, :, 2 * q:2 * q + 1].bitcast(F32), ALU.subtract).then_inc(c4_ready, 1)
            for k in range(KB):
                dve.wait_ge(sq_ready, k + 1)
                dve.tensor_copy(xT[:, k, :], ps[:, 1 + k % 4, T:2 * T]).then_inc(x_out, 1)
            variance(0, 2 * T)
            for j in range(2):
                split(PH["mod"], 0, j)

            def mod_row(i, p):
                ph = PH["mod"]
                dve.wait_ge(split_free, ph.last_chunk(i, p) + (1 + SPLIT_CREDIT))
                dve.tensor_copy(mrow[:, p * CN:(p + 1) * CN], ps[0:4, ph.bank(p), 0:CN]).then_inc(bank_free, 1)
                if p == ph.pairs - 1:
                    dve.wait_ge(mcol_ready, i + 1)
                    for q in range(2):
                        dve.tensor_tensor(mod[:, ds(i, 1), q, :],
                                          ps[:, 5, 0:2 * KB].rearrange("p (k q) -> p q k", q=2)[:, q, :],
                                          vcol("b_mod", i * KB, KB), ALU.add).then_inc(mod_ready, 1)
            gemm(PH["mod"], mod_row)
            dve.wait_ge(mod_ready, 12)
            for n, (part, q, norm) in enumerate([(1, 0, "norm_mix"), (1, 1, "norm_mix"), (4, 0, "norm_ffn")]):
                dve.scalar_tensor_tensor(out=gain[:, n, :], in0=mod[:, part, q, :], scalar=1.0, in1=vcol(norm, 0, KB),
                                         op0=ALU.add, op1=ALU.mult).then_inc(gain_ready, 1)
            dve.wait_ge(gain_ready, 3)
            for n, (src, q) in enumerate([(ctxT, 1), (xT, 0)]):
                normed(n, lambda k: src[:, ds(k, 1), :], lambda k: gain[:, q, ds(k, 1)], rstd[:, 1 - q, :],
                       lambda k: mod[:, 0, q, ds(k, 1)], lambda k: mov1[:, ds(k, 1), 0, 1 - q, :], lambda k: mov1[:, ds(k, 1), 1, 1 - q, :])

            def outer_taps(dest, src, before, after):
                n = dest.shape[-1]
                chain(dve.scalar_tensor_tensor(out=dest[:, :, 1:n], in0=src[:, :, 0:n - 1], scalar=before,
                                               in1=dest[:, :, 1:n], op0=ALU.mult, op1=ALU.add))
                return dve.scalar_tensor_tensor(out=dest[:, :, 0:n - 1], in0=src[:, :, 1:n], scalar=after,
                                                in1=dest[:, :, 0:n - 1], op0=ALU.mult, op1=ALU.add)

            def shift_both(i, p):
                ph = PH["in_kv"]
                for blk in range(2):
                    n = i * 4 + (2 * p + blk)
                    dve.wait_ge(shift_ready, n + 1)
                    ins = outer_taps(kv[:, ds(n, 1), :, :].rearrange("p n q t -> p (n q) t"),
                                     ps[:, ph.bank(p) + blk, :].rearrange("p (q t) -> p q t", q=2),
                                     vcol("shift_rkv", n + RB), vcol("shift_rkv", n + (6 * RB + RB)))
                    if blk == 0:
                        chain(ins)
                ins.then_inc(bank_free, 1)

            def shift_lora(i, p):
                ph = PH["in_lora"]
                if p == 0:
                    for blk, name in enumerate(("shift_wd", "shift_ad")):
                        dve.wait_ge(shift_ready, 2 * RB + blk + 1)
                        ins = outer_taps(wdad[0:LORA, blk, :, :], ps[0:LORA, blk, :].rearrange("p (q t) -> p q t", q=2),
                                         vcol(name, 0, rows=LORA), vcol(name, 2, rows=LORA))
                        if blk == 0:
                            chain(ins)
                    ins.then_inc(bank_free, 1)
                    return
                summed(ph, i, p, px[:, :, :]).then_inc(bank_free, 1)
                dve.wait_ge(bank_free, ph.pair(i, p) + (1 + BANK_CREDIT))
                for blk in range(2):
                    dve.wait_ge(shift_ready, 2 * RB + 2 + blk + 1)
                    chain(outer_taps(gd[:, blk:blk + 1, :], px[:, blk:blk + 1, :], vcol("shift_gd", blk), vcol("shift_gd", 4 + blk)))

            def shift_r(i, p):
                ph = PH["in_r"]
                summed(ph, i, p, px[:, :, :]).then_inc(bank_free, 1)
                dve.wait_ge(bank_free, ph.pair(i, p) + (1 + BANK_CREDIT))
                for blk in range(2):
                    n = i * 4 + (2 * p + blk)
                    dve.wait_ge(shift_ready, n + (2 * RB + 4 + 1))
                    chain(outer_taps(r[:, ds(n, 1), :], px[:, blk:blk + 1, :], vcol("shift_rkv", n), vcol("shift_rkv", n + 6 * RB)))

            gemm(PH["in_kv"], shift_both, per_trip=6)
            gemm(PH["in_lora"], shift_lora, per_trip=7)
            gemm(PH["in_r"], shift_r, per_trip=8)
            gemm(PH["in_rest"], lambda i, p: summed(PH["in_rest"], i, p, proj[:, ds(i * 4 + 2 * p, 2), :]).then_inc(bank_free, 1))
            chain(dve.tensor_tensor(proj[:, 0:4, :], proj[:, 0:4, :], proj[:, 4:8, :], ALU.mult))
            dve.wait_ge(x_spilled, 16)
            dve.sem_inc(conv_mid, 1)
            for blk in range(4):
                dve.wait_ge(conv_mid, blk + 2)
                dest, src = (x.rearrange("p (n t) -> p n t", t=GRID_W) for x in (ymix[:, RB + blk, :], proj[:, blk, :]))
                chain(outer_taps(dest, src, vcol("conv_w", blk), vcol("conv_w", 8 + blk)))
                chain(dve.tensor_tensor(ymix[:, RB + blk, :], ymix[:, RB + blk, :], proj[:, 8 + blk, :], ALU.mult))
            for n in range(2):
                dve.wait_ge(four_done, n + 1)
                chain(dve.tensor_copy(ymix[:, RB + 4 + 2 * n:RB + 6 + 2 * n, :], ps[:, n, :].rearrange("p (a t) -> p a t", a=2)))
            dve.sem_inc(mix_done, 1)

            def front(b, q, stage):
                def done(d, ins, name):
                    front_dve[d].done(ins, (q, name))

                def own(d, name):
                    front_dve[d].wait(dve, (q, name), b)

                def products(name, x, e, dst, after):
                    for d in range(2):
                        front_act[d].wait(dve, (q, after), b)
                        for h in range(2):
                            hs = slice(h * HEAD, (h + 1) * HEAD)
                            done(d, dve.tensor_tensor(dst[d][hs, :, hs], chunks_of(x[d][hs, :]), chunks_of(e[d][hs, :]), ALU.mult), f"{name}{h}")

                first, both = q == 0, range(2)
                kkq = kk[:, q * T:(q + 1) * T]
                row = lambda x: x.rearrange("p a t -> p (a t)")
                alpha = lambda: products("a", [kkq, kkq], ex, bdA[q], "eex")
                beta = lambda: products("b", av, en, bdB[q], "en")
                kappa = lambda: products("k", kd, en, bdK[q], "en")

                def rate_key():
                    for d in both:
                        done(d, dve.tensor_tensor(av[d][:, :], av[d][:, :], kkq, ALU.mult), "ba")

                if stage == 1:
                    if first:
                        done(0, dve.tensor_scalar(kq[:, :], kv[:, ds(b, 1), :, :].rearrange("p a q t -> p (a q t)"), vcol("k_k", b), None, ALU.mult), "kq")
                    for d in both:
                        front_act[d].wait(dve, (q, "sg"), b)
                        done(d, dve.tensor_scalar(lw[d][:, :], lw[d][:, :], DECAY_SCALE, None, ALU.mult), "lw")
                    for d in both:
                        own(d, "lw")
                        way = slice(None, None, 1 if d == 0 else -1)
                        done(d, dve.tensor_tensor_scan(L[d][:, way], inside, lw[d][:, way], 0.0, ALU.mult, ALU.add), "L")
                    for d in both:
                        own(d, "L")
                        done(d, dve.tensor_tensor(ex[d][:, :], L[d][:, :], lw[d][:, :], ALU.subtract), "Lx")
                if stage == 2:
                    if first:
                        front_pe[0].wait(dve, (q, "kk"), b)
                        done(0, dve.tensor_scalar(kn[:, :], ps[:, 1, :], KK_EPS * KK_EPS, None, ALU.max), "kv")
                    for d in both:
                        front_act[d].wait(dve, (q, "sa"), b)
                        done(d, dve.tensor_scalar(kd[d][:, :], av[d][:, :], vcol("k_a", b), oka[:, ds(b, 1)], ALU.mult, ALU.add), "kf")
                    for d in both:
                        own(d, "kf")
                        done(d, dve.tensor_tensor(kd[d][:, :], kd[d][:, :], row(kv[:, ds(b, 1), q, :]), ALU.mult), "kd")
                    if not first:
                        rate_key()
                    for d in both:
                        own(d, "kd" if first else "ba")
                step = lambda ins, name: (done(0, ins, name), own(0, name))
                if stage == 3:
                    if first:
                        front_act[0].wait(dve, (q, "ksqrt"), b)
                        done(0, dve.reciprocal(kk[:, 0:T], kk[:, 0:T]), "n0")
                    if not first:
                        done(1, dve.tensor_tensor(kn[:, 0:T], kd[0][:, :], kd[1][:, :], ALU.add), "rk0")
                        own(1, "rk0")
                        done(1, dve.scalar_tensor_tensor(out=kn[:, 0:T], in0=kn[:, 0:T], scalar=vcol("r_k", b), in1=row(r[:, ds(b, 1), :]),
                                                         op0=ALU.mult, op1=ALU.mult), "rk1")
                    kappa()
                    if not first:
                        alpha()
                if stage == 4:
                    if first:
                        step(dve.reciprocal(kk[:, T:2 * T], kk[:, T:2 * T]), "n1")
                        step(dve.tensor_tensor(knt[:, :], kk[:, :], kk[:, :], ALU.mult), "n2")
                        step(dve.tensor_tensor(knt[:, :], knt[:, :], kn[:, :], ALU.mult), "n3")
                    else:
                        beta()
                        for d in both:
                            front_act[d].wait(dve, (q, "ep"), b)
                            done(d, dve.tensor_tensor(bdA[q][d][:, :, P:P + C], chunks_of(row(r[:, ds(b, 1), :])), chunks_of(L[d][:, :]), ALU.mult), "rho")
                if stage == 5:
                    if first:
                        step(dve.tensor_scalar(knt[:, :], knt[:, :], -0.5, 1.5, ALU.mult, ALU.add), "n4")
                        step(dve.tensor_tensor(kk[:, :], kk[:, :], knt[:, :], ALU.mult), "n5")
                        step(dve.tensor_tensor(kk[:, :], kk[:, :], kq[:, :], ALU.mult), "kk")
                        rate_key()
                        alpha()
                        own(0, "ba")
                        own(1, "ba")
                        beta()
                    else:
                        own(0, "rho")
                        own(1, "rho")
                        front_pe[1].wait(dve, (q, "rk"), b)
                        done(1, dve.tensor_tensor(row(r[:, ds(b, 1), :]), ps[:, 5, 0:T], row(kv[:, ds(b + RB, 1), q, :]), ALU.mult), "bonus")

            def unit(b, q, ahead=True):
                def done(d, ins, name):
                    scan_dve[d].done(ins, (q, name))

                def own(d, name):
                    scan_dve[d].wait(dve, (q, name), b)

                w = P + C * q
                bank = lambda d, n: ps[:, 4 * d + n, :].rearrange("p (c n) -> p c n", c=NC)
                for d in range(2):
                    if q == 0:
                        done(d, dve.memset(S[d][:, :], 0.0), "S")
                    else:
                        front_pe[d].wait(dve, (q, "G1"), b)
                        done(d, dve.tensor_tensor(in_pairs(tokBQ[d][:, :, P:P + C]), two_banks(4 * d, w, P, C), over_banks(upto[d]), ALU.mult), "Q")
                for d in range(2):
                    scan_pe[d].wait(dve, (q, "G2"), b)
                    if q:
                        done(d, dve.tensor_tensor(in_pairs(RT[d][:, :, :]), two_banks(4 * d + 2, w, P, C), over_banks(upto[d]), ALU.mult), "R")
                    done(d, dve.tensor_tensor(in_pairs(MT[d][:, :, :]), two_banks(4 * d + 2, w, 0, P), over_banks(strict[d]), ALU.mult), "M")
                for d in range(2):
                    scan_pe[d].wait(dve, (q, "tK"), b)
                    done(d, dve.tensor_copy(tokK[d][:, :, :], bank(d, 2)), "oK")
                    if d == 0:
                        scan_pe[d].wait(dve, (q, "tV"), b)
                        done(d, dve.tensor_copy(tokV[:, :, :], bank(d, 3)), "oV")
                for d in range(2):
                    scan_pool[d].wait(dve, (q, "m0"), b)
                    scan_pe[d].wait(dve, (q, "L0"), b)
                    done(d, dve.tensor_tensor(XT[q][d][:, :, :], over_chunks(ident), ULa[d][:, :, :], ALU.subtract), "T0")
                    done(d, dve.tensor_tensor(XY[d][:, :, 0, :], over_chunks(ident), bank(d, 1), ALU.subtract), "X0")
                for l in FRONT:
                    for d in range(2):
                        if l < LEVELS - 1:
                            scan_pe[d].wait(dve, (q, f"X{l}"), b)
                            done(d, dve.tensor_tensor(XY[d][:, :, 0, :], XY[d][:, :, 0, :], bank(d, 3), ALU.subtract), f"X{l}")
                        scan_pe[d].wait(dve, (q, f"T{l}"), b)
                        done(d, dve.tensor_tensor(XT[q][d][:, :, :], XT[q][d][:, :, :], bank(d, 0), ALU.subtract), f"T{l}")
                    if ahead:
                        front(*following(b, q), l)
                y = ymix[:, ds(b, 1), :].rearrange("p a t -> p (a t)")
                for d in range(2):
                    scan_pe[d].wait(dve, (q, "A"), b)
                    done(d, dve.tensor_tensor(in_pairs(AT[d][:, :, :]), two_banks(4 * d, w, 0, P), over_banks(ident), ALU.add), "AT")
                    if q:
                        rho = in_pairs(bdA[q][d][:, :, P:P + C])
                        done(d, dve.tensor_tensor(rho, two_banks(4 * d, w, P, C), rho, ALU.add), "rho2")
                    scan_pe[d].wait(dve, (q, "B"), b)
                    done(d, dve.tensor_tensor(BM[q][d][:, :, :], bank(d, 2),
                                              pc[q][d][:, :].rearrange("p (c n) -> p c n", n=1).broadcast_to([P, NC, P]), ALU.mult), "Bm")
                    if q and d == 0:
                        done(d, dve.tensor_copy(y, ps[:, 3, 0:T]), "Y0")
                    elif q:
                        own(0, "Y0")
                        done(d, dve.tensor_tensor(y, ps[:, 7, 0:T], y, ALU.add), "Y0")
                for n in range(NC - q):
                    for d in range(2):
                        c = in_order(d)[n]
                        scan_pe[d].wait(dve, (q, f"st{n}"), b)
                        own(d, f"s{n - 1}" if n else "Bm")
                        done(d, dve.scalar_tensor_tensor(out=S[d][:, :], in0=ps[:, 4 * d + 2, c * P:(c + 1) * P], scalar=pc[q][d][:, c:c + 1],
                                                         in1=BM[q][d][:, c, :], op0=ALU.mult, op1=ALU.add), f"s{n}")
                if q:
                    for d in range(2):
                        scan_pe[d].wait(dve, (q, f"st{NC - 1}"), b)
                        scan_dve[1 - d].wait(dve, (q, "y" if d else "Y0"), b)
                        done(d, dve.tensor_tensor(y, ps[:, 4 * d + 3, T:2 * T], y, ALU.add), "y")

            chain(dve.tensor_scalar(oka, vcol("k_a", 0, RB), -1.0, 1.0, ALU.mult, ALU.add))
            dve.wait_ge(kscan_in, 16)
            dve.wait_ge(bd_clear, 13)
            for stage in FRONT:
                front(0, 0, stage)
            with dve.Fori(0, RB - 1) as b:
                unit(b, 0)
                unit(b, 1)
            unit(RB - 1, 0)
            unit(RB - 1, 1, ahead=False)
            with dve.Fori(0, RB // 2) as i:
                y, bonus, g = (x[:, ds(i * 2, 2), :].rearrange("p a t -> p (a t)") for x in (ymix, r, gate))
                step = lambda ins, name: (gnd.done(ins, name), gnd.wait(dve, name, i))
                gnp.wait(dve, "mean", i)
                gnd.done(dve.scalar_tensor_tensor(out=yc[:, :], in0=ps[:, 4, :], scalar=-1.0 / HEAD, in1=y, op0=ALU.mult, op1=ALU.add), "c")
                gnp.wait(dve, "var", i)
                gnd.done(dve.tensor_scalar(yv[:, :], ps[:, 5, :], 1.0 / HEAD, GN_EPS, ALU.mult, ALU.add), "v")
                gna.wait(dve, "sqrt", i)
                step(dve.reciprocal(yn[:, :], yn[:, :]), "n0")
                step(dve.tensor_tensor(ysq[:, :], yn[:, :], yn[:, :], ALU.mult), "n1")
                step(dve.tensor_tensor(ysq[:, :], ysq[:, :], yv[:, :], ALU.mult), "n2")
                step(dve.tensor_scalar(ysq[:, :], ysq[:, :], -0.5, 1.5, ALU.mult, ALU.add), "n3")
                step(dve.tensor_tensor(yn[:, :], yn[:, :], ysq[:, :], ALU.mult), "n4")
                gnd.done(dve.tensor_tensor(yn[:, :], yn[:, :], yc[:, :], ALU.mult), "yn")
                gna.wait(dve, "w1", i)
                step(dve.tensor_tensor(yn[:, :], yn[:, :], bonus, ALU.add), "b")
                dve.wait_ge(gate_out, RB // 2)
                step(dve.tensor_tensor(y, yn[:, :], g, ALU.mult), "g")
            dve.sem_inc(ymix_done, 1)
            for n in range(4):
                dve.wait_ge(yhi, n + 1)
                dve.tensor_tensor(mov[:, 4 * n:4 * n + 4, 1, :], ymix[:, 4 * n:4 * n + 4, :], mov[:, 4 * n:4 * n + 4, 0, :].bitcast(F32), ALU.subtract)\
                   .then_inc(ylo, 1)
            def residual(ph, part):
                def evacuate(i, p):
                    summed(ph, i, p, px[:, :, :]).then_inc(bank_free, 1)
                    dve.wait_ge(bank_free, ph.pair(i, p) + (1 + BANK_CREDIT))
                    n = i * (2 * ph.pairs) + 2 * p
                    if part is None:
                        chain(dve.tensor_tensor(xT[:, ds(n, 2), :], px[:, :, :], xT[:, ds(n, 2), :], ALU.add))
                        return
                    for blk in range(2):
                        ins = dve.scalar_tensor_tensor(out=xT[:, ds(n + blk, 1), :], in0=px[:, blk:blk + 1, :], scalar=mod[:, part, 0, ds(n + blk, 1)],
                                                       in1=xT[:, ds(n + blk, 1), :], op0=ALU.mult, op1=ALU.add)
                        mark = chain.mark(ins)
                    chain.wait(mark)
                return evacuate, ph.pairs * (1 if part is None else 2)

            def add_residual(name, part):
                if PH[name] is order[-1]:
                    last_residual(PH[name])
                else:
                    gemm(PH[name], *residual(PH[name], part))
                dve.sem_inc(x_done, 1)

            def last_residual(ph):
                def evacuate(i, p):
                    summed(ph, i, p, px[:, :, :]).then_inc(bank_free, 1)
                    dve.wait_ge(bank_free, ph.pair(i, p) + (1 + BANK_CREDIT))
                    n = i * (2 * ph.pairs) + 2 * p
                    dve.tensor_tensor(xT[:, ds(n, 2), :], px[:, :, :], xT[:, ds(n, 2), :], ALU.add).then_inc(res_done, 1)
                    dve.wait_ge(res_done, i * ph.pairs + (p + 1))
                gemm(ph, evacuate)

            def gated(e, ph):
                before = e * PH["ffn"].trips
                def evacuate(i, p):
                    if p == 0:
                        summed(ph, i, p, gbuf[:, :, :]).then_inc(bank_free, 1)
                        return
                    dve.wait_ge(ffn_lo, i + (before + 1))
                    summed(ph, i, p, ubuf[:, :, :]).then_inc(bank_free, 1)
                    dve.wait_ge(bank_free, ph.pair(i, p) + (1 + BANK_CREDIT))
                    dve.wait_ge(ffn_s, i + (before + 1))
                    dve.tensor_tensor(ubuf[:, :, :], sbuf[:, :, :], ubuf[:, :, :], ALU.mult).then_inc(ffn_h, 1)
                    dve.wait_ge(ffn_hi, i + (before + 1))
                    dve.tensor_tensor(hid[:, ds(i * 2, 2), 1, :], ubuf[:, :, :], hid[:, ds(i * 2, 2), 0, :].bitcast(F32), ALU.subtract)\
                       .then_inc(ffn_lo, 1)
                return evacuate

            def norm_and_ffn(e, stat, norm, g, shift, suffix, gate_part):
                variance(stat, T)
                normed(norm, lambda k: xT[:, ds(k, 1), :], g, rstd[:, 0, :], shift,
                       lambda k: mov[:, ds(k, 1), 0, :], lambda k: mov[:, ds(k, 1), 1, :])
                gemm(PH["ffn" + suffix], gated(e, PH["ffn" + suffix]))
                add_residual("down" + suffix, gate_part)

            dve.sem_inc(ffn_lo, 1)
            dve.wait_ge(x_back, 16)
            add_residual("out", 2)
            norm_and_ffn(0, 1, 2, lambda k: gain[:, 2, ds(k, 1)], lambda k: mod[:, 3, 0, ds(k, 1)], "", 5)

            def scale_residual(stat, name, n0):
                variance(stat, T)
                for k in range(KB):
                    dve.scalar_tensor_tensor(out=xT[:, k, :], in0=xT[:, k, :], scalar=vcol(name, k), in1=rstd[:, 0, :], op0=ALU.mult, op1=ALU.mult)\
                       .then_inc(x_scaled, 1)
                dve.wait_ge(x_scaled, n0 + KB)

            scale_residual(2, "norm_final", 0)
            dve.sem_inc(x_done, 1)
            variance(3, T)
            normed(3, lambda k: xT[:, ds(k, 1), :], lambda k: vcol("ln1_w_2", k), rstd[:, 0, :], None,
                   lambda k: mov[:, ds(k, 1), 0, :], lambda k: mov[:, ds(k, 1), 1, :])
            gemm(PH["in_2"], lambda i, p: summed(PH["in_2"], i, p, p2[:, ds(i * 4 + 2 * p, 2), :]).then_inc(bank_free, 1))
            dve.wait_ge(bank_free, IN2_OUT)
            dve.wait_ge(lam_exp, 2)
            lw1, e1, w1, w2, s1 = (lcol[:, n, :] for n in range(1, 6))
            chain(dve.tensor_scalar(w1, e1, 2.0, None, ALU.add))
            chain(dve.reciprocal(w1, w1))
            chain(dve.tensor_tensor(w1, w1, e1, ALU.mult))
            chain(dve.tensor_tensor(w2, w1, w1, ALU.mult))
            chain(dve.tensor_scalar(s1, w2, 1.0 / 17, None, ALU.mult))
            for n in range(15, 1, -2):
                chain(dve.scalar_tensor_tensor(out=s1, in0=s1, scalar=1.0 / n, in1=w2, op0=ALU.add, op1=ALU.mult))
            chain(dve.scalar_tensor_tensor(out=s1, in0=s1, scalar=1.0, in1=w1, op0=ALU.add, op1=ALU.mult))
            chain(dve.tensor_scalar(e1, vcol("lru_lambda_2", 0, RB), 0.0, LRU_C / 2, ALU.min, ALU.mult))
            dve.scalar_tensor_tensor(out=lw1, in0=s1, scalar=-LRU_C, in1=e1, op0=ALU.mult, op1=ALU.add).then_inc(lam_ready, 1)
            marks = {}
            for tap in (2, 1, 0):
                lag = 3 - tap
                for n in range(RB):
                    if tap == 2:
                        dve.wait_ge(lru_mid, n + 1)
                    else:
                        chain.wait(marks[n])
                    ins = dve.scalar_tensor_tensor(out=lu[:, n, lag:T], in0=p2[:, LX + n, 0:T - lag], scalar=vcol("conv_w_2", tap * RB + n),
                                                   in1=lu[:, n, lag:T], op0=ALU.mult, op1=ALU.add)
                    if tap:
                        marks[n] = chain.mark(ins)
                    else:
                        ins.then_inc(lru_u, 1)
            dve.wait_ge(lru_t, RB)
            chain(dve.tensor_scalar(linv[:, :, :], la[:, :, :], -1.0, 1.0, ALU.mult, ALU.add))
            chain(dve.reciprocal(linv[:, :, :], linv[:, :, :]))
            dve.wait_ge(lru_sq, 1)
            dve.wait_ge(lru_iu, 1)
            m1 = chain.mark(dve.scalar_tensor_tensor(out=la[:, :, :], in0=la[:, :, :], scalar=1.0, in1=linv[:, :, :], op0=ALU.add, op1=ALU.mult))
            chain(dve.tensor_tensor(linv[:, :, :], linv[:, :, :], p2[:, LX:LX + RB, :], ALU.mult))
            chain(dve.tensor_tensor(lb[:, :, :], lb[:, :, :], linv[:, :, :], ALU.mult))
            for n in range(RB):
                m1 = chain.mark(dve.tensor_tensor_scan(lu[:, n, :], la[:, n, :], lb[:, n, :], 0.0, ALU.mult, ALU.add))
            chain.wait(m1)
            dve.wait_ge(lru_gelu, 1)
            chain(dve.tensor_tensor(p2[:, LX:LX + RB, :], lu[:, :, :], p2[:, LG:LG + RB, :], ALU.mult))
            def head(h, first=False):
                retp.wait(dve, "sw", h)
                if not first:
                    retp.wait(dve, "sc", h - 1)
                retd.done(dve.tensor_tensor(rqk[:, :, :], ps[:, 0, :].rearrange("p (a t) -> p a t", a=2), both(rsin), ALU.mult), "qs")
                retd.wait(dve, "qs", h)
                retg.wait(dve, "qc", h)
                retd.done(dve.tensor_tensor(rqk[:, :, :], rqk[:, :, :], rqc[:, :, :], ALU.add), "qr")
                retp.wait(dve, "sc", h)
                if not first:
                    retp.wait(dve, "o", h - 1)
                retd.done(dve.tensor_tensor(rp[:, :], ps[:, 2, 0:T + P], kret[:, ds(h * (T + P) + (2 * T + P), T + P)], ALU.mult), "pr")

            dve.wait_ge(kret_in, 16)
            head(0, True)
            with dve.Fori(0, RET_HEADS - 1) as i:
                head(i + 1)
            dve.wait_ge(ret_silu, 1)
            with dve.Fori(0, RET_HEADS // 2) as i:
                o = ro[:, ds(i * 2, 2), :].rearrange("p a t -> p (a t)")
                step = lambda ins, name: (rnd.done(ins, name), rnd.wait(dve, name, i))
                rnp.wait(dve, "mean", i)
                rnd.done(dve.scalar_tensor_tensor(out=oc[:, :], in0=ps[:, 4, :], scalar=-1.0 / P, in1=o, op0=ALU.mult, op1=ALU.add), "c")
                rnp.wait(dve, "var", i)
                rnd.done(dve.tensor_scalar(ov[:, :], ps[:, 5, :], 1.0 / P, RMS_EPS, ALU.mult, ALU.add), "v")
                rna.wait(dve, "sqrt", i)
                step(dve.reciprocal(on[:, :], on[:, :]), "n0")
                step(dve.tensor_tensor(osq[:, :], on[:, :], on[:, :], ALU.mult), "n1")
                step(dve.tensor_tensor(osq[:, :], osq[:, :], ov[:, :], ALU.mult), "n2")
                step(dve.tensor_scalar(osq[:, :], osq[:, :], -0.5, 1.5, ALU.mult, ALU.add), "n3")
                step(dve.tensor_tensor(on[:, :], on[:, :], osq[:, :], ALU.mult), "n4")
                step(dve.tensor_tensor(on[:, :], on[:, :], oc[:, :], ALU.mult), "yn")
                for blk in range(2):
                    n = i * 2 + blk
                    half = slice(blk * T, (blk + 1) * T)
                    rnd.done(dve.tensor_scalar(on[:, half], on[:, half], vcol("ret_gn_w_2", n), None, ALU.mult), f"w{blk}")
                rnd.wait(dve, "w1", i)
                step(dve.tensor_tensor(p2[:, ds(i * 2 + RB, 2), :].rearrange("p a t -> p (a t)"), on[:, :],
                                       p2[:, ds(i * 2 + RG, 2), :].rearrange("p a t -> p (a t)"), ALU.mult), "g")
            dve.sem_inc(y2_done, 1)
            for n in range(4):
                dve.wait_ge(y2_hi, n + 1)
                dve.tensor_tensor(mov[:, 4 * n:4 * n + 4, 1, :], p2[:, 4 * n:4 * n + 4, :], mov[:, 4 * n:4 * n + 4, 0, :].bitcast(F32), ALU.subtract)\
                   .then_inc(y2_lo, 1)
            add_residual("out_2", None)
            norm_and_ffn(1, 4, 4, lambda k: vcol("ln2_w_2", k), None, "_2", None)
            scale_residual(5, "final_norm_w_2", KB)
            for n in range(1, 8, 2):
                dve.wait_ge(row_turned, n + 1)
                dve.tensor_copy(orow[:, n % 2, (n // 2) * BANK:(n // 2 + 1) * BANK], ps[:, n, :]).then_inc(row_dve, 1)

        @block.tensor
        def _(pe):
            pe.sem_inc(split_free, SPLIT_CREDIT)

            def gemm(ph, product):
                def trip(i):
                    for p in range(ph.pairs):
                        pe.wait_ge(bank_free, ph.pair(i, p) + 1)
                        for c in range(ph.per_pair):
                            j = p * ph.per_pair + c
                            pe.wait_ge(lo_ready, ph.chunk(i, j) + (1 + RING))
                            for kk in range(CK):
                                k = c * CK + kk
                                mm = product(p, ph.slot(j), kk, k, k == 0, k == ph.rows - 1)
                            mm.then_inc(split_free, 1)
                    after(i) if after else None
                after = AFTER.get(ph.name)
                loop(pe, ph, trip)

            def on_x(ph, moving):
                def product(p, s, kk, k, first, last):
                    for blk in range(2):
                        b, w = ph.bank(p) + blk, slice(blk * P, (blk + 1) * P)
                        pe.matmul(ps[:, b, :], hi[:, s, kk, w], moving(k, None), start=first, stop=False)
                        mm = pe.matmul(ps[:, b, 0:T], lo[:, s, kk, w], moving(k, 0), start=False, stop=last)
                    return mm
                return product

            def on_both(ph, widths):
                def product(p, s, kk, k, first, last):
                    for blk in range(2):
                        b, w = ph.bank(p) + blk, slice(blk * widths, (blk + 1) * widths)
                        pe.matmul(ps[0:widths, b, :], hi[:, s, kk, w], mov1[:, k, 0, :, :], start=first, stop=False)
                        pe.matmul(ps[0:widths, b, :], hi[:, s, kk, w], mov1[:, k, 1, :, :], start=False, stop=False)
                        mm = pe.matmul(ps[0:widths, b, :], lo[:, s, kk, w], mov1[:, k, 0, :, :], start=False, stop=last)
                    return mm
                return product

            def sums_of_squares(n, width):
                for k in range(KB):
                    pe.wait_ge(sq_ready, n * KB + k + 1)
                    pe.matmul(ps[:, 7, 0:width], ones, sq[:, k % 2, 0:width], start=(k == 0), stop=(k == KB - 1))\
                      .then_inc(sq_used, 1)

            AFTER = {}
            pe.wait_ge(const_in, 16)
            pe.wait_ge(vec_in, 16 * VEC_DMAS)
            for t in range(4):
                mm = pe.transpose(ps[:, 0, t * P:(t + 1) * P], vrow[:, t, :], ident)
            mm.then_inc(vec_turned, 1)
            pe.wait_ge(row_in, 32)
            for k in range(KB + 1):
                if k < KB:
                    if k >= 4:
                        pe.wait_ge(sq_ready, k - 3)
                        pe.wait_ge(x_out, k - 3)
                    for a, src in enumerate((crow, xrow)):
                        for h in range(2):
                            mm = pe.transpose(ps[:, 1 + k % 4, (2 * a + h) * P:(2 * a + h + 1) * P],
                                              src[:, h, k * P:(k + 1) * P], ident)
                    mm.then_inc(turned, 1)
                if k >= 1:
                    pe.wait_ge(sq_ready, k)
                    pe.matmul(ps[:, 7, :], ones, sq[:, (k - 1) % 2, :], start=(k == 1), stop=(k == KB)).then_inc(sq_used, 1)
            pe.wait_ge(c4_ready, 2)
            pe.wait_ge(vec_ready, 1)
            pe.wait_ge(x_out, KB)
            pe.wait_ge(ctx_out, KB)

            def mod_rows(p, s, kk, k, first, last):
                b = PH["mod"].bank(p)
                pe.matmul(ps[:, b, 0:CN], c4[:, k, :], hi[:, s, kk, :], start=first, stop=False)
                return pe.matmul(ps[:, b, 0:CN], c4[:, k, :], lo[:, s, kk, :], start=False, stop=last)

            def mod_columns(i):
                pe.wait_ge(bank_free, PH["mod"].pair(i, PH["mod"].pairs - 1) + (1 + BANK_CREDIT))
                for k in range(KB):
                    mm = pe.matmul(ps[:, 5, 2 * k:2 * k + 2], mrow[:, k * P:(k + 1) * P], sel[0:4, 0:2], start=True, stop=True)
                mm.then_inc(mcol_ready, 1)
            AFTER["mod"] = mod_columns
            gemm(PH["mod"], mod_rows)
            pe.wait_ge(mov_ready, 2 * KB)
            gemm(PH["in_kv"], on_both(PH["in_kv"], P))
            lora_both, lora_x = on_both(PH["in_lora"], LORA), on_x(PH["in_lora"], lambda k, h: mov1[:, k, :, 1, :] if h is None else mov1[:, k, h, 1, :])
            gemm(PH["in_lora"], lambda p, *a: (lora_both, lora_x)[p](p, *a))
            for name in ("in_r", "in_rest"):
                gemm(PH[name], on_x(PH[name], lambda k, h: mov1[:, k, :, 1, :] if h is None else mov1[:, k, h, 1, :]))
            pe.wait_ge(bank_free, REST_OUT)
            pe.wait_ge(four_in, 16)
            for n in range(4):
                h = n // 2
                for blk in range(2 * (n % 2), 2 * (n % 2) + 2):
                    mm = pe.matmul(ps[:, 4 + n, (blk % 2) * T:(blk % 2 + 1) * T], proj[:, 12 + blk, h * P:(h + 1) * P], kfour[:, 0, :],
                                   start=True, stop=True)
                mm.then_inc(uf_turned, 1)
            pe.wait_ge(uf_ready, 4)
            for blk in range(4):
                for n, (h, cs) in enumerate((h, cs) for h in range(2) for cs in range(2)):
                    mm = pe.matmul(ps[:, blk // 2, (blk % 2) * T:(blk % 2 + 1) * T], uf[:, h, blk, cs, :], kfour[:, 1 + 2 * h + cs, :],
                                   start=(n == 0), stop=(n == 3))
                if blk % 2:
                    mm.then_inc(four_done, 1)

            def each(sem_of, d, name, bank, lhs, rhs, n=P, paired=False):
                for c in range(NC):
                    if paired:
                        o = ps[:, 4 * d + bank + c // 2, (c % 2) * n:(c % 2 + 1) * n]
                    else:
                        o = ps[:, 4 * d + bank, c * n:(c + 1) * n]
                    mm = lhs(c, o) if rhs is None else pe.matmul(o, lhs(c), rhs(c), start=True, stop=True)
                if name:
                    sem_of[d].done(mm, name)

            def two(d, name, bank, lhs1, rhs1, lhs2, rhs2, n):
                for c in range(NC):
                    o = ps[:, 4 * d + bank, c * n:(c + 1) * n]
                    pe.matmul(o, lhs1(c), rhs1(c), start=True, stop=False)
                    mm = pe.matmul(o, lhs2(c), rhs2(c), start=False, stop=True)
                if name:
                    scan_pe[d].done(mm, name)

            def front(b, q, stage):
                first = q == 0
                if stage == 1:
                    pe.wait_ge(decw_in, b * 32 + 32)
                    for d in range(2):
                        for n in range(2):
                            mm = pe.matmul(ps[:, 4 * d + 1, n * T:(n + 1) * T], decw[0:LORA, 2 * n + d, :], wdad[0:LORA, n, q, :], start=True, stop=True)
                        front_pe[d].done(mm, (q, "zz"))
                if stage == 2 and first:
                    front_act[0].wait(pe, (q, "ksq"), b)
                    front_pe[0].done(pe.matmul(ps[:, 1, :], blk64, kn[:, :], start=True, stop=True), (q, "kk"))
                if stage == 5 and not first:
                    front_dve[1].wait(pe, (q, "rk1"), b)
                    front_act[1].wait(pe, (q, "sa"), b)
                    front_pe[1].done(pe.matmul(ps[:, 5, 0:T], blk64, kn[:, 0:T], start=True, stop=True), (q, "rk"))

            def front_out(b, q):
                for d in range(2):
                    front_act[d].wait(pe, (q, "sa"), b)
                if q == 0:
                    front_dve[0].wait(pe, (q, "kv"), b)
                else:
                    front_dve[1].wait(pe, (q, "bonus"), b)

            def gram(b, q, d):
                w = P + C * q
                front_dve[d].wait(pe, (q, "rho" if q else "b1"), b)
                each(front_pe, d, (q, "G1"), 0, lambda c: bdB[q][d][:, c, :], lambda c: bdA[q][d][:, c, 0:w], w, paired=True)

            def unit(b, q, ahead=True):
                w = P + C * q
                if q:
                    for d in range(2):
                        scan_dve[d].wait(pe, (0, f"s{NC - 1}"), b)
                for d in range(2):
                    each(scan_pe, d, (q, "G2"), 2, lambda c: bdK[q][d][:, c, :], lambda c: bdA[q][d][:, c, 0:w], w, paired=True)
                for d in range(2):
                    act, dve = scan_act[d], scan_dve[d]
                    act.wait(pe, (q, "U"), b)
                    each(scan_pe, d, (q, "tA"), 0, lambda c, o: pe.transpose(o, bdA[q][d][:, c, 0:P], ident), None)
                    each(scan_pe, d, (q, "tB"), 1, lambda c, o: pe.transpose(o, bdB[q][d][:, c, :], ident), None)
                    dve.wait(pe, (q, "M"), b)
                    each(scan_pe, d, (q, "tK"), 2, lambda c, o: pe.transpose(o, bdK[q][d][:, c, :], ident), None)
                    if d == 0:
                        front_act[0].wait(pe, (q, "bv1"), b)
                        each(scan_pe, d, (q, "tV"), 3, lambda c, o: pe.transpose(o, bdV[:, c, :], ident), None)
                for d in range(2):
                    scan_dve[0].wait(pe, (q, "oV"), b)
                    scan_act[d].wait(pe, (q, "oB"), b)
                    each(scan_pe, d, (q, "MV"), 0, lambda c: MT[d][:, c, :], lambda c: tokV[:, c, :])
                    scan_pool[d].wait(pe, (q, "m0"), b)
                    each(scan_pe, d, (q, "L0"), 1, lambda c, o: pe.transpose(o, ULa[d][:, c, :], ident), None)
                for l in FRONT:
                    lev = (ULa, MT)[l % 2]
                    for d in range(2):
                        scan_pool[d].wait(pe, (q, f"m{l}"), b)
                        scan_dve[d].wait(pe, (q, f"T{l - 1}" if l > 1 else "X0"), b)
                        each(scan_pe, d, (q, f"Y{l}"), 2, lambda c: lev[d][:, c, :], lambda c: XY[d][:, c, 0, :])
                    if ahead:
                        front(*following(b, q), l)
                    for d in range(2):
                        scan_act[d].wait(pe, (q, f"Yb{l}"), b)
                        if l == 1:
                            scan_act[d].wait(pe, (q, "oMV"), b)
                        if l < LEVELS - 1:
                            each(scan_pe, d, (q, f"X{l}"), 3, lambda c: XT[q][d][:, c, :], lambda c: XY[d][:, c, 1, :])
                        each(scan_pe, d, (q, f"T{l}"), 0, lambda c: XY[d][:, c, 1, :], lambda c: XT[q][d][:, c, :])
                for d in range(2):
                    scan_dve[d].wait(pe, (q, f"T{LEVELS - 1}"), b)
                    each(scan_pe, d, (q, "Z"), 2, lambda c: XT[q][d][:, c, :], lambda c: tokR[d][:, c, :, :], 2 * P, paired=True)
                if ahead:
                    front_out(*following(b, q))
                for d in range(2):
                    scan_act[d].wait(pe, (q, "Z"), b)
                    each(scan_pe, d, (q, "A"), 0, lambda c: XY[d][:, c, 0, :], lambda c: tokBQ[d][:, c, 0:w], w, paired=True)
                    two(d, None if q else (q, "B"), 2, lambda c: tokK[d][:, c, :], lambda c: tokV[:, c, :],
                        lambda c: tokBQ[d][:, c, 0:P], lambda c: XY[d][:, c, 1, :], P)
                    if q:
                        two(d, (q, "B"), 3, lambda c: tokV[:, c, :], lambda c: RT[d][:, c, :],
                            lambda c: XY[d][:, c, 1, :], lambda c: tokBQ[d][:, c, P:P + C], C)
                for n in range(NC):
                    for d in range(2):
                        c = in_order(d)[n]
                        scan_dve[d].wait(pe, (q, f"s{n - 1}" if n else "Y0" if q else "Bm"), b)
                        if q:
                            mm = pe.matmul(ps[:, 4 * d + 3, T + c * C:T + (c + 1) * C], S[d][:, :], bdA[q][d][:, c, P:P + C], start=True, stop=True)
                        if n < NC - q:
                            mm = pe.matmul(ps[:, 4 * d + 2, c * P:(c + 1) * P], AT[d][:, c, :], S[d][:, :], start=True, stop=True)
                        scan_pe[d].done(mm, (q, f"st{n}"))
                    if ahead and n < 2:
                        gram(*following(b, q), n)
                if q:
                    for d in range(2):
                        scan_dve[d].wait(pe, (1, "y"), b)

            pe.wait_ge(wd_ready, 1)
            pe.wait_ge(mix_done, 1)
            for stage in FRONT:
                front(0, 0, stage)
            front_out(0, 0)
            for d in range(2):
                gram(0, 0, d)
            with pe.Fori(0, RB - 1) as b:
                unit(b, 0)
                unit(b, 1)
            unit(RB - 1, 0)
            unit(RB - 1, 1, ahead=False)
            pe.wait_ge(scan_dve[0].sem, RB * len(scan_dve[0].names))
            pe.wait_ge(scan_dve[1].sem, RB * len(scan_dve[1].names))
            pe.wait_ge(gup_in, 16)
            pe.wait_ge(gd_ready, 1)
            for n in range(RB):
                if n >= 8:
                    pe.wait_ge(gate_out, n // 2 - 3)
                for k in range(2):
                    mm = pe.matmul(ps[:, n // 2 % 4, (n % 2) * T:(n % 2 + 1) * T], gup[:, k, n * P:(n + 1) * P], gd[:, k, :], start=(k == 0), stop=(k == 1))
                if n % 2:
                    mm.then_inc(gate_mm, 1)
            with pe.Fori(0, RB // 2) as i:
                gnp.done(pe.matmul(ps[:, 4, :], blk64, ymix[:, ds(i * 2, 2), :], start=True, stop=True), "mean")
                gna.wait(pe, "sq", i)
                gnp.done(pe.matmul(ps[:, 5, :], blk64, ysq[:, :], start=True, stop=True), "var")
            pe.wait_ge(gate_out, RB // 2)
            on_mov = lambda k, h: mov[:, k, :, :] if h is None else mov[:, k, h, :]
            on_hid = lambda k, h: hid[:, k, :, :] if h is None else hid[:, k, h, :]

            def norm_and_ffn(e, stat, norm, suffix):
                sums_of_squares(stat, T)
                pe.wait_ge(mov_ready, (norm + 1) * KB)
                gemm(PH["ffn" + suffix], on_x(PH["ffn" + suffix], on_mov))
                pe.wait_ge(ffn_lo, (e + 1) * PH["ffn"].trips + 1)
                gemm(PH["down" + suffix], on_x(PH["down" + suffix], on_hid))

            pe.wait_ge(ylo, 4)
            gemm(PH["out"], on_x(PH["out"], on_mov))
            norm_and_ffn(0, 1, 2, "")
            sums_of_squares(2, T)
            sums_of_squares(3, T)
            pe.wait_ge(mov_ready, 4 * KB)
            gemm(PH["in_2"], on_x(PH["in_2"], on_mov))
            pe.wait_ge(gw_in, 32)
            pe.wait_ge(bank_free, IN2_OUT)
            for n in range(RB):
                pe.wait_ge(lru_u, n + 1)
                for g in range(2):
                    mm = pe.matmul(ps[:, 4 * g + n // 2, (n % 2) * T:(n % 2 + 1) * T], gw[:, g, n, :], lu[:, n, :], start=True, stop=True)
                if n % 2:
                    mm.then_inc(lru_gates, 1)
            pe.wait_ge(lru_i, 2 * RB)
            def head(h, first=False):
                retg.wait(pe, "v", h)
                if not first:
                    reta.wait(pe, "vt", h - 1)
                for n in range(2):
                    mm = pe.transpose(ps[:, 1, n * P:(n + 1) * P], rv[:, n * P:(n + 1) * P], ident)
                retp.done(mm, "vt")
                if not first:
                    retd.wait(pe, "qs", h - 1)
                retp.done(pe.matmul(ps[:, 0, :].rearrange("p (a b t) -> p a b t", a=2, b=1), swap, qk_of(h), start=True, stop=True), "sw")
                retd.wait(pe, "qr", h)
                pe.matmul(ps[:, 2, 0:T], rqk[:, 1, 0:P], rqk[:, 0, :], start=True, stop=True)
                retp.done(pe.matmul(ps[:, 2, T:T + P], rqk[:, 1, P:T], rqk[:, 0, P:T], start=True, stop=True), "sc")
                retd.wait(pe, "pr", h)
                reta.wait(pe, "vt", h)
                if not first:
                    reta.wait(pe, "o", h - 1)
                pe.matmul(ps[:, 3, 0:T], rvt[:, 0, :], rp[:, 0:T], start=True, stop=False)
                retp.done(pe.matmul(ps[:, 3, P:T], rvt[:, 1, :], rp[:, T:T + P], start=False, stop=True), "o")

            pe.wait_ge(kret_in, 16)
            head(0, True)
            with pe.Fori(0, RET_HEADS - 1) as i:
                head(i + 1)
            reta.wait(pe, "o", RET_HEADS - 1)
            with pe.Fori(0, RET_HEADS // 2) as i:
                rnp.done(pe.matmul(ps[:, 4, :], ones, ro[:, ds(i * 2, 2), :], start=True, stop=True), "mean")
                rna.wait(pe, "sq", i)
                rnp.done(pe.matmul(ps[:, 5, :], ones, osq[:, :], start=True, stop=True), "var")
                rnd.wait(pe, "v", i)
            pe.wait_ge(y2_lo, 4)
            gemm(PH["out_2"], on_x(PH["out_2"], on_mov))
            norm_and_ffn(1, 4, 4, "_2")
            sums_of_squares(5, T)
            pe.wait_ge(x_scaled, 2 * KB)
            pe.wait_ge(bank_free, PH["down_2"].pair(1, 3) + 1 + BANK_CREDIT)
            for n in range(8):
                for k in range(4):
                    mm = pe.transpose(ps[:, n, k * P:(k + 1) * P], xT[:, 4 * (n // 2) + k, (n % 2) * P:(n % 2 + 1) * P], ident)
                mm.then_inc(row_turned, 1)


INPUTS = ["x", "c", "ctx", "c_ctx", "w_mod", "b_mod", "norm_mix", "w_in", "rw_shift", "dec_w0", "dec_up", "iclr_a0",
          "iclr_up", "k_k", "k_a", "r_k", "ln_w", "ln_b", "g_up", "conv_w", "w_out", "norm_ffn", "w_gate", "w_up",
          "w_down", "norm_final", "ln1_w_2", "w_in_2", "conv_w_2", "conv_b_2", "gate_a_w_2", "gate_a_b_2",
          "gate_x_w_2", "gate_x_b_2", "lru_lambda_2", "ret_gn_w_2", "w_out_2", "ln2_w_2", "w_ffn_gate_2",
          "w_ffn_up_2", "w_ffn_down_2", "final_norm_w_2"]


def kernel(**inputs):
    import concourse.bacc as bacc
    from concourse.bass_utils import run_bass_kernel_spmd as run

    nc = bacc.Bacc("TRN2", target_bir_lowering=False, num_devices=1)
    arrays = {"in_" + n: np.ascontiguousarray(inputs[n]) for n in INPUTS}
    arrays = {n: a[0] if a.shape[0] == 1 and n[3:] not in ("x", "c", "ctx") and a.ndim > 1 else a for n, a in arrays.items()}
    arrays.update(constants())
    given = {n: nc.dram_tensor(n, a.shape, F32, kind="ExternalInput").ap() for n, a in arrays.items()}
    given = {n.removeprefix("in_"): ap for n, ap in given.items()}
    out = nc.dram_tensor("out_h", (1, T, D), F32, kind="ExternalOutput").ap()
    program(nc, given, out)
    return run(nc, [arrays], core_ids=[0]).results[0]["out_h"]
```

```python
from contextlib import ExitStack

import numpy as np

import concourse.bass as bass
from concourse import mybir

F32 = mybir.dt.float32
F32R = mybir.dt.float32r
ALU = mybir.AluOpType
ACT = mybir.ActivationFunctionType
ds = bass.ds

P = 128
D = 2048
T = 256
KB = D // P
HEAD = 64
D_RWKV, D_CONV, D_FOUR = D // 2, D // 4, D // 4
RB = D_RWKV // P
LORA = 96
GATE = 256
D_FF = ((8 * D + 3 * 256 - 1) // (3 * 256)) * 256
FB = D_FF // P
WD0 = 3 * D_RWKV
GD0 = WD0 + 2 * LORA
CG0 = GD0 + GATE
D_IN = CG0 + 3 * D_CONV + D_FOUR
D_IN_2 = 6 * (D // 2)
GRID_W = 64
GELU = float(np.sqrt(2 / np.pi))
RMS_EPS, GN_EPS, KK_EPS = 1e-6, 64e-5, 1e-12
LRU_BLOCKS, LRU_C = 8, 8.0
RET_HEADS = 8
DECAY_SCALE = -float(np.exp(np.float32(-0.5)))

RING = 4
CK, CN = 4, 256
BANK = 512
C = 64
NC = T // C

STREAM = [
    ("mod", 1, 16, KB), ("in_kv", 4, 2, KB), ("in_lora", 1, 2, KB), ("in_r", 2, 2, KB), ("in_rest", 4, 2, KB),
    ("out", 4, 2, KB), ("ffn", 22, 2, KB), ("down", 2, 4, FB),
    ("in_2", 4, 2, KB), ("in_2_heads", RET_HEADS, 2, KB), ("out_2", 4, 2, KB), ("ffn_2", 22, 2, KB), ("down_2", 2, 4, FB),
]

MOD0 = {"in_kv": 2, "in_rest": 4}
SIDE = 4


class Phase:

    def __init__(self, name, trips, pairs, rows, g0, p0):
        self.name, self.trips, self.pairs, self.rows = name, trips, pairs, rows
        self.per_pair = n = rows // CK
        self.g0, self.p0 = g0, p0
        self.order = []
        for p in range(pairs):
            for c in range(n):
                self.order.append((False, p, c))
                if name in MOD0 and c % 2 == 0:
                    self.order += [(True, 2 * p + c // 2, e) for e in range(n)]
        self.chunks = len(self.order)

    def chunk(self, i, j):
        return i * self.chunks + (self.g0 + j)

    def slot(self, j):
        return (self.g0 + j) % RING

    def rounds(self, i, j):
        return i * (self.chunks // RING) + (self.g0 + j) // RING

    def pair(self, i, p):
        return i * self.pairs + (self.p0 + p)

    def bank(self, p):
        return 2 * ((self.p0 + p) % 2)

    def last_chunk(self, i, p, side=False):
        return self.chunk(i, self.order.index((side, p, self.per_pair - 1)))

    def completed(self, j):
        side, p, c = self.order[j]
        return (side, p) if c == self.per_pair - 1 else None

    def side(self, i, m):
        return i * SIDE + (4 * SIDE * (self.name == "in_rest") + m + 1)


def phases():
    out, g, p = {}, 0, 0
    for name, trips, pairs, rows in STREAM:
        ph = Phase(name, trips, pairs, rows, g, p)
        assert trips == 1 or ph.chunks % RING == 0
        out[name] = ph
        g += trips * ph.chunks
        p += trips * pairs
    return out, g


class Steps:

    def __init__(self, sem, names):
        self.sem, self.names = sem, list(names)
        assert len(set(self.names)) == len(self.names)
        self.at = 0

    def value(self, name, rounds=0):
        return rounds * len(self.names) + (self.names.index(name) + 1)

    def done(self, ins, name):
        assert self.names[self.at % len(self.names)] == name, (name, self.names[self.at % len(self.names)])
        self.at += 1
        ins.then_inc(self.sem, 1)

    def wait(self, eng, name, rounds=0):
        eng.wait_ge(self.sem, self.value(name, rounds))


class Chain:

    def __init__(self, eng, sem):
        self.eng, self.sem, self.base, self.n, self.i, self.per = eng, sem, 0, 0, None, 0

    def loop(self, i, per):
        self.base, self.i, self.per, self.n = self.base + self.n, i, per, 0

    def end(self, trips):
        assert self.n == self.per, (self.n, self.per)
        self.base, self.n, self.i = self.base + trips * self.per, 0, None

    def mark(self, ins):
        ins.then_inc(self.sem, 1)
        self.n += 1
        return self.base + self.n if self.i is None else self.i * self.per + (self.base + self.n)

    def wait(self, value):
        self.eng.wait_ge(self.sem, value)

    def __call__(self, ins):
        self.wait(self.mark(ins))


def vector_rows():
    order = [
        [("b_mod", 96), ("norm_mix", 16), ("norm_ffn", 16)],
        [("ln1_w_2", 16), ("ln2_w_2", 16), ("norm_final", 16), ("final_norm_w_2", 16), ("dec_w0", 16),
         ("iclr_a0", 16), ("k_k", 8), ("k_a", 8), ("r_k", 8), ("ln_w", 8)],
        [("ln_b", 8), ("conv_w", 12), ("conv_w_2", 32), ("conv_b_2", 8), ("gate_a_b_2", 8), ("gate_x_b_2", 8),
         ("lru_lambda_2", 8), ("ret_gn_w_2", 8)],
        [("shift_rkv", 72), ("shift_gd", 6), ("shift_wd", 3), ("shift_ad", 3)],
    ]
    out = {}
    for t, row in enumerate(order):
        at = 0
        for name, n in row:
            out[name] = (t, at, n)
            at += n
        assert at <= P
    return out


VROWS = vector_rows()


def constants():
    f = np.float32
    eye = np.eye(P, dtype=f)
    blk = np.kron(np.eye(2, dtype=f), np.ones((HEAD, HEAD), f))
    sel = np.zeros((P, P), f)
    sel[0, 0] = sel[1, 0] = sel[2, 1] = sel[3, 1] = 1
    n = np.arange(HEAD)
    cos_h = np.cos(2 * np.pi * np.outer(n, n) / HEAD)
    sin_h = np.sin(2 * np.pi * np.outer(n, n) / HEAD)
    four_h = np.concatenate([np.kron(np.eye(2), cos_h), np.kron(np.eye(2), sin_h)], 1)
    m = np.arange(T)
    ang = 2 * np.pi * (np.outer(m, m) % T) / T
    norm = 1 / np.sqrt(T * HEAD)
    four_t = np.stack([np.cos(ang) * norm, -np.sin(ang) * norm], 1)
    four_t = four_t.reshape(2, P, 2, T).transpose(1, 0, 2, 3).reshape(P, 4 * T)
    basics = np.concatenate([eye, blk, sel, np.ones((P, P), f)], 1).astype(f)
    fourier = np.concatenate([four_h, four_t], 1).astype(f)

    s, t = np.arange(C)[:, None], np.arange(C)[None, :]
    scan = []
    for d in range(2):
        before = s < t if d == 0 else s > t
        two = lambda a: np.kron(np.eye(2), a)
        row = [two(before)]
        size = 1
        while size < C:
            row.append(two(before & (s // (2 * size) == t // (2 * size)) & (s // size != t // size)))
            size *= 2
        scan += row + [np.concatenate([before | (s == t)] * 2, 0)]
    first = np.tile((np.arange(T) % C != 0).astype(f), (P, 1))
    scan = np.concatenate(scan + [first], 1).astype(f)

    half = P // 2
    inv_freq = f(10000.0) ** (-np.arange(0, P, 2, dtype=f) / f(P))
    rot = np.arange(T, dtype=f)[None, :] * inv_freq[:, None]
    cos, sin = np.cos(rot).astype(f), np.sin(rot).astype(f)
    swap = np.zeros((P, P), f)
    swap[np.arange(half) + half, np.arange(half)] = -1
    swap[np.arange(half), np.arange(half) + half] = 1
    log_gamma = np.log1p(-np.exp2(-5.0 - np.arange(RET_HEADS)))
    sp, tt = np.arange(P)[:, None], np.arange(T)[None, :]
    decay = []
    for h in range(RET_HEADS):
        d0 = np.where(tt >= sp, np.exp(log_gamma[h] * np.maximum(tt - sp, 0)) * P ** -0.5, 0)
        decay += [d0, d0[:, :P]]
    ret = np.concatenate([np.concatenate([cos, cos], 0), np.concatenate([sin, sin], 0), swap] + decay, 1).astype(f)
    ret = np.concatenate([ret[:, :2 * T + P], np.eye(P) - 1 / P, ret[:, 2 * T + P:]], 1).astype(f)
    return {"k_basics": basics, "k_fourier": fourier, "k_scan": scan, "k_ret": ret}


LEVELS = 6
SCAN_DIR = P * (1 + LEVELS) + C


def program(nc, A, out):
    PH, TOTAL = phases()
    order = [PH[row[0]] for row in STREAM]
    base = -(-nc.sbuf_base // 32) * 32
    KIB = 1024

    def at(name, offset, shape, dt=F32):
        return nc.alloc_sbuf_tensor_at(name, shape, dt, offset=base + offset)

    raw = at("raw", 0, [P, RING, CK, CN])
    hi = at("hi", 16 * KIB, [P, RING, CK, CN], F32R)
    lo = at("lo", 32 * KIB, [P, RING, CK, CN], F32R)
    fix = 48 * KIB
    vec = at("vec", fix, [P, 4, P])
    mod = at("mod", fix + 2048, [P, 2, 6 * KB])
    gain = at("gain", fix + 2816, [P, 4, KB])
    lcol = at("lcol", fix + 3072, [P, 8, RB])
    basics = at("basics", fix + 3584, [P, 4, P])
    rstd = at("rstd", fix + 5632, [P, 2, T])
    tmp = at("tmp", fix + 7680, [P, 2, 2, T])
    sq = at("sq", fix + 11776, [P, 2, 2 * T])
    nt = at("nt", fix + 15872, [P, 4, T])
    gd = at("gd", fix + 11776, [P, 2, T])
    wdad = at("wdad", fix + 13824, [P, 2, 2, T])
    px = at("px", fix + 17920, [P, 2, T])
    decw = at("decw", fix + 17920, [P, 4, P])
    xT = at("xT", 68 * KIB, [P, KB, T])
    ymix = at("ymix", 68 * KIB, [P, KB, T])
    R = 84 * KIB
    xrow = at("xrow", R, [P, 2, D])
    crow = at("crow", R + 16 * KIB, [P, 2, D])
    vrow = at("vrow", R + 32 * KIB, [P, 4, P])
    ctxT = at("ctxT", R + 40 * KIB, [P, KB, T])
    c4 = at("c4", R + 120 * KIB, [P, KB, 32], F32R)
    raw_more = at("raw_more", R + 76 * KIB, [P, RING, CK, CN])
    cvec = at("cvec", R + 64 * KIB + 512, [2 * KB, P])
    csil = at("csil", R + 64 * KIB, [P, 2, KB])
    mrow = at("mrow", R + 66 * KIB, [4, D])
    mrow2 = at("mrow2", fix + 5632, [4, 2, CN])
    kv = at("kv", R, [P, 2 * RB, 2, T])
    r = at("r", R + 32 * KIB, [P, RB, T])
    proj = at("proj", R + 40 * KIB, [P, 16, T])
    mov1 = at("mov1", R + 56 * KIB, [P, KB, 2, 2, T], F32R)

    oka = lcol[:, 0, :]
    nt_var, nt_sqrt = (nt[:, 2 * n:2 * n + 2, :].rearrange("p a t -> p (a t)") for n in range(2))
    ident, blk64, sel, ones = (basics[:, n, :] for n in range(4))
    ps = nc.alloc_psum_tensor("ps", [P, 8, BANK], F32)

    xres = nc.dram_tensor("xres", [P, KB * T], F32, kind="Internal").ap()

    def vcol(name, n, count=1, rows=P):
        t, first, _ = VROWS[name]
        return vec[0:rows, t, ds(first + n, count)]

    sems = {}

    def sem(name):
        sems[name] = nc.alloc_semaphore(name)
        return sems[name]

    raw_in = [sem(f"raw_in{s}") for s in range(2 * RING)]
    hi_ready, lo_ready, split_free = sem("hi_ready"), sem("lo_ready"), sem("split_free")
    bank_free, tmp_ready = sem("bank_free"), sem("tmp_ready")
    SPLIT_CREDIT, BANK_CREDIT = RING, 2
    TURN = (1, 3, 4, 6)
    VEC_AT = 5
    TURN0 = 4

    def turned_at(p):
        return range(max(2 * (p - TURN0), 0), max(min(2 * (p - TURN0) + 2, KB), 0))

    LOWS0 = PH["in_lora"].p0 + 1
    v_chain, a_chain, g_chain = sem("v_chain"), sem("a_chain"), sem("g_chain")
    c_in, c_turned = sem("c_in"), sem("c_turned")
    vec_in = [sem("vec_in0"), sem("vec_in1")]
    vec_clear, row_in, const_in = sem("vec_clear"), sem("row_in"), sem("const_in")
    vec_turned, vec_ready = sem("vec_turned"), sem("vec_ready")
    turned, ctx_out, x_out = sem("turned"), sem("ctx_out"), sem("x_out")
    csil_ready, chi_ready, c4_clear, c4_ready = sem("csil_ready"), sem("chi_ready"), sem("c4_clear"), sem("c4_ready")
    mrow_ready, mcol_ready, mod_ready, gain_ready = (sem(n) for n in ("mrow_ready", "mcol_ready", "mod_ready", "gain_ready"))
    side_free = sem("side_free")
    sq_ready, sq_used, var_ready, sqrt_ready, rstd_ready = (
        sem(n) for n in ("sq_ready", "sq_used", "var_ready", "sqrt_ready", "rstd_ready"))
    nt_ready, nhi_ready, mov_ready = sem("nt_ready"), sem("nhi_ready"), sem("mov_ready")
    shift_ready = sem("shift_ready")
    M0 = R + 56 * KIB
    kfour = at("kfour", 68 * KIB, [P, 5, T])
    uf = at("uf", M0 + 5 * KIB, [P, 2, 4, 2, P])
    x_spilled, four_in, uf_turned, uf_ready, four_done, conv_mid, conv_done, mix_done = (
        sem(n) for n in ("x_spilled", "four_in", "uf_turned", "uf_ready", "four_done", "conv_mid", "conv_done",
                         "mix_done"))
    REST_DONE = PH["in_rest"].last_chunk(3, 1) + 1 + SPLIT_CREDIT
    REST_OUT = PH["in_rest"].pair(3, 1) + 1 + BANK_CREDIT

    def per_dir(name, offset, shape, step):
        return [at(f"{name}{d}", offset + d * step, shape) for d in range(2)]

    kscan = at("kscan", R + 40 * KIB, [P, 2 * SCAN_DIR + T])
    strict = [kscan[:, d * SCAN_DIR:d * SCAN_DIR + P] for d in range(2)]
    level = [[kscan[:, d * SCAN_DIR + (1 + n) * P:d * SCAN_DIR + (2 + n) * P] for n in range(LEVELS)] for d in range(2)]
    upto = [kscan[:, d * SCAN_DIR + (1 + LEVELS) * P:(d + 1) * SCAN_DIR] for d in range(2)]
    inside = kscan[:, 2 * SCAN_DIR:2 * SCAN_DIR + T]
    S0 = R + 49 * KIB
    bdV = at("bdV", S0, [P, NC, P])
    tokV = at("tokV", S0 + 2048, [P, NC, P])
    S = per_dir("S", S0 + 4096, [P, P], 512)
    kk = at("kk", fix + 5632, [P, 2 * T])
    kq = at("kq", fix + 7680, [P, 2 * T])
    kn = at("kn", fix + 9728, [P, 2 * T])
    DIR = 33 * KIB
    def per_unit(name, shape, ctx_offset, x_offset):
        return [[at(f"{name}{q}{d}", ((hi2, lo2)[d] + ctx_offset) if q == 0 else M0 + x_offset + d * DIR, shape) for d in range(2)]
                for q in range(2)]

    hi2, lo2 = 24 * KIB, 40 * KIB
    bdA = per_unit("bdA", [P, NC, P + C], 0, 0)
    bdB = per_unit("bdB", [P, NC, P], 3072, 3072)
    bdK = per_unit("bdK", [P, NC, P], 5120, 5120)
    pc = [per_dir(f"pc{q}", S0 + 5120 + 64 * q, [P, NC], 32) for q in range(2)]
    tokR = per_dir("tokR", M0 + 7168, [P, NC, 2, P], DIR)
    tokBQ = per_dir("tokBQ", M0 + 11264, [P, NC, P + C], DIR)
    tokK = per_dir("tokK", M0 + 14336, [P, NC, P], DIR)
    U = per_dir("U", M0 + 16384, [P, NC, P], DIR)
    ULa = per_dir("ULa", M0 + 18432, [P, NC, P], DIR)
    MT = per_dir("MT", M0 + 20480, [P, NC, P], DIR)
    RT = per_dir("RT", M0 + 22528, [P, NC, C], DIR)
    XY = per_dir("XY", M0 + 23552, [P, NC, 2, P], DIR)
    lw, L, ex, en, av, kd = ([x for x in per_dir(n, M0 + 27648 + 1024 * k, [P, T], DIR)]
                             for k, n in enumerate(("lw", "L", "ex", "en", "av", "kd")))
    XT, AT, BM = bdB, U, bdK
    bcol = lcol[:, 6, 0:4]

    FRONT = range(1, LEVELS)

    def steps(kind, names):
        return [Steps(sem(f"{kind}{d}"), [(q, n) for q in range(2) for n in names(q, d)]) for d in range(2)]

    def front_pe_names(q, d):
        return ["zz"] + (["kk"] if q == 0 and d == 0 else []) + (["rk"] if q and d else []) + ["G1"]

    def front_act_names(q, d):
        out = (["bc0", "bc1"] if q == 0 and d == 0 else []) + (["bv0", "bv1"] if d == 0 else []) + ["sg", "sa"]
        out += (["ksq"] if q == 0 and d == 0 else []) + ["eex", "en", "pc"] + (["ep"] if q else [])
        return out + (["ksqrt"] if q == 0 and d == 0 else [])

    def front_dve_names(q, d):
        out = (["kq"] if q == 0 and d == 0 else []) + ["lw", "L", "Lx"] + (["kv"] if q == 0 and d == 0 else []) + ["kf", "kd"]
        if q:
            return out + ["ba"] + (["rk0", "rk1"] if d else []) + ["k0", "k1", "a0", "a1", "b0", "b1", "rho"] + (["bonus"] if d else [])
        if d == 0:
            return out + ["n0", "k0", "k1", "n1", "n2", "n3", "n4", "n5", "kk", "ba", "a0", "a1", "b0", "b1"]
        return out + ["k0", "k1", "ba", "a0", "a1", "b0", "b1"]

    def pe_names(q, d):
        out = ["G2", "tA", "tB", "tK"] + (["tV"] if d == 0 else []) + ["MV", "L0"]
        for l in range(1, LEVELS):
            out += [f"Y{l}"] + ([f"X{l}"] if l < LEVELS - 1 else []) + [f"T{l}"]
        return out + ["Z", "A", "B"] + [f"st{n}" for n in range(NC)]

    def act_names(q, d):
        return ["U", "oA", "oB", "oMV"] + [f"Yb{l}" for l in range(1, LEVELS)] + ["Z"]

    def dve_names(q, d):
        out = (["Q", "R"] if q else ["S"]) + ["M", "oK"] + (["oV"] if d == 0 else []) + ["T0", "X0"]
        for l in range(1, LEVELS):
            out += ([f"X{l}"] if l < LEVELS - 1 else []) + [f"T{l}"]
        out += ["AT"] + (["rho2"] if q else []) + ["Bm"] + (["Y0"] if q else [])
        return out + [f"s{n}" for n in range(NC - q)] + (["y"] if q else [])

    def pool_names(q, d):
        return [f"m{l}" for l in range(LEVELS)]

    front_pe, front_act, front_dve = (steps(k, n) for k, n in (
        ("front_pe", front_pe_names), ("front_act", front_act_names), ("front_dve", front_dve_names)))
    scan_pe, scan_act, scan_dve, scan_pool = (steps(k, n) for k, n in (
        ("scan_pe", pe_names), ("scan_act", act_names), ("scan_dve", dve_names), ("scan_pool", pool_names)))

    def following(b, q):
        return (b, 1) if q == 0 else (b + 1, 0)

    decw_in, kscan_in, bd_clear, wd_ready = sem("decw_in"), sem("kscan_in"), sem("bd_clear"), sem("wd_ready")

    def in_order(d):
        return range(NC) if d == 0 else range(NC - 1, -1, -1)

    def chunks_of(ap):
        return ap.rearrange("p (c t) -> p c t", c=NC)

    def over_chunks(ap):
        n = ap.shape[-1]
        return ap.rearrange("p (a n) -> p a n", a=1).broadcast_to([P, NC, n])

    def over_banks(ap):
        n = ap.shape[-1]
        return ap.rearrange("p (a b n) -> p a b n", a=1, b=1).broadcast_to([P, 2, NC // 2, n])

    def two_banks(b, width, first, count):
        return ps[:, b:b + 2, 0:2 * width].rearrange("p b (c n) -> p b c n", c=2)[:, :, :, first:first + count]

    def in_pairs(ap):
        return ap.rearrange("p (a b) n -> p a b n", a=2)

    gup = at("gup", R + 122 * KIB, [P, 2, P])
    gsq = at("gsq", hi2 + 7 * KIB, [P, T])
    gvar = at("gvar", lo2 + 7 * KIB, [P, T])
    gn = at("gn", S0 + 5 * KIB + 512, [P, T])
    gup_in, gd_ready, scan_done, ymix_done = (sem(n) for n in ("gup_in", "gd_ready", "scan_done", "ymix_done"))
    gnp, gna, gnd = (Steps(sem(s), n) for s, n in (
        ("gn_pe", ["mean", "var", "gate"]), ("gn_act", ["sq", "sqrt"]),
        ("gn_dve", ["c", "v", "n0", "n1", "n2", "n3", "n4", "yn", "w", "b", "g"])))

    mov = at("mov", R + 88 * KIB, [P, KB, 2, T], F32R)
    hid = at("hid", R, [P, FB, 2, T], F32R)
    gbuf = at("gbuf", fix + 11776, [P, 2, T])
    sbuf = at("sbuf", fix + 13824, [P, 2, T])
    ubuf = at("ubuf", fix + 15872, [P, 2, T])
    yhi, ylo, x_back, res_done = sem("yhi"), sem("ylo"), sem("x_back"), sem("res_done")
    ffn_g, ffn_s, ffn_h, ffn_hi, ffn_lo = (sem(n) for n in ("ffn_g", "ffn_s", "ffn_h", "ffn_hi", "ffn_lo"))
    knt = at("knt", M0 + 27648, [P, 2 * T])

    LX, LG, RQ, RK, RV, RG = (n * RB for n in range(6))
    p2 = at("p2", R, [P, 6 * RB, T])
    KRET = 2 * T + 2 * P + RET_HEADS * (T + P)
    kret = at("kret", R + 48 * KIB, [P, KRET])
    rcos, rsin = (kret[:, n * T:(n + 1) * T] for n in range(2))
    swap, less_mean = (kret[:, 2 * T + n * P:2 * T + (n + 1) * P] for n in range(2))
    gw = at("gw", R + 63 * KIB, [P, 2, P])
    lu, la, lA, lb, li, lq, gq, gz = (at(n, R + (64 + k) * KIB, [P, T])
                                      for k, n in enumerate(("lu", "la", "lA", "lb", "li", "lq", "gq", "gz")))
    rqk = at("rqk", R + 72 * KIB, [P, 2, T])
    rqc = at("rqc", R + 74 * KIB, [P, 2, T])
    rv = at("rv", R + 76 * KIB, [P, T])
    rvt = at("rvt", R + 77 * KIB, [P, 2, P])
    rp = at("rp", R + 78 * KIB, [P, T + P])
    rsq, rvar, ron, rsg = (at(n, R + (80 + k) * KIB, [P, T]) for k, n in enumerate(("rsq", "rvar", "ron", "rsg")))
    orow = at("orow", R, [P, 2, D])
    HEADS_DONE = PH["in_2_heads"].last_chunk(RET_HEADS - 1, 1) + 1 + SPLIT_CREDIT
    RESIDUAL_PAIRS = RB
    SUM_STEPS = {"out": 2, "down": 4, "out_2": 2, "down_2": 2}
    SUMS0, steps = {}, 0
    for name, n in SUM_STEPS.items():
        SUMS0[name], steps = steps, steps + 1 + RESIDUAL_PAIRS * n
    sums_ready = sem("sums_ready")
    sums, sums_w, sq_pair = sq[:, 0, :].rearrange("p (a t) -> p a t", a=2), sq[:, 1, 0:T], nt[:, 0:2, :]
    x_done, x_scaled, lam_exp, lam_ready, gw_in, kret_in = (
        sem(n) for n in ("x_done", "x_scaled", "lam_exp", "lam_ready", "gw_in", "kret_in"))
    lrup, lrua, lrud, lrug = (Steps(sem(s), n) for s, n in (
        ("lru_pe", ["g"]), ("lru_act", ["u", "r", "i", "t", "gt", "sq"]),
        ("lru_dve", ["c2", "c1", "c0", "x3", "z", "om", "inv", "a", "h", "hg", "y"]), ("lru_pool", ["iu", "b1", "b2"])))
    retp, reta, retd, retg = (Steps(sem(s), n) for s, n in (
        ("ret_pe", ["cv", "sw", "sc", "o", "var"]), ("ret_act", ["vt", "sg", "sq", "sqrt"]),
        ("ret_dve", ["qs", "qr", "pr", "v", "n0", "n1", "n2", "n3", "n4", "on", "w", "y"]), ("ret_pool", ["v", "qc", "sgm"])))
    y2_hi, y2_lo, row_turned, row_act, row_dve, result_out = (
        sem(n) for n in ("y2_hi", "y2_lo", "row_turned", "row_act", "row_dve", "result_out"))

    def both(ap):
        return ap.rearrange("p (a n) -> p a n", a=1).broadcast_to([P, 2, T])

    def one(x, n):
        return x[:, ds(n, 1), :].rearrange("p a t -> p (a t)")

    def head_pair(p, h):
        return p2[:, RQ + 2 * RB * p:RQ + 2 * RB * (p + 1), :].rearrange("p (a h) t -> p a h t", a=2)[:, :, ds(h, 1), :]

    def trip_out(h):
        return PH["in_2_heads"].pair(h, 1) + (1 + BANK_CREDIT)

    def qk_of(h):
        return p2[:, RQ:RQ + 2 * RB, :].rearrange("p (a h) t -> p a h t", a=2)[:, :, ds(h, 1), :]

    def modcol(part, q, n, count=1):
        return mod[:, q, ds(n + part * KB, count)]

    def raw_at(ph, i, j):
        if ph.name == "mod" and j < ph.chunks:
            s = j % (2 * RING)
            return raw[:, s, :, :] if s < RING else raw_more[:, s - RING, :, :], raw_in[s], j // (2 * RING) + 1
        s = ph.slot(j)
        return raw[:, s, :, :], raw_in[s], ph.rounds(i, j) + (1 - PH["mod"].chunks // (2 * RING))

    def load_vectors(eng, which):
        eng.wait_ge(vec_clear, 1)
        for number, (name, (t, first, n)) in enumerate(VROWS.items()):
            if number % 2 != which:
                continue
            if name.startswith("shift"):
                c0, width = {"shift_rkv": (0, P), "shift_gd": (GD0, P), "shift_wd": (WD0, LORA),
                             "shift_ad": (WD0 + LORA, LORA)}[name]
                src = A["rw_shift"][:, c0:c0 + n // 3 * width]
                for tap in range(3):
                    eng.dma_start(vrow[first + tap * (n // 3):first + (tap + 1) * (n // 3), t, 0:width],
                                  src[tap].rearrange("(n c) -> n c", c=width)).then_inc(vec_in[which], 16)
                continue
            src = A[name]
            names = " ".join("abcd"[:len(src.shape)])
            flat = src.rearrange(f"{names} -> ({names})") if len(src.shape) > 1 else src
            eng.dma_start(vrow[first:first + n, t, :], flat.rearrange("(n c) -> n c", c=P)).then_inc(vec_in[which], 16)

    VEC_DMAS = [sum(3 if n.startswith("shift") else 1 for n in list(VROWS)[which::2]) for which in range(2)]

    def weights(w, rows, col):
        return w[rows * P:(rows + CK) * P, ds(col, CN)].rearrange("(k p) n -> p k n", p=P)

    def chunk_source(ph, i, j):
        side, p, c = ph.order[j]
        q = c * CK
        if side:
            return weights(A["w_mod"], q, i * (D // 2) + (MOD0[ph.name] * D + p * CN))
        if ph.name == "mod":
            return weights(A["w_mod"], q, p * CN)
        if ph.name == "in_kv":
            return weights(A["w_in"], q, i * (2 * CN) + (D_RWKV + p * CN))
        if ph.name == "in_lora":
            return weights(A["w_in"], q, (WD0, GD0)[p])
        if ph.name == "in_r":
            return weights(A["w_in"], q, i * (2 * CN) + p * CN)
        if ph.name == "in_rest":
            return weights(A["w_in"], q, i * (2 * CN) + (CG0 + p * CN))
        if ph.name in ("ffn", "ffn_2"):
            tail = "" if ph.name == "ffn" else "_2"
            w = A[("w_gate", "w_up")[p]] if not tail else A[("w_ffn_gate_2", "w_ffn_up_2")[p]]
            return weights(w, q, i * CN)
        if ph.name == "in_2_heads":
            rows = c // 2 * 2 * CK
            return A["w_in_2"][rows * P:(rows + 2 * CK) * P, ds(i * P + (D * (1 + p) + c % 2 * (D // 2)), P)]\
                .rearrange("(k p) n -> p k n", p=P)
        w = {"out": "w_out", "down": "w_down", "in_2": "w_in_2", "out_2": "w_out_2", "down_2": "w_ffn_down_2"}[ph.name]
        return weights(A[w], q, i * (ph.pairs * CN) + p * CN)

    def loop(eng, ph, body, peel=False):
        if peel:
            body(0)
            with eng.Fori(0, ph.trips - 1) as i:
                body(i + 1)
            return
        if ph.trips == 1:
            body(0)
            return
        ends = ph is order[-1]
        with eng.Fori(0, ph.trips - ends) as i:
            body(i)
        if ends:
            body(ph.trips - 1)

    with nc.Block() as block:

        @block.sync
        def _(sp):
            for ph in order:
                def trip(i):
                    for j in range(ph.chunks):
                        if ph.name == "mod" and j == 2 * RING:
                            for rows, name in ((xrow, "x"), (crow, "ctx")):
                                sp.dma_start(rows[:, :, :], A[name][0].rearrange("(a p) d -> p a d", p=P)).then_inc(row_in, 16)
                            load_vectors(sp, 0)
                        if ph.name != "mod":
                            sp.wait_ge(lo_ready, ph.chunk(i, j) + 1)
                        elif j >= 2 * RING:
                            sp.wait_ge(lo_ready, j - 2 * RING + 1 + RING)
                        dst, arrives, _ = raw_at(ph, i, j)
                        src = chunk_source(ph, i, j)
                        if ph.name == "in_2_heads":
                            dst = dst.rearrange("p k (a n) -> p (k a) n", a=2)
                        sp.dma_start(dst, src).then_inc(arrives, 16)
                if ph.name == "in_r":
                    sp.wait_ge(mov_ready, 2 * KB)
                    sp.dma_start(xres.rearrange("p (k t) -> p k t", k=KB), xT[:, :, :]).then_inc(x_spilled, 16)
                loop(sp, ph, trip)
            for n in range(8):
                sp.wait_ge((row_act, row_dve)[n % 2], n // 2 + 1)
                sp.dma_start(out[0, (n % 2) * P:(n % 2 + 1) * P, (n // 2) * BANK:(n // 2 + 1) * BANK],
                             orow[:, n % 2, (n // 2) * BANK:(n // 2 + 1) * BANK]).then_inc(result_out, 16)
            sp.wait_ge(x_spilled, 16)
            sp.wait_ge(result_out, 8 * 16)

        @block.gpsimd
        def _(pool):
            pool.memset(vrow[:, :, :], 0.0).then_inc(vec_clear, 1)
            pool.memset(c4[:, :, :].bitcast(F32), 0.0).then_inc(c4_clear, 1)
            pool.dma_start(basics[:, :, :], A["k_basics"].rearrange("p (a n) -> p a n", a=4)).then_inc(const_in, 16)
            load_vectors(pool, 1)

            pool.wait_ge(x_spilled, 16)
            pool.dma_start(kfour[:, :, :], A["k_fourier"].rearrange("p (a n) -> p a n", a=5)).then_inc(four_in, 16)

            def load_lora(b):
                for n, name in enumerate(("dec_up", "iclr_up")):
                    pool.dma_start(decw[0:LORA, 2 * n:2 * n + 2, :], A[name][:, :, ds(b, P)].rearrange("d p n -> p d n"))\
                        .then_inc(decw_in, 16)

            def clear(tiles):
                for bd in tiles:
                    pool.memset(bd, 0.0).then_inc(bd_clear, 1)

            pool.wait_ge(split_free, REST_DONE)
            load_lora(0)
            clear(x[q][d][:, :, 0:P] for q, d in ((0, 0), (0, 1), (1, 1)) for x in (bdA, bdB, bdK))
            pool.wait_ge(conv_done, 1)
            pool.dma_start(kscan[:, :], A["k_scan"]).then_inc(kscan_in, 16)
            clear([bdV[:, :, :]])
            pool.wait_ge(mix_done, 1)
            clear(x[1][0][:, :, 0:P] for x in (bdA, bdB, bdK))

            def mask_levels(b, q, gate_of=None):
                for l in range(LEVELS):
                    for d in range(2):
                        dst = (ULa, MT)[l % 2][d]
                        if l == 0:
                            scan_act[d].wait(pool, (q, "U"), b)
                        else:
                            scan_pe[d].wait(pool, (q, ("MV", "L0", "Y1", "Y2", "Y3")[l - 1]), b)
                            if l == 2:
                                scan_dve[d].wait(pool, (q, "T0"), b)
                        if l == LEVELS - 1 and d == 0 and gate_of is not None:
                            gnp.wait(pool, "gate", gate_of)
                        scan_pool[d].done(pool.tensor_tensor(dst[:, :, :], U[d][:, :, :], over_chunks(level[d][l]), ALU.mult),
                                          (q, f"m{l}"))

            pool.wait_ge(kscan_in, 16)
            def load_gate(b):
                pool.dma_start(gup[:, :, :], A["g_up"].rearrange("(k p) n -> p k n", p=P)[:, :, ds(b, P)]).then_inc(gup_in, 16)

            load_gate(0)
            mask_levels(0, 0)
            with pool.Fori(0, RB - 1) as b:
                front_pe[1].wait(pool, (1, "zz"), b)
                load_lora(b * P + P)
                mask_levels(b, 1)
                mask_levels(b + 1, 0, gate_of=b)
                load_gate(b * P + P)
            mask_levels(RB - 1, 1)

            pool.wait_ge(ylo, 4)
            pool.wait_ge(x_spilled, 16)
            pool.dma_start(xT[:, :, :], xres.rearrange("p (k t) -> p k t", k=KB)).then_inc(x_back, 16)

            def load_gates(h):
                for n, name in enumerate(("gate_a_w_2", "gate_x_w_2")):
                    pool.dma_start(gw[:, n:n + 1, :], A[name][ds(h, 1)].rearrange("n c d -> c n d")).then_inc(gw_in, 16)

            pool.wait_ge(x_done, 2)
            pool.dma_start(kret[:, :], A["k_ret"]).then_inc(kret_in, 16)
            load_gates(0)

            def retention(h):
                retg.done(pool.tensor_copy(rv[:, :], one(p2, h + RV)), "v")
                retg.done(pool.tensor_tensor(rqc[:, :, :], qk_of(h), both(rcos), ALU.mult), "qc")

            def gate(h):
                retg.done(pool.tensor_tensor(rsg[:, :], rsg[:, :], one(p2, h + RG), ALU.mult), "sgm")

            def side(h):
                pool.wait_ge(bank_free, trip_out(h - 1))
                first = isinstance(h, int) and h == 0
                if not first:
                    retention(h - 1)
                if not first:
                    reta.wait(pool, "sg", h - 1)
                lrua.wait(pool, "i", h)
                lrug.done(pool.tensor_tensor(lb[:, :], lb[:, :], lu[:, :], ALU.mult), "iu")
                if not (isinstance(h, int) and h == RET_HEADS - 1):
                    load_gates(h + 1)
                if not first:
                    gate(h - 1)
                lrua.wait(pool, "sq", h)
                lrud.wait(pool, "inv", h)
                lrug.done(pool.tensor_tensor(lq[:, :], lq[:, :], li[:, :], ALU.mult), "b1")
                lrug.wait(pool, "b1", h)
                lrug.done(pool.tensor_tensor(lb[:, :], lb[:, :], lq[:, :], ALU.mult), "b2")

            pool.wait_ge(kret_in, 16)
            side(0)
            with pool.Fori(0, RET_HEADS - 2) as i:
                side(i + 1)
            side(RET_HEADS - 1)
            pool.wait_ge(bank_free, trip_out(RET_HEADS - 1))
            retention(RET_HEADS - 1)
            reta.wait(pool, "sg", RET_HEADS - 1)
            gate(RET_HEADS - 1)

        @block.scalar
        def _(act):
            chain = Chain(act, a_chain)

            def split(ph, i, j):
                if isinstance(i, int) and ph.chunk(i, j) >= TOTAL:
                    return
                s = ph.slot(j)
                src, arrived, loads = raw_at(ph, i, j)
                act.wait_ge(arrived, loads * 16)
                act.wait_ge(split_free, ph.chunk(i, j) + 1)
                act.activation(hi[:, s, :, :], src, ACT.Copy).then_inc(hi_ready, 1)

            def gemm(ph, evacuate, side=None):
                def trip(i):
                    for j in range(ph.chunks):
                        split(ph, i, j + 2)
                        if side:
                            side(i, j)
                        pair = ph.completed(j)
                        if pair and not pair[0]:
                            evacuate(i, pair[1])
                loop(act, ph, trip, peel=side)

            def lows(ph, i, p, wait=True):
                if wait:
                    act.wait_ge(split_free, ph.last_chunk(i, p) + (1 + SPLIT_CREDIT))
                b, t = ph.bank(p), (ph.p0 + p) % 2
                act.activation(tmp[:, t, :, :], ps[:, b:b + 2, T:2 * T], ACT.Copy).then_inc(tmp_ready, 1)

            def sqrt_of_variance(n, width):
                act.wait_ge(var_ready, n + 1)
                act.activation(nt_sqrt[:, 0:width], nt_var[:, 0:width], ACT.Sqrt).then_inc(sqrt_ready, 1)

            def normed_hi(n, *jobs):
                per = 4 // len(jobs)
                with act.Fori(0, KB // per) as i:
                    for e in range(4):
                        dest, shift = jobs[e % len(jobs)]
                        k = i * per + e // len(jobs)
                        act.wait_ge(nt_ready, i * 4 + (n * KB + e + 1))
                        if shift is None:
                            ins = act.activation(dest(k), nt[:, e, :], ACT.Copy)
                        else:
                            ins = act.activation(dest(k), nt[:, e, :], ACT.Identity, bias=shift(k))
                        ins.then_inc(nhi_ready, 1)

            for q, name in enumerate(("c", "c_ctx")):
                flat = A[name].rearrange("a c -> (a c)") if len(A[name].shape) > 1 else A[name]
                act.dma_start(cvec[q * KB:(q + 1) * KB, :], flat.rearrange("(n c) -> n c", c=P)).then_inc(c_in, 16)
            act.wait_ge(c_turned, 1)
            act.activation(csil[:, :, :], ps[:, 0, 0:2 * KB].rearrange("p (q k) -> p q k", q=2), ACT.Silu).then_inc(csil_ready, 1)
            act.wait_ge(csil_ready, 1)
            act.wait_ge(c4_clear, 1)
            for q in range(2):
                act.activation(c4[:, :, 2 * q:2 * q + 1], csil[:, q, :], ACT.Copy).then_inc(chi_ready, 1)
            for j in range(2):
                split(PH["mod"], 0, j)

            def turn(i, p):
                if p == VEC_AT:
                    act.wait_ge(vec_turned, 1)
                    act.activation(vec[:, :, :], ps[:, 5, :].rearrange("p (a n) -> p a n", a=4), ACT.Copy).then_inc(vec_ready, 1)
                for k in turned_at(p):
                    act.wait_ge(turned, k + 1)
                    act.activation(ctxT[:, k, :], ps[:, TURN[k % 4], 0:T], ACT.Copy).then_inc(ctx_out, 1)
                    if k >= 2:
                        act.wait_ge(sq_used, k - 1)
                    act.activation(sq[:, k % 2, :], ps[:, TURN[k % 4], :], ACT.Square).then_inc(sq_ready, 1)
                if p == TURN0 + KB // 2 + 1:
                    sqrt_of_variance(0, 2 * T)
            gemm(PH["mod"], turn)
            act.wait_ge(gain_ready, 2)
            normed_hi(0, *[(lambda k, q=q: mov1[:, k, 0, 1 - q, :], lambda k, q=q: modcol(0, q, k)) for q in (1, 0)])

            def shift_both(i, p):
                ph = PH["in_kv"]
                act.wait_ge(split_free, ph.last_chunk(i, p) + (1 + SPLIT_CREDIT))
                for blk in range(2):
                    n = i * 4 + (2 * p + blk)
                    act.activation(kv[:, ds(n, 1), :, :], ps[:, ph.bank(p) + blk, :], ACT.Copy,
                                   scale=vcol("shift_rkv", n + (3 * RB + RB))).then_inc(shift_ready, 1)

            def shift_lora(i, p):
                ph = PH["in_lora"]
                act.wait_ge(split_free, ph.last_chunk(i, p) + (1 + SPLIT_CREDIT))
                if p == 0:
                    for blk, name in enumerate(("shift_wd", "shift_ad")):
                        act.activation(wdad[0:LORA, blk, :, :], ps[0:LORA, blk, :], ACT.Copy,
                                       scale=vcol(name, 1, rows=LORA)).then_inc(shift_ready, 1)
                    return
                lows(ph, i, p, wait=False)
                for blk in range(2):
                    act.wait_ge(bank_free, ph.pair(i, p) + (1 + BANK_CREDIT))
                    act.activation(gd[:, blk, :], px[:, blk, :], ACT.Copy, scale=vcol("shift_gd", 2 + blk)).then_inc(shift_ready, 1)

            def shift_r(i, p):
                lows(PH["in_r"], i, p)
                for blk in range(2):
                    n = i * 4 + (2 * p + blk)
                    act.wait_ge(bank_free, PH["in_r"].pair(i, p) + (1 + BANK_CREDIT))
                    act.activation(r[:, ds(n, 1), :], px[:, blk, :], ACT.Copy,
                                   scale=vcol("shift_rkv", n + 3 * RB)).then_inc(shift_ready, 1)

            gemm(PH["in_kv"], shift_both)
            gemm(PH["in_lora"], shift_lora)
            gemm(PH["in_r"], shift_r)

            gemm(PH["in_rest"], lambda i, p: lows(PH["in_rest"], i, p))
            act.activation(lcol[:, 1, :], vcol("lru_lambda_2", 0, RB), ACT.Abs).then_inc(lam_exp, 1)
            act.wait_ge(lam_exp, 1)
            act.activation(lcol[:, 2, :], lcol[:, 1, :], ACT.Exp, scale=-1.0).then_inc(lam_exp, 1)
            act.activation(wdad[0:LORA, 0, :, :], wdad[0:LORA, 0, :, :], ACT.Tanh).then_inc(wd_ready, 1)
            act.wait_ge(conv_mid, 1)
            for blk in range(4):
                act.activation(ymix[:, RB + blk, :], proj[:, blk, :], ACT.Copy, scale=vcol("conv_w", 4 + blk)).then_inc(conv_mid, 1)
            for n in range(4):
                act.wait_ge(uf_turned, n + 1)
                act.activation(uf[:, n // 2, 2 * (n % 2):2 * (n % 2) + 2, :, :], ps[:, 4 + n, :], ACT.Copy).then_inc(uf_ready, 1)

            def front(b, q, stage):
                def done(d, ins, name):
                    front_act[d].done(ins, (q, name))
                first = q == 0
                if stage == 1:
                    if first:
                        for n, name in enumerate(("dec_w0", "iclr_a0")):
                            done(0, act.activation(bcol[:, 2 * n:2 * n + 2], vcol(name, 0, 2 * RB).rearrange("p (d n) -> p d n", d=2)[:, :, ds(b, 1)],
                                                   ACT.Copy), f"bc{n}")
                    for h in range(2):
                        hs = slice(h * HEAD, (h + 1) * HEAD)
                        done(0, act.activation(bdV[hs, :, hs], kv[hs, ds(b + RB, 1), q, :], ACT.Copy), f"bv{h}")
                    if first:
                        front_act[0].wait(act, (q, "bc1"), b)
                    for d in range(2):
                        front_pe[d].wait(act, (q, "zz"), b)
                        done(d, act.activation(lw[d][:, :], ps[:, 4 * d + 1, 0:T], ACT.Sigmoid, bias=bcol[:, d:d + 1]), "sg")
                        done(d, act.activation(av[d][:, :], ps[:, 4 * d + 1, T:2 * T], ACT.Sigmoid, bias=bcol[:, 2 + d:3 + d]), "sa")
                    if first:
                        front_dve[0].wait(act, (q, "kq"), b)
                        done(0, act.activation(kn[:, :], kq[:, :], ACT.Square), "ksq")
                if stage == 2:
                    for d in range(2):
                        front_dve[d].wait(act, (q, "Lx"), b)
                        done(d, act.activation(ex[d][:, :], ex[d][:, :], ACT.Exp), "eex")
                        done(d, act.activation(en[d][:, :], L[d][:, :], ACT.Exp, scale=-1.0), "en")
                        last = C - 1 if d == 0 else 0
                        done(d, act.activation(pc[q][d][:, :], chunks_of(L[d][:, :])[:, :, last], ACT.Exp), "pc")
                        if q:
                            front_act[d].wait(act, (q, "pc"), b)
                            done(d, act.activation(L[d][:, :], L[d][:, :], ACT.Exp), "ep")
                    if first:
                        front_dve[0].wait(act, (q, "kv"), b)
                        done(0, act.activation(kk[:, :], kn[:, :], ACT.Sqrt), "ksqrt")

            def group_norm(b, stage):
                if stage == 3:
                    gnd.wait(act, "c", b)
                    gna.done(act.activation(gsq[:, :], ymix[:, ds(b, 1), :].rearrange("p a t -> p (a t)"), ACT.Square), "sq")
                if stage == 5:
                    gnd.wait(act, "v", b)
                    gna.done(act.activation(gn[:, :], gvar[:, :], ACT.Sqrt), "sqrt")

            def unit(b, q, ahead=True, norm=None):
                for d in range(2):
                    front_pe[d].wait(act, (q, "G1"), b)
                    if q:
                        scan_dve[d].wait(act, (q, "Q"), b)
                    scan_act[d].done(act.activation(in_pairs(U[d][:, :, :]), two_banks(4 * d, P + C * q, 0, P), ACT.Copy), (q, "U"))
                for name, src, bank, dst in (("oA", "tA", 0, lambda d: tokR[d][:, :, 0, :]), ("oB", "tB", 1, lambda d: tokBQ[d][:, :, 0:P]),
                                             ("oMV", "MV", 0, lambda d: tokR[d][:, :, 1, :])):
                    for d in range(2):
                        scan_pe[d].wait(act, (q, src), b)
                        scan_act[d].done(act.activation(dst(d), ps[:, 4 * d + bank, :], ACT.Copy), (q, name))
                for l in FRONT:
                    for d in range(2):
                        scan_pe[d].wait(act, (q, f"Y{l}"), b)
                        scan_act[d].done(act.activation(XY[d][:, :, 1, :], ps[:, 4 * d + 2, :], ACT.Copy), (q, f"Yb{l}"))
                    if ahead:
                        front(*following(b, q), l)
                    if norm is not None:
                        group_norm(norm, l)
                for d in range(2):
                    scan_pe[d].wait(act, (q, "Z"), b)
                    scan_act[d].done(act.activation(XY[d][:, :, :, :].rearrange("p (a b) z n -> p a (b z n)", a=2), ps[:, 4 * d + 2:4 * d + 4, :],
                                                    ACT.Copy, scale=-1.0), (q, "Z"))
                for d in range(2):
                    scan_pe[d].wait(act, (q, f"st{NC - 1}"), b)

            act.activation(gd[:, :, :], gd[:, :, :], ACT.Sigmoid).then_inc(gd_ready, 1)
            act.wait_ge(bd_clear, 13)
            for stage in FRONT:
                front(0, 0, stage)
            unit(0, 0)
            with act.Fori(0, RB - 1) as b:
                unit(b, 1)
                unit(b + 1, 0, norm=b)
            unit(RB - 1, 1, ahead=False)
            for stage in FRONT:
                group_norm(RB - 1, stage)
            act.wait_ge(scan_done, 1)
            for n in (0, 2, 3, 1):
                if n == 1:
                    act.wait_ge(ymix_done, 1)
                act.activation(mov[:, 4 * n:4 * n + 4, 0, :], ymix[:, 4 * n:4 * n + 4, :], ACT.Copy).then_inc(yhi, 1)
            def gated(e, ph):
                def evacuate(i, p):
                    lows(ph, i, p)
                    if p == 0:
                        act.wait_ge(bank_free, ph.pair(i, p) + (1 + BANK_CREDIT))
                        act.activation(sbuf[:, :, :], gbuf[:, :, :], ACT.Silu).then_inc(ffn_s, 1)
                    else:
                        act.wait_ge(ffn_h, i + (e * PH["ffn"].trips + 1))
                        act.activation(hid[:, ds(i * 2, 2), 0, :], ubuf[:, :, :], ACT.Copy).then_inc(ffn_hi, 1)
                return evacuate

            def norm_and_ffn(e, stat, norm, shift, suffix):
                sqrt_of_variance(stat, T)
                normed_hi(norm, (lambda k: mov[:, ds(k, 1), 0, :], shift))
                gemm(PH["ffn" + suffix], gated(e, PH["ffn" + suffix]))
                gemm(PH["down" + suffix], lambda i, p: lows(PH["down" + suffix], i, p))

            gemm(PH["out"], lambda i, p: lows(PH["out"], i, p))
            norm_and_ffn(0, 1, 2, lambda k: modcol(3, 0, k), "")
            for stat in (2, 3):
                sqrt_of_variance(stat, T)
            normed_hi(3, (lambda k: mov[:, ds(k, 1), 0, :], None))
            gemm(PH["in_2"], lambda i, p: lows(PH["in_2"], i, p))

            def lru(h, j):
                if j == 0:
                    act.wait_ge(bank_free, trip_out(h - 1))
                    lrua.done(act.activation(lu[:, :], one(p2, h + LX), ACT.Identity, scale=vcol("conv_w_2", h + 3 * RB),
                                             bias=vcol("conv_b_2", h)), "u")
                if j == 3:
                    lrup.wait(act, "g", h)
                    lrua.done(act.activation(la[:, :], ps[:, 4, 0:T], ACT.Sigmoid, bias=vcol("gate_a_b_2", h)), "r")
                    lrua.done(act.activation(lb[:, :], ps[:, 4, T:2 * T], ACT.Sigmoid, bias=vcol("gate_x_b_2", h)), "i")
                    lrua.wait(act, "r", h)
                    lrua.done(act.activation(la[:, :], la[:, :], ACT.Tanh, scale=lcol[:, 1, ds(h, 1)]), "t")
                    lrud.wait(act, "z", h)
                    lrua.done(act.activation(gz[:, :], gq[:, :], ACT.Tanh), "gt")
                if j == 5:
                    lrua.wait(act, "t", h)
                    lrua.done(act.activation(lq[:, :], la[:, :], ACT.Sqrt, scale=-4.0), "sq")

            def retention(h, j):
                if j == 2:
                    retp.wait(act, "cv", h)
                    reta.done(act.activation(rvt[:, :, :], ps[:, 7, 0:T], ACT.Copy), "vt")
                if j == 3:
                    reta.done(act.activation(rsg[:, :], one(p2, h + RG), ACT.Sigmoid), "sg")
                if j == 4:
                    retp.wait(act, "o", h)
                    reta.done(act.activation(rsq[:, :], ps[:, 5, 0:T], ACT.Square), "sq")
                if j == 6:
                    retd.wait(act, "v", h)
                    reta.done(act.activation(ron[:, :], rvar[:, :], ACT.Sqrt), "sqrt")

            def side(h, j):
                lru(h, j)
                if not (isinstance(h, int) and h == 0):
                    retention(h - 1, j)

            def y_hi(n):
                act.activation(mov[:, 4 * n:4 * n + 4, 0, :], p2[:, 4 * n:4 * n + 4, :], ACT.Copy).then_inc(y2_hi, 1)

            act.wait_ge(lam_ready, 1)
            gemm(PH["in_2_heads"], lambda i, p: lows(PH["in_2_heads"], i, p), side)
            act.wait_ge(bank_free, trip_out(RET_HEADS - 1))
            for j in range(8):
                retention(RET_HEADS - 1, j)
                if j in (2, 4, 6):
                    y_hi(j // 2 - 1)
            retd.wait(act, "y", RET_HEADS - 1)
            y_hi(3)
            gemm(PH["out_2"], lambda i, p: lows(PH["out_2"], i, p))
            norm_and_ffn(1, 4, 4, None, "_2")
            sqrt_of_variance(5, T)
            for n in range(0, 8, 2):
                act.wait_ge(row_turned, n + 1)
                act.activation(orow[:, n % 2, (n // 2) * BANK:(n // 2 + 1) * BANK], ps[:, n, :], ACT.Copy).then_inc(row_act, 1)

        @block.vector
        def _(dve):
            chain = Chain(dve, v_chain)
            dve.sem_inc(lo_ready, RING)
            dve.sem_inc(bank_free, BANK_CREDIT)
            dve.sem_inc(side_free, BANK_CREDIT)

            def split(ph, i, j):
                if isinstance(i, int) and ph.chunk(i, j) >= TOTAL:
                    return
                s = ph.slot(j)
                dve.wait_ge(hi_ready, ph.chunk(i, j) + 1)
                dve.tensor_tensor(lo[:, s, :, :], raw_at(ph, i, j)[0], hi[:, s, :, :].bitcast(F32), ALU.subtract)\
                   .then_inc(lo_ready, 1)

            def gemm(ph, evacuate, per_trip=0, side=None):
                def trip(i):
                    if per_trip:
                        chain.loop(i if ph.trips > 1 else None, per_trip)
                    for j in range(ph.chunks):
                        split(ph, i, j + 2)
                        if side:
                            side(i, j)
                        pair = ph.completed(j)
                        if pair and pair[0]:
                            if pair[1] % 2:
                                mod_bias(ph, i, pair[1] - 1)
                            mod_row2(ph, i, pair[1])
                        elif pair:
                            evacuate(i, pair[1])
                            if ph.name in MOD0:
                                mod_bias(ph, i, 2 * pair[1] + 1)
                assert not (per_trip and ph is order[-1])
                loop(dve, ph, trip, peel=side)
                if per_trip:
                    chain.end(ph.trips)

            def summed(ph, i, p, dest):
                b, t = ph.bank(p), (ph.p0 + p) % 2
                dve.wait_ge(tmp_ready, ph.pair(i, p) + (1 - LOWS0))
                return dve.tensor_tensor(dest, ps[:, b:b + 2, 0:T], tmp[:, t, :, :], ALU.add)

            def variance(n, width):
                v, s, y = nt_var[:, 0:width], nt_sqrt[:, 0:width], rstd[:, :, :].rearrange("p a t -> p (a t)")[:, 0:width]
                dve.wait_ge(sq_used, KB + max(n, 3 if n == 2 else 0))
                if n == 3:
                    y = rstd[:, 1, :]
                    chain(dve.scalar_tensor_tensor(out=v, in0=ps[:, 7, T:2 * T], scalar=1.0 / D, in1=rstd[:, 0, :], op0=ALU.mult, op1=ALU.mult))
                    chain(dve.tensor_tensor(v, v, rstd[:, 0, :], ALU.mult))
                    dve.tensor_scalar(v, v, RMS_EPS, None, ALU.add).then_inc(var_ready, 1)
                else:
                    dve.tensor_scalar(v, ps[:, 7, 0:width], 1.0 / D, RMS_EPS, ALU.mult, ALU.add).then_inc(var_ready, 1)
                dve.wait_ge(sqrt_ready, n + 1)
                chain(dve.reciprocal(y, s))
                chain(dve.tensor_tensor(s, y, y, ALU.mult))
                chain(dve.tensor_tensor(s, s, v, ALU.mult))
                chain(dve.tensor_scalar(s, s, -0.5, 1.5, ALU.mult, ALU.add))
                chain(dve.tensor_tensor(y, y, s, ALU.mult))

            def normed(n, *jobs):
                per = 4 // len(jobs)
                with dve.Fori(0, KB // per) as i:
                    for e in range(4):
                        src, g, rs, _, _, _ = jobs[e % len(jobs)]
                        k = i * per + e // len(jobs)
                        dve.scalar_tensor_tensor(out=nt[:, e, :], in0=src(k), scalar=g(k), in1=rs, op0=ALU.mult, op1=ALU.mult).then_inc(nt_ready, 1)
                    for e in range(4):
                        _, _, _, shift, hi_of, lo_of = jobs[e % len(jobs)]
                        k = i * per + e // len(jobs)
                        dve.wait_ge(nhi_ready, i * 4 + (n * KB + e + 1))
                        if shift is None:
                            ins = dve.tensor_tensor(lo_of(k), nt[:, e, :], hi_of(k).bitcast(F32), ALU.subtract)
                        else:
                            ins = dve.scalar_tensor_tensor(out=lo_of(k), in0=nt[:, e, :], scalar=shift(k),
                                                           in1=hi_of(k).bitcast(F32), op0=ALU.add, op1=ALU.subtract)
                        ins.then_inc(mov_ready, 1)
                    dve.wait_ge(mov_ready, i * 4 + (n * KB + 4))

            for q in range(2):
                dve.wait_ge(chi_ready, q + 1)
                dve.tensor_tensor(c4[:, :, 2 * q + 1:2 * q + 2], csil[:, q, :],
                                  c4[:, :, 2 * q:2 * q + 1].bitcast(F32), ALU.subtract).then_inc(c4_ready, 1)
            for j in range(2):
                split(PH["mod"], 0, j)

            def mod_row(i, p):
                ph = PH["mod"]
                part, n = p // 8, p % 8
                dve.wait_ge(split_free, ph.last_chunk(i, p) + (1 + SPLIT_CREDIT))
                dve.tensor_copy(mrow[:, n * CN:(n + 1) * CN], ps[0:4, ph.bank(p), 0:CN]).then_inc(bank_free, 1)
                for k in turned_at(p):
                    dve.wait_ge(sq_ready, k + 1)
                    dve.tensor_copy(xT[:, k, :], ps[:, TURN[k % 4], T:2 * T]).then_inc(x_out, 1)
                if p == TURN0 + KB // 2 + 1:
                    variance(0, 2 * T)
                if n == 7:
                    dve.wait_ge(vec_ready, 1)
                    dve.wait_ge(mcol_ready, part + 1)
                    for q in range(2):
                        dve.tensor_tensor(mod[:, q, ds(part * KB, KB)],
                                          ps[:, 5, 0:2 * KB].rearrange("p (k q) -> p q k", q=2)[:, q, :],
                                          vcol("b_mod", part * KB, KB), ALU.add).then_inc(mod_ready, 1)
            gemm(PH["mod"], mod_row)
            def gains(n, part, q, norm):
                dve.scalar_tensor_tensor(out=gain[:, n, :], in0=modcol(part, q, 0, KB), scalar=1.0, in1=vcol(norm, 0, KB),
                                         op0=ALU.add, op1=ALU.mult).then_inc(gain_ready, 1)

            dve.wait_ge(mod_ready, 4)
            for q in range(2):
                gains(q, 1, q, "norm_mix")
            dve.wait_ge(gain_ready, 2)
            normed(0, *[(lambda k, src=src: src[:, ds(k, 1), :], lambda k, q=q: gain[:, q, ds(k, 1)], rstd[:, 1 - q, :],
                         lambda k, q=q: modcol(0, q, k), lambda k, q=q: mov1[:, ds(k, 1), 0, 1 - q, :],
                         lambda k, q=q: mov1[:, ds(k, 1), 1, 1 - q, :]) for src, q in ((ctxT, 1), (xT, 0))])

            def mod_row2(ph, i, m):
                dve.wait_ge(split_free, ph.last_chunk(i, m, True) + (1 + SPLIT_CREDIT))
                dve.tensor_copy(mrow2[:, m % 2, :], ps[0:4, 4 + 2 * (m % 2), 0:CN]).then_inc(side_free, 1)

            def mod_bias(ph, i, m):
                n = i * 8 + (MOD0[ph.name] * KB + 2 * m)
                dve.wait_ge(mcol_ready, ph.side(i, m) + 2)
                dve.tensor_tensor(mod[:, 0, ds(n, 2)], ps[:, 5, 0:4].rearrange("p (k q) -> p q k", q=2)[:, 0, :],
                                  vcol("b_mod", n, 2), ALU.add).then_inc(mod_ready, 1)

            def outer_taps(dest, src, before, after):
                n = dest.shape[-1]
                chain(dve.scalar_tensor_tensor(out=dest[:, :, 1:n], in0=src[:, :, 0:n - 1], scalar=before,
                                               in1=dest[:, :, 1:n], op0=ALU.mult, op1=ALU.add))
                return dve.scalar_tensor_tensor(out=dest[:, :, 0:n - 1], in0=src[:, :, 1:n], scalar=after,
                                                in1=dest[:, :, 0:n - 1], op0=ALU.mult, op1=ALU.add)

            def shift_both(i, p):
                ph = PH["in_kv"]
                for blk in range(2):
                    n = i * 4 + (2 * p + blk)
                    dve.wait_ge(shift_ready, n + 1)
                    ins = outer_taps(kv[:, ds(n, 1), :, :].rearrange("p n q t -> p (n q) t"),
                                     ps[:, ph.bank(p) + blk, :].rearrange("p (q t) -> p q t", q=2),
                                     vcol("shift_rkv", n + RB), vcol("shift_rkv", n + (6 * RB + RB)))
                    if blk == 0:
                        chain(ins)
                ins.then_inc(bank_free, 1)

            def shift_lora(i, p):
                ph = PH["in_lora"]
                if p == 0:
                    for blk, name in enumerate(("shift_wd", "shift_ad")):
                        dve.wait_ge(shift_ready, 2 * RB + blk + 1)
                        ins = outer_taps(wdad[0:LORA, blk, :, :], ps[0:LORA, blk, :].rearrange("p (q t) -> p q t", q=2),
                                         vcol(name, 0, rows=LORA), vcol(name, 2, rows=LORA))
                        if blk == 0:
                            chain(ins)
                    ins.then_inc(bank_free, 1)
                    return
                summed(ph, i, p, px[:, :, :]).then_inc(bank_free, 1)
                dve.wait_ge(bank_free, ph.pair(i, p) + (1 + BANK_CREDIT))
                for blk in range(2):
                    dve.wait_ge(shift_ready, 2 * RB + 2 + blk + 1)
                    chain(outer_taps(gd[:, blk:blk + 1, :], px[:, blk:blk + 1, :], vcol("shift_gd", blk), vcol("shift_gd", 4 + blk)))

            def shift_r(i, p):
                ph = PH["in_r"]
                summed(ph, i, p, px[:, :, :]).then_inc(bank_free, 1)
                dve.wait_ge(bank_free, ph.pair(i, p) + (1 + BANK_CREDIT))
                for blk in range(2):
                    n = i * 4 + (2 * p + blk)
                    dve.wait_ge(shift_ready, n + (2 * RB + 4 + 1))
                    chain(outer_taps(r[:, ds(n, 1), :], px[:, blk:blk + 1, :], vcol("shift_rkv", n), vcol("shift_rkv", n + 6 * RB)))

            gemm(PH["in_kv"], shift_both, per_trip=6)
            gemm(PH["in_lora"], shift_lora, per_trip=7)
            gemm(PH["in_r"], shift_r, per_trip=8)
            gemm(PH["in_rest"], lambda i, p: summed(PH["in_rest"], i, p, proj[:, ds(i * 4 + 2 * p, 2), :]).then_inc(bank_free, 1))
            dve.wait_ge(mod_ready, 4 + 32)
            gains(2, 4, 0, "norm_ffn")
            dve.wait_ge(gain_ready, 3)
            chain(dve.tensor_tensor(proj[:, 0:4, :], proj[:, 0:4, :], proj[:, 4:8, :], ALU.mult))
            dve.wait_ge(x_spilled, 16)
            dve.sem_inc(conv_mid, 1)
            for blk in range(4):
                dve.wait_ge(conv_mid, blk + 2)
                dest, src = (x.rearrange("p (n t) -> p n t", t=GRID_W) for x in (ymix[:, RB + blk, :], proj[:, blk, :]))
                chain(outer_taps(dest, src, vcol("conv_w", blk), vcol("conv_w", 8 + blk)))
                chain(dve.tensor_tensor(ymix[:, RB + blk, :], ymix[:, RB + blk, :], proj[:, 8 + blk, :], ALU.mult))
            dve.sem_inc(conv_done, 1)
            for n in range(2):
                dve.wait_ge(four_done, n + 1)
                chain(dve.tensor_copy(ymix[:, RB + 4 + 2 * n:RB + 6 + 2 * n, :], ps[:, n, :].rearrange("p (a t) -> p a t", a=2)))
            dve.sem_inc(mix_done, 1)

            def front(b, q, stage):
                def done(d, ins, name):
                    front_dve[d].done(ins, (q, name))

                def own(d, name):
                    front_dve[d].wait(dve, (q, name), b)

                def products(name, x, e, dst, after):
                    for d in range(2):
                        front_act[d].wait(dve, (q, after), b)
                        for h in range(2):
                            hs = slice(h * HEAD, (h + 1) * HEAD)
                            done(d, dve.tensor_tensor(dst[d][hs, :, hs], chunks_of(x[d][hs, :]), chunks_of(e[d][hs, :]), ALU.mult), f"{name}{h}")

                first, both = q == 0, range(2)
                kkq = kk[:, q * T:(q + 1) * T]
                row = lambda x: x.rearrange("p a t -> p (a t)")
                alpha = lambda: products("a", [kkq, kkq], ex, bdA[q], "eex")
                beta = lambda: products("b", av, en, bdB[q], "en")
                kappa = lambda: products("k", kd, en, bdK[q], "en")

                def rate_key():
                    for d in both:
                        done(d, dve.tensor_tensor(av[d][:, :], av[d][:, :], kkq, ALU.mult), "ba")

                if stage == 1:
                    if first:
                        done(0, dve.tensor_scalar(kq[:, :], kv[:, ds(b, 1), :, :].rearrange("p a q t -> p (a q t)"), vcol("k_k", b), None, ALU.mult), "kq")
                    for d in both:
                        front_act[d].wait(dve, (q, "sg"), b)
                        done(d, dve.tensor_scalar(lw[d][:, :], lw[d][:, :], DECAY_SCALE, None, ALU.mult), "lw")
                    for d in both:
                        own(d, "lw")
                        way = slice(None, None, 1 if d == 0 else -1)
                        done(d, dve.tensor_tensor_scan(L[d][:, way], inside, lw[d][:, way], 0.0, ALU.mult, ALU.add), "L")
                    for d in both:
                        own(d, "L")
                        done(d, dve.tensor_tensor(ex[d][:, :], L[d][:, :], lw[d][:, :], ALU.subtract), "Lx")
                if stage == 2:
                    if first:
                        front_pe[0].wait(dve, (q, "kk"), b)
                        done(0, dve.tensor_scalar(kn[:, :], ps[:, 1, :], KK_EPS * KK_EPS, None, ALU.max), "kv")
                    for d in both:
                        front_act[d].wait(dve, (q, "sa"), b)
                        done(d, dve.tensor_scalar(kd[d][:, :], av[d][:, :], vcol("k_a", b), oka[:, ds(b, 1)], ALU.mult, ALU.add), "kf")
                    for d in both:
                        own(d, "kf")
                        done(d, dve.tensor_tensor(kd[d][:, :], kd[d][:, :], row(kv[:, ds(b, 1), q, :]), ALU.mult), "kd")
                    if not first:
                        rate_key()
                    for d in both:
                        own(d, "kd" if first else "ba")
                step = lambda ins, name: (done(0, ins, name), own(0, name))
                if stage == 3:
                    if first:
                        front_act[0].wait(dve, (q, "ksqrt"), b)
                        done(0, dve.reciprocal(kk[:, 0:T], kk[:, 0:T]), "n0")
                    if not first:
                        done(1, dve.tensor_tensor(kn[:, 0:T], kd[0][:, :], kd[1][:, :], ALU.add), "rk0")
                        own(1, "rk0")
                        done(1, dve.scalar_tensor_tensor(out=kn[:, 0:T], in0=kn[:, 0:T], scalar=vcol("r_k", b), in1=row(r[:, ds(b, 1), :]),
                                                         op0=ALU.mult, op1=ALU.mult), "rk1")
                    kappa()
                    if not first:
                        alpha()
                if stage == 4:
                    if first:
                        step(dve.reciprocal(kk[:, T:2 * T], kk[:, T:2 * T]), "n1")
                        step(dve.tensor_tensor(knt[:, :], kk[:, :], kk[:, :], ALU.mult), "n2")
                        step(dve.tensor_tensor(knt[:, :], knt[:, :], kn[:, :], ALU.mult), "n3")
                    else:
                        beta()
                        for d in both:
                            front_act[d].wait(dve, (q, "ep"), b)
                            done(d, dve.tensor_tensor(bdA[q][d][:, :, P:P + C], chunks_of(row(r[:, ds(b, 1), :])), chunks_of(L[d][:, :]), ALU.mult), "rho")
                if stage == 5:
                    if first:
                        step(dve.tensor_scalar(knt[:, :], knt[:, :], -0.5, 1.5, ALU.mult, ALU.add), "n4")
                        step(dve.tensor_tensor(kk[:, :], kk[:, :], knt[:, :], ALU.mult), "n5")
                        step(dve.tensor_tensor(kk[:, :], kk[:, :], kq[:, :], ALU.mult), "kk")
                        rate_key()
                        alpha()
                        own(0, "ba")
                        own(1, "ba")
                        beta()
                    else:
                        own(0, "rho")
                        own(1, "rho")
                        front_pe[1].wait(dve, (q, "rk"), b)
                        done(1, dve.tensor_tensor(row(r[:, ds(b, 1), :]), ps[:, 5, 0:T], row(kv[:, ds(b + RB, 1), q, :]), ALU.mult), "bonus")

            def group_norm(b, stage):
                y, bonus = (x[:, ds(b, 1), :].rearrange("p a t -> p (a t)") for x in (ymix, r))
                step = lambda ins, name: (gnd.done(ins, name), gnd.wait(dve, name, b))
                if stage == 2:
                    gnp.wait(dve, "mean", b)
                    gnd.done(dve.scalar_tensor_tensor(out=y, in0=ps[:, 1, 0:T], scalar=-1.0 / HEAD, in1=y, op0=ALU.mult, op1=ALU.add), "c")
                if stage == 4:
                    gnp.wait(dve, "gate", b)
                    gnd.done(dve.tensor_scalar(gvar[:, :], ps[:, 1, T:2 * T], 1.0 / HEAD, GN_EPS, ALU.mult, ALU.add), "v")
                if stage == 5:
                    gna.wait(dve, "sqrt", b)
                    step(dve.reciprocal(gn[:, :], gn[:, :]), "n0")
                    step(dve.tensor_tensor(gsq[:, :], gn[:, :], gn[:, :], ALU.mult), "n1")
                    step(dve.tensor_tensor(gsq[:, :], gsq[:, :], gvar[:, :], ALU.mult), "n2")
                    step(dve.tensor_scalar(gsq[:, :], gsq[:, :], -0.5, 1.5, ALU.mult, ALU.add), "n3")
                    step(dve.tensor_tensor(gn[:, :], gn[:, :], gsq[:, :], ALU.mult), "n4")
                    step(dve.tensor_tensor(gn[:, :], gn[:, :], y, ALU.mult), "yn")
                    step(dve.tensor_scalar(gn[:, :], gn[:, :], vcol("ln_w", b), vcol("ln_b", b), ALU.mult, ALU.add), "w")
                    step(dve.tensor_tensor(gn[:, :], gn[:, :], bonus, ALU.add), "b")
                    step(dve.tensor_tensor(y, gn[:, :], ps[:, 1, 0:T], ALU.mult), "g")

            def unit(b, q, ahead=True, norm=None):
                def done(d, ins, name):
                    scan_dve[d].done(ins, (q, name))

                def own(d, name):
                    scan_dve[d].wait(dve, (q, name), b)

                w = P + C * q
                bank = lambda d, n: ps[:, 4 * d + n, :].rearrange("p (c n) -> p c n", c=NC)
                for d in range(2):
                    if q == 0:
                        done(d, dve.memset(S[d][:, :], 0.0), "S")
                    else:
                        front_pe[d].wait(dve, (q, "G1"), b)
                        done(d, dve.tensor_tensor(in_pairs(tokBQ[d][:, :, P:P + C]), two_banks(4 * d, w, P, C), over_banks(upto[d]), ALU.mult), "Q")
                for d in range(2):
                    scan_pe[d].wait(dve, (q, "G2"), b)
                    if q:
                        done(d, dve.tensor_tensor(in_pairs(RT[d][:, :, :]), two_banks(4 * d + 2, w, P, C), over_banks(upto[d]), ALU.mult), "R")
                    done(d, dve.tensor_tensor(in_pairs(MT[d][:, :, :]), two_banks(4 * d + 2, w, 0, P), over_banks(strict[d]), ALU.mult), "M")
                for d in range(2):
                    scan_pe[d].wait(dve, (q, "tK"), b)
                    done(d, dve.tensor_copy(tokK[d][:, :, :], bank(d, 2)), "oK")
                    if d == 0:
                        scan_pe[d].wait(dve, (q, "tV"), b)
                        done(d, dve.tensor_copy(tokV[:, :, :], bank(d, 3)), "oV")
                for d in range(2):
                    scan_pool[d].wait(dve, (q, "m0"), b)
                    scan_pe[d].wait(dve, (q, "L0"), b)
                    done(d, dve.tensor_tensor(XT[q][d][:, :, :], over_chunks(ident), ULa[d][:, :, :], ALU.subtract), "T0")
                    done(d, dve.tensor_tensor(XY[d][:, :, 0, :], over_chunks(ident), bank(d, 1), ALU.subtract), "X0")
                for l in FRONT:
                    for d in range(2):
                        if l < LEVELS - 1:
                            scan_pe[d].wait(dve, (q, f"X{l}"), b)
                            done(d, dve.tensor_tensor(XY[d][:, :, 0, :], XY[d][:, :, 0, :], bank(d, 3), ALU.subtract), f"X{l}")
                        scan_pe[d].wait(dve, (q, f"T{l}"), b)
                        done(d, dve.tensor_tensor(XT[q][d][:, :, :], XT[q][d][:, :, :], bank(d, 0), ALU.subtract), f"T{l}")
                    if ahead:
                        front(*following(b, q), l)
                    if norm is not None:
                        group_norm(norm, l)
                y = ymix[:, ds(b, 1), :].rearrange("p a t -> p (a t)")
                for d in range(2):
                    scan_pe[d].wait(dve, (q, "A"), b)
                    done(d, dve.tensor_tensor(in_pairs(AT[d][:, :, :]), two_banks(4 * d, w, 0, P), over_banks(ident), ALU.add), "AT")
                    if q:
                        rho = in_pairs(bdA[q][d][:, :, P:P + C])
                        done(d, dve.tensor_tensor(rho, two_banks(4 * d, w, P, C), rho, ALU.add), "rho2")
                    scan_pe[d].wait(dve, (q, "B"), b)
                    done(d, dve.tensor_tensor(BM[q][d][:, :, :], bank(d, 2),
                                              pc[q][d][:, :].rearrange("p (c n) -> p c n", n=1).broadcast_to([P, NC, P]), ALU.mult), "Bm")
                    if q and d == 0:
                        done(d, dve.tensor_copy(y, ps[:, 3, 0:T]), "Y0")
                    elif q:
                        own(0, "Y0")
                        done(d, dve.tensor_tensor(y, ps[:, 7, 0:T], y, ALU.add), "Y0")
                for n in range(NC - q):
                    for d in range(2):
                        c = in_order(d)[n]
                        scan_pe[d].wait(dve, (q, f"st{n}"), b)
                        own(d, f"s{n - 1}" if n else "Bm")
                        done(d, dve.scalar_tensor_tensor(out=S[d][:, :], in0=ps[:, 4 * d + 2, c * P:(c + 1) * P], scalar=pc[q][d][:, c:c + 1],
                                                         in1=BM[q][d][:, c, :], op0=ALU.mult, op1=ALU.add), f"s{n}")
                if q:
                    for d in range(2):
                        scan_pe[d].wait(dve, (q, f"st{NC - 1}"), b)
                        scan_dve[1 - d].wait(dve, (q, "y" if d else "Y0"), b)
                        done(d, dve.tensor_tensor(y, ps[:, 4 * d + 3, T:2 * T], y, ALU.add), "y")

            dve.wait_ge(lam_exp, 2)
            lw1, e1, w1, w2, s1 = (lcol[:, n, :] for n in range(1, 6))
            chain(dve.tensor_scalar(w1, e1, 2.0, None, ALU.add))
            chain(dve.reciprocal(w1, w1))
            chain(dve.tensor_tensor(w1, w1, e1, ALU.mult))
            chain(dve.tensor_tensor(w2, w1, w1, ALU.mult))
            chain(dve.tensor_scalar(s1, w2, 1.0 / 17, None, ALU.mult))
            for n in range(15, 1, -2):
                chain(dve.scalar_tensor_tensor(out=s1, in0=s1, scalar=1.0 / n, in1=w2, op0=ALU.add, op1=ALU.mult))
            chain(dve.scalar_tensor_tensor(out=s1, in0=s1, scalar=1.0, in1=w1, op0=ALU.add, op1=ALU.mult))
            chain(dve.tensor_scalar(e1, vcol("lru_lambda_2", 0, RB), 0.0, LRU_C / 2, ALU.min, ALU.mult))
            dve.scalar_tensor_tensor(out=lw1, in0=s1, scalar=-LRU_C, in1=e1, op0=ALU.mult, op1=ALU.add).then_inc(lam_ready, 1)
            chain(dve.tensor_scalar(oka, vcol("k_a", 0, RB), -1.0, 1.0, ALU.mult, ALU.add))
            dve.wait_ge(kscan_in, 16)
            dve.wait_ge(bd_clear, 13)
            for stage in FRONT:
                front(0, 0, stage)
            unit(0, 0)
            with dve.Fori(0, RB - 1) as b:
                unit(b, 1)
                unit(b + 1, 0, norm=b)
            unit(RB - 1, 1, ahead=False)
            dve.sem_inc(scan_done, 1)
            for stage in FRONT:
                group_norm(RB - 1, stage)
            dve.sem_inc(ymix_done, 1)
            for at_n, n in enumerate((0, 2, 3, 1)):
                dve.wait_ge(yhi, at_n + 1)
                dve.tensor_tensor(mov[:, 4 * n:4 * n + 4, 1, :], ymix[:, 4 * n:4 * n + 4, :], mov[:, 4 * n:4 * n + 4, 0, :].bitcast(F32), ALU.subtract)\
                   .then_inc(ylo, 1)
            def add_squares(ph, i, p, n):
                per = SUM_STEPS[ph.name]
                before = i * (ph.pairs * per) + (SUMS0[ph.name] + 1 + p * per)
                pair = xT[:, ds(n, 2), :]
                dve.tensor_tensor(sq_pair, pair, pair, ALU.mult).then_inc(sums_ready, 1)
                dve.wait_ge(sums_ready, before + 1)
                dve.tensor_tensor(sums, sums, sq_pair, ALU.add).then_inc(sums_ready, 1)
                if ph.name == "down":
                    for blk in range(2):
                        dve.scalar_tensor_tensor(out=sums_w, in0=sq_pair[:, blk, :], scalar=gain[:, 0, ds(n + blk, 1)], in1=sums_w,
                                                 op0=ALU.mult, op1=ALU.add).then_inc(sums_ready, 1)
                        dve.wait_ge(sums_ready, before + (3 + blk))
                else:
                    dve.wait_ge(sums_ready, before + 2)

            def residual(ph, part):
                def evacuate(i, p):
                    summed(ph, i, p, px[:, :, :]).then_inc(bank_free, 1)
                    dve.wait_ge(bank_free, ph.pair(i, p) + (1 + BANK_CREDIT))
                    n = i * (2 * ph.pairs) + 2 * p
                    if ph.name == "out":
                        dve.wait_ge(x_back, 16)
                    if part is None:
                        chain(dve.tensor_tensor(xT[:, ds(n, 2), :], px[:, :, :], xT[:, ds(n, 2), :], ALU.add))
                        add_squares(ph, i, p, n)
                        return
                    for blk in range(2):
                        ins = dve.scalar_tensor_tensor(out=xT[:, ds(n + blk, 1), :], in0=px[:, blk:blk + 1, :], scalar=modcol(part, 0, n + blk),
                                                       in1=xT[:, ds(n + blk, 1), :], op0=ALU.mult, op1=ALU.add)
                        mark = chain.mark(ins)
                    chain.wait(mark)
                    add_squares(ph, i, p, n)
                return evacuate, ph.pairs * (1 if part is None else 2)

            def add_residual(name, part):
                if name == "down":
                    final = vcol("norm_final", 0, KB)
                    chain(dve.tensor_tensor(gain[:, 0, :], final, final, ALU.mult))
                    chain(dve.tensor_tensor(gain[:, 1, :], final, vcol("ln1_w_2", 0, KB), ALU.mult))
                dve.memset(sq[:, :, :], 0.0).then_inc(sums_ready, 1)
                dve.wait_ge(sums_ready, SUMS0[name] + 1)
                if PH[name] is order[-1]:
                    last_residual(PH[name])
                else:
                    gemm(PH[name], *residual(PH[name], part))
                dve.sem_inc(x_done, 1)

            def last_residual(ph):
                def evacuate(i, p):
                    summed(ph, i, p, px[:, :, :]).then_inc(bank_free, 1)
                    dve.wait_ge(bank_free, ph.pair(i, p) + (1 + BANK_CREDIT))
                    n = i * (2 * ph.pairs) + 2 * p
                    dve.tensor_tensor(xT[:, ds(n, 2), :], px[:, :, :], xT[:, ds(n, 2), :], ALU.add).then_inc(res_done, 1)
                    dve.wait_ge(res_done, i * ph.pairs + (p + 1))
                    add_squares(ph, i, p, n)
                gemm(ph, evacuate)

            def gated(e, ph):
                before = e * PH["ffn"].trips
                def evacuate(i, p):
                    if p == 0:
                        summed(ph, i, p, gbuf[:, :, :]).then_inc(bank_free, 1)
                        return
                    dve.wait_ge(ffn_lo, i + (before + 1))
                    summed(ph, i, p, ubuf[:, :, :]).then_inc(bank_free, 1)
                    dve.wait_ge(bank_free, ph.pair(i, p) + (1 + BANK_CREDIT))
                    dve.wait_ge(ffn_s, i + (before + 1))
                    dve.tensor_tensor(ubuf[:, :, :], sbuf[:, :, :], ubuf[:, :, :], ALU.mult).then_inc(ffn_h, 1)
                    dve.wait_ge(ffn_hi, i + (before + 1))
                    dve.tensor_tensor(hid[:, ds(i * 2, 2), 1, :], ubuf[:, :, :], hid[:, ds(i * 2, 2), 0, :].bitcast(F32), ALU.subtract)\
                       .then_inc(ffn_lo, 1)
                return evacuate

            def norm_and_ffn(e, stat, norm, g, shift, suffix, gate_part):
                variance(stat, T)
                normed(norm, (lambda k: xT[:, ds(k, 1), :], g, rstd[:, 0, :], shift,
                              lambda k: mov[:, ds(k, 1), 0, :], lambda k: mov[:, ds(k, 1), 1, :]))
                gemm(PH["ffn" + suffix], gated(e, PH["ffn" + suffix]))
                add_residual("down" + suffix, gate_part)

            dve.sem_inc(ffn_lo, 1)
            add_residual("out", 2)
            norm_and_ffn(0, 1, 2, lambda k: gain[:, 2, ds(k, 1)], lambda k: modcol(3, 0, k), "", 5)

            def scale_block(name, k):
                dve.scalar_tensor_tensor(out=xT[:, ds(k, 1), :], in0=xT[:, ds(k, 1), :], scalar=vcol(name, k), in1=rstd[:, 0:1, :],
                                         op0=ALU.mult, op1=ALU.mult).then_inc(x_scaled, 1)

            def in_2(i, p):
                summed(PH["in_2"], i, p, p2[:, ds(i * 4 + 2 * p, 2), :]).then_inc(bank_free, 1)
                for blk in range(2):
                    scale_block("norm_final", i * 4 + (2 * p + blk))

            variance(2, T)
            variance(3, T)
            chain(dve.tensor_tensor(rstd[:, 1, :], rstd[:, 1, :], rstd[:, 0, :], ALU.mult))
            normed(3, (lambda k: xT[:, ds(k, 1), :], lambda k: gain[:, 1, ds(k, 1)], rstd[:, 1, :], None,
                       lambda k: mov[:, ds(k, 1), 0, :], lambda k: mov[:, ds(k, 1), 1, :]))
            gemm(PH["in_2"], in_2)
            dve.wait_ge(x_scaled, KB)

            def lru(h, j):
                step = lambda ins, name: (lrud.done(ins, name), lrud.wait(dve, name, h))
                if j == 0:
                    lrua.wait(dve, "u", h)
                    for tap in (2, 1, 0):
                        lag = 3 - tap
                        step(dve.scalar_tensor_tensor(out=lu[:, lag:T], in0=one(p2, h + LX)[:, 0:T - lag], scalar=vcol("conv_w_2", h + tap * RB),
                                                      in1=lu[:, lag:T], op0=ALU.mult, op1=ALU.add), f"c{tap}")
                if j == 1:
                    lg = one(p2, h + LG)
                    step(dve.scalar_tensor_tensor(out=gq[:, :], in0=lg, scalar=0.044715 * GELU, in1=lg, op0=ALU.mult, op1=ALU.mult), "x3")
                    step(dve.scalar_tensor_tensor(out=gq[:, :], in0=gq[:, :], scalar=GELU, in1=lg, op0=ALU.add, op1=ALU.mult), "z")
                if j == 4:
                    lrua.wait(dve, "t", h)
                    step(dve.tensor_scalar(li[:, :], la[:, :], -1.0, 1.0, ALU.mult, ALU.add), "om")
                    step(dve.reciprocal(li[:, :], li[:, :]), "inv")
                    lrud.done(dve.scalar_tensor_tensor(out=lA[:, :], in0=la[:, :], scalar=1.0, in1=li[:, :], op0=ALU.add, op1=ALU.mult), "a")
                if j == 6:
                    lrug.wait(dve, "b2", h)
                    lrud.wait(dve, "a", h)
                    lrud.done(dve.tensor_tensor_scan(lu[:, :], lA[:, :], lb[:, :], 0.0, ALU.mult, ALU.add), "h")
                    lrua.wait(dve, "gt", h)
                    step(dve.scalar_tensor_tensor(out=gz[:, :], in0=gz[:, :], scalar=1.0, in1=one(p2, h + LG), op0=ALU.add, op1=ALU.mult), "hg")
                    step(dve.scalar_tensor_tensor(out=one(p2, h + LX), in0=lu[:, :], scalar=0.5, in1=gz[:, :], op0=ALU.mult, op1=ALU.mult), "y")

            def retention(h, j):
                step = lambda ins, name: (retd.done(ins, name), retd.wait(dve, name, h))
                if j == 2:
                    retp.wait(dve, "sw", h)
                    retd.done(dve.tensor_tensor(rqk[:, :, :], ps[:, 5, :].rearrange("p (a t) -> p a t", a=2), both(rsin), ALU.mult), "qs")
                    retd.wait(dve, "qs", h)
                    retg.wait(dve, "qc", h)
                    retd.done(dve.tensor_tensor(rqk[:, :, :], rqk[:, :, :], rqc[:, :, :], ALU.add), "qr")
                if j == 3:
                    retp.wait(dve, "sc", h)
                    retd.done(dve.tensor_tensor(rp[:, :], ps[:, 6, 0:T + P], kret[:, ds(h * (T + P) + (2 * T + 2 * P), T + P)], ALU.mult), "pr")
                if j == 6:
                    retp.wait(dve, "var", h)
                    retd.done(dve.tensor_scalar(rvar[:, :], ps[:, 7, T:2 * T], 1.0 / P, RMS_EPS, ALU.mult, ALU.add), "v")
                if j == 7:
                    reta.wait(dve, "sqrt", h)
                    step(dve.reciprocal(ron[:, :], ron[:, :]), "n0")
                    step(dve.tensor_tensor(rsq[:, :], ron[:, :], ron[:, :], ALU.mult), "n1")
                    step(dve.tensor_tensor(rsq[:, :], rsq[:, :], rvar[:, :], ALU.mult), "n2")
                    step(dve.tensor_scalar(rsq[:, :], rsq[:, :], -0.5, 1.5, ALU.mult, ALU.add), "n3")
                    step(dve.tensor_tensor(ron[:, :], ron[:, :], rsq[:, :], ALU.mult), "n4")
                    step(dve.tensor_tensor(ron[:, :], ps[:, 5, 0:T], ron[:, :], ALU.mult), "on")
                    step(dve.tensor_scalar(ron[:, :], ron[:, :], vcol("ret_gn_w_2", h), None, ALU.mult), "w")
                    retg.wait(dve, "sgm", h)
                    step(dve.tensor_tensor(one(p2, h + RB), ron[:, :], rsg[:, :], ALU.mult), "y")

            def side(h, j):
                lru(h, j)
                if not (isinstance(h, int) and h == 0):
                    retention(h - 1, j)

            def heads_out(i, p):
                ph = PH["in_2_heads"]
                b, t = ph.bank(p), (ph.p0 + p) % 2
                dve.wait_ge(tmp_ready, ph.pair(i, p) + (1 - LOWS0))
                dve.tensor_tensor(head_pair(p, i), ps[:, b:b + 2, 0:T].rearrange("p a (o t) -> p a o t", o=1),
                                  tmp[:, t, :, :].rearrange("p a (o t) -> p a o t", o=1), ALU.add).then_inc(bank_free, 1)

            def y_lo(n):
                dve.wait_ge(y2_hi, n + 1)
                dve.tensor_tensor(mov[:, 4 * n:4 * n + 4, 1, :], p2[:, 4 * n:4 * n + 4, :], mov[:, 4 * n:4 * n + 4, 0, :].bitcast(F32), ALU.subtract)\
                   .then_inc(y2_lo, 1)

            dve.wait_ge(kret_in, 16)
            gemm(PH["in_2_heads"], heads_out, side=side)
            dve.wait_ge(bank_free, trip_out(RET_HEADS - 1))
            for j in range(8):
                retention(RET_HEADS - 1, j)
                if j in (3, 6):
                    y_lo(j // 3 - 1)
            y_lo(2)
            y_lo(3)
            add_residual("out_2", None)
            norm_and_ffn(1, 4, 4, lambda k: vcol("ln2_w_2", k), None, "_2", None)
            variance(5, T)
            def row_out(n):
                dve.wait_ge(row_turned, n + 1)
                dve.tensor_copy(orow[:, n % 2, (n // 2) * BANK:(n // 2 + 1) * BANK], ps[:, n, :]).then_inc(row_dve, 1)
            for n in range(1, 8, 2):
                for k in range(4 * (n // 2), 4 * (n // 2 + 1)):
                    scale_block("final_norm_w_2", k)
                if n > 1:
                    row_out(n - 2)
            row_out(7)

        @block.tensor
        def _(pe):
            pe.sem_inc(split_free, SPLIT_CREDIT)

            def gemm(ph, product, ready=None, after=None, chunk=None):
                def trip(i):
                    for j, (side, p, c) in enumerate(ph.order):
                        if c == 0 and side:
                            pe.wait_ge(side_free, ph.side(i, p))
                        elif c == 0:
                            pe.wait_ge(bank_free, ph.pair(i, p) + 1)
                        pe.wait_ge(lo_ready, ph.chunk(i, j) + (1 + RING))
                        if ready and p == 0 and not side:
                            pe.wait_ge(*ready(c))
                        for kk in range(CK if not chunk else 0):
                            k = c * CK + kk
                            if side:
                                mm = mod_rows(4 + 2 * (p % 2), ph.slot(j), kk, k, k == 0, k == ph.rows - 1)
                            else:
                                mm = product(p, ph.slot(j), kk, k, k == 0, k == ph.rows - 1)
                        if chunk:
                            mm = chunk(p, ph.slot(j), c)
                        mm.then_inc(split_free, 1)
                        if after:
                            after(i, j)
                loop(pe, ph, trip, peel=chunk)

            def on_x(ph, moving):
                def product(p, s, kk, k, first, last):
                    for blk in range(2):
                        b, w = ph.bank(p) + blk, slice(blk * P, (blk + 1) * P)
                        pe.matmul(ps[:, b, :], hi[:, s, kk, w], moving(k, None), start=first, stop=False)
                        mm = pe.matmul(ps[:, b, 0:T], lo[:, s, kk, w], moving(k, 0), start=False, stop=last)
                    return mm
                return product

            def on_both(ph, widths):
                def product(p, s, kk, k, first, last):
                    for blk in range(2):
                        b, w = ph.bank(p) + blk, slice(blk * widths, (blk + 1) * widths)
                        pe.matmul(ps[0:widths, b, :], hi[:, s, kk, w], mov1[:, k, 0, :, :], start=first, stop=False)
                        pe.matmul(ps[0:widths, b, :], hi[:, s, kk, w], mov1[:, k, 1, :, :], start=False, stop=False)
                        mm = pe.matmul(ps[0:widths, b, :], lo[:, s, kk, w], mov1[:, k, 0, :, :], start=False, stop=last)
                    return mm
                return product

            def sums_of_squares(name):
                pe.wait_ge(sums_ready, SUMS0[name] + 1 + RESIDUAL_PAIRS * SUM_STEPS[name])
                for blk in range(2):
                    mm = pe.matmul(ps[:, 7, 0:T], ones, sums[:, blk, :], start=(blk == 0), stop=(blk == 1))
                mm.then_inc(sq_used, 1)
                if name == "down":
                    pe.matmul(ps[:, 7, T:2 * T], ones, sums_w[:, :], start=True, stop=True).then_inc(sq_used, 1)

            pe.wait_ge(const_in, 16)
            pe.wait_ge(c_in, 32)
            pe.transpose(ps[:, 0, 0:2 * KB], cvec[:, :], ident[0:2 * KB, 0:2 * KB]).then_inc(c_turned, 1)
            pe.wait_ge(c4_ready, 2)

            def mod_rows(b, s, kk, k, first, last):
                pe.matmul(ps[0:32, b, 0:CN], c4[:, k, :], hi[:, s, kk, :], start=first, stop=False)
                return pe.matmul(ps[0:32, b, 0:CN], c4[:, k, :], lo[:, s, kk, :], start=False, stop=last)

            def turn(p):
                if p == VEC_AT:
                    for which in range(2):
                        pe.wait_ge(vec_in[which], 16 * VEC_DMAS[which])
                    for t in range(4):
                        mm = pe.transpose(ps[:, 5, t * P:(t + 1) * P], vrow[:, t, :], ident)
                    mm.then_inc(vec_turned, 1)
                if p == TURN0:
                    pe.wait_ge(row_in, 32)
                for k in range(2 * (p - TURN0), 2 * (p - TURN0) + 2):
                    if k in turned_at(p):
                        if k >= 4:
                            pe.wait_ge(sq_ready, k - 3)
                            pe.wait_ge(x_out, k - 3)
                        for a, src in enumerate((crow, xrow)):
                            for h in range(2):
                                mm = pe.transpose(ps[:, TURN[k % 4], (2 * a + h) * P:(2 * a + h + 1) * P],
                                                  src[:, h, k * P:(k + 1) * P], ident)
                        mm.then_inc(turned, 1)
                    if 0 <= k - 2 < KB:
                        pe.wait_ge(sq_ready, k - 1)
                        pe.matmul(ps[:, 7, :], ones, sq[:, k % 2, :], start=(k == 2), stop=(k == KB + 1)).then_inc(sq_used, 1)

            def mod_columns(i, j):
                done = PH["mod"].completed(j)
                if done:
                    turn(done[1])
                if not done or done[1] % 8 < 7:
                    return
                pe.wait_ge(bank_free, PH["mod"].pair(i, done[1]) + (1 + BANK_CREDIT))
                pe.wait_ge(vec_ready, 1)
                for k in range(KB):
                    mm = pe.matmul(ps[:, 5, 2 * k:2 * k + 2], mrow[:, k * P:(k + 1) * P], sel[0:4, 0:2], start=True, stop=True)
                mm.then_inc(mcol_ready, 1)
            gemm(PH["mod"], lambda p, *a: mod_rows(PH["mod"].bank(p), *a), after=mod_columns)
            def side_columns(ph):
                def columns(i, j):
                    done = ph.completed(j - 1) if j else None
                    if done and done[0]:
                        m = done[1]
                        pe.wait_ge(side_free, ph.side(i, m) + BANK_CREDIT)
                        pe.wait_ge(mod_ready, ph.side(i, m) + 3)
                        for blk in range(2):
                            mm = pe.matmul(ps[:, 5, 2 * blk:2 * blk + 2], mrow2[:, m % 2, blk * P:(blk + 1) * P], sel[0:4, 0:2], start=True, stop=True)
                        mm.then_inc(mcol_ready, 1)
                return columns

            normed_x = lambda k, h: mov1[:, k, :, 1, :] if h is None else mov1[:, k, h, 1, :]
            gemm(PH["in_kv"], on_both(PH["in_kv"], P), after=side_columns(PH["in_kv"]),
                 ready=lambda c: (mov_ready, 2 * (c + 1) * CK))
            lora_both, lora_x = on_both(PH["in_lora"], LORA), on_x(PH["in_lora"], normed_x)
            gemm(PH["in_lora"], lambda p, *a: (lora_both, lora_x)[p](p, *a))
            gemm(PH["in_r"], on_x(PH["in_r"], normed_x))
            gemm(PH["in_rest"], on_x(PH["in_rest"], normed_x), after=side_columns(PH["in_rest"]))
            pe.wait_ge(bank_free, REST_OUT)
            pe.wait_ge(mod_ready, 4 + 32)
            pe.wait_ge(four_in, 16)
            for n in range(4):
                h = n // 2
                for blk in range(2 * (n % 2), 2 * (n % 2) + 2):
                    mm = pe.matmul(ps[:, 4 + n, (blk % 2) * T:(blk % 2 + 1) * T], proj[:, 12 + blk, h * P:(h + 1) * P], kfour[:, 0, :],
                                   start=True, stop=True)
                mm.then_inc(uf_turned, 1)
            pe.wait_ge(uf_ready, 4)
            for blk in range(4):
                for n, (h, cs) in enumerate((h, cs) for h in range(2) for cs in range(2)):
                    mm = pe.matmul(ps[:, blk // 2, (blk % 2) * T:(blk % 2 + 1) * T], uf[:, h, blk, cs, :], kfour[:, 1 + 2 * h + cs, :],
                                   start=(n == 0), stop=(n == 3))
                if blk % 2:
                    mm.then_inc(four_done, 1)

            def each(sem_of, d, name, bank, lhs, rhs, n=P, paired=False):
                for c in range(NC):
                    if paired:
                        o = ps[:, 4 * d + bank + c // 2, (c % 2) * n:(c % 2 + 1) * n]
                    else:
                        o = ps[:, 4 * d + bank, c * n:(c + 1) * n]
                    mm = lhs(c, o) if rhs is None else pe.matmul(o, lhs(c), rhs(c), start=True, stop=True)
                if name:
                    sem_of[d].done(mm, name)

            def two(d, name, bank, lhs1, rhs1, lhs2, rhs2, n):
                for c in range(NC):
                    o = ps[:, 4 * d + bank, c * n:(c + 1) * n]
                    pe.matmul(o, lhs1(c), rhs1(c), start=True, stop=False)
                    mm = pe.matmul(o, lhs2(c), rhs2(c), start=False, stop=True)
                if name:
                    scan_pe[d].done(mm, name)

            def front(b, q, stage):
                first = q == 0
                if stage == 1:
                    pe.wait_ge(decw_in, b * 32 + 32)
                    for d in range(2):
                        for n in range(2):
                            mm = pe.matmul(ps[:, 4 * d + 1, n * T:(n + 1) * T], decw[0:LORA, 2 * n + d, :], wdad[0:LORA, n, q, :], start=True, stop=True)
                        front_pe[d].done(mm, (q, "zz"))
                if stage == 2 and first:
                    front_act[0].wait(pe, (q, "ksq"), b)
                    front_pe[0].done(pe.matmul(ps[:, 1, :], blk64, kn[:, :], start=True, stop=True), (q, "kk"))
                if stage == 5 and not first:
                    front_dve[1].wait(pe, (q, "rk1"), b)
                    front_act[1].wait(pe, (q, "sa"), b)
                    front_pe[1].done(pe.matmul(ps[:, 5, 0:T], blk64, kn[:, 0:T], start=True, stop=True), (q, "rk"))

            def front_out(b, q):
                for d in range(2):
                    front_act[d].wait(pe, (q, "sa"), b)
                if q == 0:
                    front_dve[0].wait(pe, (q, "kv"), b)
                else:
                    front_dve[1].wait(pe, (q, "bonus"), b)

            def gram(b, q, d):
                w = P + C * q
                front_dve[d].wait(pe, (q, "rho" if q else "b1"), b)
                each(front_pe, d, (q, "G1"), 0, lambda c: bdB[q][d][:, c, :], lambda c: bdA[q][d][:, c, 0:w], w, paired=True)

            def group_norm(b, stage):
                if stage == 2:
                    gnp.done(pe.matmul(ps[:, 1, 0:T], blk64, ymix[:, ds(b, 1), :], start=True, stop=True), "mean")
                if stage == 4:
                    gna.wait(pe, "sq", b)
                    gnp.done(pe.matmul(ps[:, 1, T:2 * T], blk64, gsq[:, :], start=True, stop=True), "var")
                    pe.wait_ge(gup_in, b * 16 + 16)
                    for k in range(2):
                        mm = pe.matmul(ps[:, 1, 0:T], gup[:, k, :], gd[:, k, :], start=(k == 0), stop=(k == 1))
                    gnp.done(mm, "gate")

            def unit(b, q, ahead=True, norm=None):
                w = P + C * q
                if q:
                    for d in range(2):
                        scan_dve[d].wait(pe, (0, f"s{NC - 1}"), b)
                for d in range(2):
                    each(scan_pe, d, (q, "G2"), 2, lambda c: bdK[q][d][:, c, :], lambda c: bdA[q][d][:, c, 0:w], w, paired=True)
                for d in range(2):
                    act, dve = scan_act[d], scan_dve[d]
                    act.wait(pe, (q, "U"), b)
                    each(scan_pe, d, (q, "tA"), 0, lambda c, o: pe.transpose(o, bdA[q][d][:, c, 0:P], ident), None)
                    each(scan_pe, d, (q, "tB"), 1, lambda c, o: pe.transpose(o, bdB[q][d][:, c, :], ident), None)
                    dve.wait(pe, (q, "M"), b)
                    each(scan_pe, d, (q, "tK"), 2, lambda c, o: pe.transpose(o, bdK[q][d][:, c, :], ident), None)
                    if d == 0:
                        front_act[0].wait(pe, (q, "bv1"), b)
                        each(scan_pe, d, (q, "tV"), 3, lambda c, o: pe.transpose(o, bdV[:, c, :], ident), None)
                for d in range(2):
                    scan_dve[0].wait(pe, (q, "oV"), b)
                    scan_act[d].wait(pe, (q, "oB"), b)
                    each(scan_pe, d, (q, "MV"), 0, lambda c: MT[d][:, c, :], lambda c: tokV[:, c, :])
                    scan_pool[d].wait(pe, (q, "m0"), b)
                    each(scan_pe, d, (q, "L0"), 1, lambda c, o: pe.transpose(o, ULa[d][:, c, :], ident), None)
                for l in FRONT:
                    lev = (ULa, MT)[l % 2]
                    for d in range(2):
                        scan_pool[d].wait(pe, (q, f"m{l}"), b)
                        scan_dve[d].wait(pe, (q, f"T{l - 1}" if l > 1 else "X0"), b)
                        each(scan_pe, d, (q, f"Y{l}"), 2, lambda c: lev[d][:, c, :], lambda c: XY[d][:, c, 0, :])
                    if ahead:
                        front(*following(b, q), l)
                    if norm is not None:
                        if l == 2:
                            front_act[0].wait(pe, (1, "sa"), b)
                        group_norm(norm, l)
                    for d in range(2):
                        scan_act[d].wait(pe, (q, f"Yb{l}"), b)
                        if l == 1:
                            scan_act[d].wait(pe, (q, "oMV"), b)
                        if l < LEVELS - 1:
                            each(scan_pe, d, (q, f"X{l}"), 3, lambda c: XT[q][d][:, c, :], lambda c: XY[d][:, c, 1, :])
                        each(scan_pe, d, (q, f"T{l}"), 0, lambda c: XY[d][:, c, 1, :], lambda c: XT[q][d][:, c, :])
                for d in range(2):
                    scan_dve[d].wait(pe, (q, f"T{LEVELS - 1}"), b)
                    each(scan_pe, d, (q, "Z"), 2, lambda c: XT[q][d][:, c, :], lambda c: tokR[d][:, c, :, :], 2 * P, paired=True)
                if ahead:
                    front_out(*following(b, q))
                if norm is not None:
                    gnd.wait(pe, "g", norm)
                for d in range(2):
                    scan_act[d].wait(pe, (q, "Z"), b)
                    each(scan_pe, d, (q, "A"), 0, lambda c: XY[d][:, c, 0, :], lambda c: tokBQ[d][:, c, 0:w], w, paired=True)
                    two(d, None if q else (q, "B"), 2, lambda c: tokK[d][:, c, :], lambda c: tokV[:, c, :],
                        lambda c: tokBQ[d][:, c, 0:P], lambda c: XY[d][:, c, 1, :], P)
                    if q:
                        two(d, (q, "B"), 3, lambda c: tokV[:, c, :], lambda c: RT[d][:, c, :],
                            lambda c: XY[d][:, c, 1, :], lambda c: tokBQ[d][:, c, P:P + C], C)
                for n in range(NC):
                    for d in range(2):
                        c = in_order(d)[n]
                        scan_dve[d].wait(pe, (q, f"s{n - 1}" if n else "Y0" if q else "Bm"), b)
                        if q:
                            mm = pe.matmul(ps[:, 4 * d + 3, T + c * C:T + (c + 1) * C], S[d][:, :], bdA[q][d][:, c, P:P + C], start=True, stop=True)
                        if n < NC - q:
                            mm = pe.matmul(ps[:, 4 * d + 2, c * P:(c + 1) * P], AT[d][:, c, :], S[d][:, :], start=True, stop=True)
                        scan_pe[d].done(mm, (q, f"st{n}"))
                    if ahead and n < 2:
                        gram(*following(b, q), n)
                if q:
                    for d in range(2):
                        scan_dve[d].wait(pe, (1, "y"), b)

            pe.wait_ge(gd_ready, 1)
            pe.wait_ge(wd_ready, 1)
            pe.wait_ge(mix_done, 1)
            for stage in FRONT:
                front(0, 0, stage)
            front_out(0, 0)
            for d in range(2):
                gram(0, 0, d)
            unit(0, 0)
            with pe.Fori(0, RB - 1) as b:
                unit(b, 1)
                unit(b + 1, 0, norm=b)
            unit(RB - 1, 1, ahead=False)
            for stage in FRONT:
                group_norm(RB - 1, stage)
            on_mov = lambda k, h: mov[:, k, :, :] if h is None else mov[:, k, h, :]
            on_hid = lambda k, h: hid[:, k, :, :] if h is None else hid[:, k, h, :]

            def norm_and_ffn(e, norm, suffix):
                sums_of_squares("out" + suffix)
                gemm(PH["ffn" + suffix], on_x(PH["ffn" + suffix], on_mov), ready=lambda c: (mov_ready, norm * KB + (c + 1) * CK))
                gemm(PH["down" + suffix], on_x(PH["down" + suffix], on_hid),
                     ready=lambda c: (ffn_lo, e * PH["ffn"].trips + (c + 1) * CK // 2 + 1))

            gemm(PH["out"], on_x(PH["out"], on_mov), ready=lambda c: (ylo, 4 if c else 1))
            norm_and_ffn(0, 2, "")
            sums_of_squares("down")
            gemm(PH["in_2"], on_x(PH["in_2"], on_mov), ready=lambda c: (mov_ready, 3 * KB + (c + 1) * CK))

            def lru(h, j):
                if j == 1:
                    pe.wait_ge(gw_in, h * 32 + 32)
                    lrud.wait(pe, "c0", h)
                    for g in range(2):
                        mm = pe.matmul(ps[:, 4, g * T:(g + 1) * T], gw[:, g, :], lu[:, :], start=True, stop=True)
                    lrup.done(mm, "g")

            def retention(h, j):
                if j == 0:
                    retg.wait(pe, "v", h)
                    for n in range(2):
                        mm = pe.matmul(ps[:, 7, n * P:(n + 1) * P], rv[:, n * P:(n + 1) * P], less_mean, start=True, stop=True)
                    retp.done(mm, "cv")
                    retp.done(pe.matmul(ps[:, 5, :].rearrange("p (a b t) -> p a b t", a=2, b=1), swap, qk_of(h), start=True, stop=True), "sw")
                if j == 1:
                    retd.wait(pe, "qr", h)
                    pe.matmul(ps[:, 6, 0:T], rqk[:, 1, 0:P], rqk[:, 0, :], start=True, stop=True)
                    retp.done(pe.matmul(ps[:, 6, T:T + P], rqk[:, 1, P:T], rqk[:, 0, P:T], start=True, stop=True), "sc")
                if j == 2:
                    retd.wait(pe, "pr", h)
                    reta.wait(pe, "vt", h)
                    pe.matmul(ps[:, 5, 0:T], rvt[:, 0, :], rp[:, 0:T], start=True, stop=False)
                    retp.done(pe.matmul(ps[:, 5, P:T], rvt[:, 1, :], rp[:, T:T + P], start=False, stop=True), "o")
                if j == 4:
                    reta.wait(pe, "sq", h)
                    retp.done(pe.matmul(ps[:, 7, T:2 * T], ones, rsq[:, :], start=True, stop=True), "var")

            def side(h, j):
                lru(h, j)
                if not (isinstance(h, int) and h == 0):
                    retention(h - 1, j)

            pe.wait_ge(kret_in, 16)

            def of_head(p, s, c):
                b = PH["in_2_heads"].bank(p) + c % 2
                w_hi, w_lo = (w[:, s, :, :].rearrange("p k (a n) -> p (k a) n", a=2) for w in (hi, lo))
                for kk in range(2 * CK):
                    k = c // 2 * 2 * CK + kk
                    pe.matmul(ps[:, b, :], w_hi[:, kk, :], on_mov(k, None), start=(k == 0), stop=False)
                    mm = pe.matmul(ps[:, b, 0:T], w_lo[:, kk, :], on_mov(k, 0), start=False, stop=(k == KB - 1))
                return mm

            gemm(PH["in_2_heads"], None, after=side, chunk=of_head)
            for j in range(8):
                retention(RET_HEADS - 1, j)
            gemm(PH["out_2"], on_x(PH["out_2"], on_mov), ready=lambda c: (y2_lo, c + 1))
            norm_and_ffn(1, 4, "_2")
            sums_of_squares("down_2")
            pe.wait_ge(bank_free, PH["down_2"].pair(1, 3) + 1 + BANK_CREDIT)
            for n in range(8):
                pe.wait_ge(x_scaled, KB + 4 * (n // 2 + 1))
                for k in range(4):
                    mm = pe.transpose(ps[:, n, k * P:(k + 1) * P], xT[:, 4 * (n // 2) + k, (n % 2) * P:(n % 2 + 1) * P], ident)
                mm.then_inc(row_turned, 1)


INPUTS = ["x", "c", "ctx", "c_ctx", "w_mod", "b_mod", "norm_mix", "w_in", "rw_shift", "dec_w0", "dec_up", "iclr_a0",
          "iclr_up", "k_k", "k_a", "r_k", "ln_w", "ln_b", "g_up", "conv_w", "w_out", "norm_ffn", "w_gate", "w_up",
          "w_down", "norm_final", "ln1_w_2", "w_in_2", "conv_w_2", "conv_b_2", "gate_a_w_2", "gate_a_b_2",
          "gate_x_w_2", "gate_x_b_2", "lru_lambda_2", "ret_gn_w_2", "w_out_2", "ln2_w_2", "w_ffn_gate_2",
          "w_ffn_up_2", "w_ffn_down_2", "final_norm_w_2"]


def kernel(**inputs):
    import concourse.bacc as bacc
    from concourse.bass_utils import run_bass_kernel_spmd as run

    nc = bacc.Bacc("TRN2", target_bir_lowering=False, num_devices=1)
    arrays = {"in_" + n: np.ascontiguousarray(inputs[n]) for n in INPUTS}
    arrays = {n: a[0] if a.shape[0] == 1 and n[3:] not in ("x", "c", "ctx") and a.ndim > 1 else a for n, a in arrays.items()}
    arrays.update(constants())
    given = {n: nc.dram_tensor(n, a.shape, F32, kind="ExternalInput").ap() for n, a in arrays.items()}
    given = {n.removeprefix("in_"): ap for n, ap in given.items()}
    out = nc.dram_tensor("out_h", (1, T, D), F32, kind="ExternalOutput").ap()
    program(nc, given, out)
    return run(nc, [arrays], core_ids=[0]).results[0]["out_h"]
```
